# Optimizing a Trainium2 kernel written in Bass

```python
import jax
import jax.numpy as jnp
from jax import lax
import numpy as np

D_MODEL = 2048
BATCH = 1
SEQ = 128
DEPTH = 2
DEC_BATCH = 1
DEC_SEQ = 128
PAST_LEN = 128

GRID_W = 64
HEAD_DIM = 128
N_HEADS_A = D_MODEL // (2 * HEAD_DIM)
N_HEADS_B = D_MODEL // (2 * HEAD_DIM)
N_KV_B = max(1, N_HEADS_B // 4)
G_B = N_HEADS_B // N_KV_B
NA_ROWS = 8
NA_COLS = 16
WIN_B = 128
BLK = 128
D_RNN = D_MODEL
N_RG_BLOCKS = 16
RG_BLOCK = D_RNN // N_RG_BLOCKS
CONV_W = 4
CONV_PAD_L = 2
RG_C = 8.0
D_FF = 4 * D_MODEL
ROPE_BASE = 10000.0
EPS = 1e-6
NEG = -1e30
N_ATT_LAYERS = (DEPTH + 1) // 2
N_REC_LAYERS = DEPTH // 2
QA_W = N_HEADS_A * HEAD_DIM
QB_W = N_HEADS_B * HEAD_DIM
KVB_W = N_KV_B * HEAD_DIM
D_ATT_IN = 3 * QA_W + QB_W + 2 * KVB_W
D_ATT_OUT = QA_W + QB_W

kernel_name = "hybrid_diffusion_na_swa_rglru_step"

def rmsnorm(x, g):
    xf = x.astype(jnp.float32)
    y = xf * lax.rsqrt(jnp.mean(xf * xf, axis=-1, keepdims=True) + EPS)
    return (y * g.astype(jnp.float32)).astype(x.dtype)

def adaln(cond, w, b):
    m = jax.nn.silu(cond) @ w + b
    return [t[:, None, :] for t in jnp.split(m, 6, axis=-1)]

def _rope_axis(x, pos):
    d = x.shape[-1]
    inv = ROPE_BASE ** (-jnp.arange(0, d, 2, dtype=jnp.float32) / d)
    ang = pos.astype(jnp.float32)[:, None] * inv[None, :]
    cos = jnp.cos(ang)[None, :, None, :]
    sin = jnp.sin(ang)[None, :, None, :]
    x1, x2 = jnp.split(x.astype(jnp.float32), 2, axis=-1)
    return jnp.concatenate([x1 * cos - x2 * sin, x2 * cos + x1 * sin], axis=-1).astype(x.dtype)

def rope_2d(x):
    t = jnp.arange(x.shape[1])
    half = x.shape[-1] // 2
    return jnp.concatenate([_rope_axis(x[..., :half], t // GRID_W),
                            _rope_axis(x[..., half:], t % GRID_W)], axis=-1)

def dense_ctx_attention(q, k, v, sink):
    s = jnp.einsum('bqhgd,bkhd->bhgqk', q, k).astype(jnp.float32) * (HEAD_DIM ** -0.5)
    if sink is not None:
        B, H, G, Lq, _ = s.shape
        s_sink = jnp.broadcast_to(sink.astype(jnp.float32)[None, :, :, None, None], (B, H, G, Lq, 1))
        p = jax.nn.softmax(jnp.concatenate([s_sink, s], axis=-1), axis=-1)[..., 1:]
    else:
        p = jax.nn.softmax(s, axis=-1)
    return jnp.einsum('bhgqk,bkhd->bqhgd', p.astype(v.dtype), v)

def neighbourhood_attention(q, k, v, kc, vc, rpb):
    B, T, H, D = q.shape
    R = T // GRID_W
    kh = min(NA_ROWS, R)
    r = jnp.arange(R)
    row_idx = jnp.clip(r - kh // 2, 0, R - kh)[:, None] + jnp.arange(kh)[None, :]
    j = jnp.arange(GRID_W)
    start_c = jnp.clip(j - NA_COLS // 2, 0, GRID_W - NA_COLS)
    qg = q.reshape(B, R, GRID_W, H, D)
    kb = k.reshape(B, R, GRID_W, H, D)[:, row_idx]
    vb = v.reshape(B, R, GRID_W, H, D)[:, row_idx]
    s = jnp.einsum('brqhd,brikhd->bhrqik', qg, kb).astype(jnp.float32) * (HEAD_DIM ** -0.5)
    dr = row_idx - r[:, None] + (NA_ROWS - 1)
    dc = jnp.clip(j[None, :] - j[:, None] + (NA_COLS - 1), 0, 2 * NA_COLS - 2)
    in_win = (j[None, :] >= start_c[:, None]) & (j[None, :] < start_c[:, None] + NA_COLS)
    bias = rpb[:, dr[:, None, :, None], dc[None, :, None, :]].astype(jnp.float32)
    s = jnp.where(in_win[None, None, None, :, None, :], s + bias[None], NEG)
    sc = jnp.einsum('brqhd,bchd->bhrqc', qg, kc).astype(jnp.float32) * (HEAD_DIM ** -0.5)
    nk = kh * GRID_W
    p = jax.nn.softmax(jnp.concatenate([s.reshape(B, H, R, GRID_W, nk), sc], axis=-1), axis=-1)
    p_nb = p[..., :nk].reshape(B, H, R, GRID_W, kh, GRID_W).astype(v.dtype)
    p_c = p[..., nk:].astype(v.dtype)
    o = jnp.einsum('bhrqik,brikhd->brqhd', p_nb, vb) + jnp.einsum('bhrqc,bchd->brqhd', p_c, vc)
    return o.reshape(B, T, H, D)

def window_attention(q, k, v, kc, vc, sink):
    B, T, Hkv, G, D = q.shape
    nb = T // BLK
    qb = q.reshape(B, nb, BLK, Hkv, G, D)
    pad = jnp.zeros((B, BLK, Hkv, D), k.dtype)
    kp = jnp.concatenate([pad, k, pad], axis=1)
    vp = jnp.concatenate([pad, v, pad], axis=1)
    idx = jnp.arange(nb)[:, None] * BLK + jnp.arange(3 * BLK)[None, :]
    kb = kp[:, idx]
    vb = vp[:, idx]
    qpos = jnp.arange(nb)[:, None] * BLK + jnp.arange(BLK)[None, :]
    kpos = idx - BLK
    valid = ((jnp.abs(qpos[:, :, None] - kpos[:, None, :]) <= WIN_B)
             & (kpos >= 0)[:, None, :] & (kpos < T)[:, None, :])
    s = jnp.einsum('bnqhgd,bnkhd->bhgnqk', qb, kb).astype(jnp.float32) * (HEAD_DIM ** -0.5)
    s = jnp.where(valid[None, None, None], s, NEG)
    sc = jnp.einsum('bnqhgd,bchd->bhgnqc', qb, kc).astype(jnp.float32) * (HEAD_DIM ** -0.5)
    s_sink = jnp.broadcast_to(sink.astype(jnp.float32)[None, :, :, None, None, None], (B, Hkv, G, nb, BLK, 1))
    p = jax.nn.softmax(jnp.concatenate([s_sink, s, sc], axis=-1), axis=-1)
    p_band = p[..., 1:1 + 3 * BLK].astype(v.dtype)
    p_ctx = p[..., 1 + 3 * BLK:].astype(v.dtype)
    o = jnp.einsum('bhgnqk,bnkhd->bnqhgd', p_band, vb) + jnp.einsum('bhgnqc,bchd->bnqhgd', p_ctx, vc)
    return o.reshape(B, T, Hkv * G, D)

def att_project(h, w_in):
    B, L, _ = h.shape
    cuts = [QA_W, 2 * QA_W, 3 * QA_W, 3 * QA_W + QB_W, 3 * QA_W + QB_W + KVB_W]
    qa, ka, va, qb, kb, vb = jnp.split(h @ w_in, cuts, axis=-1)
    sa = (B, L, N_HEADS_A, HEAD_DIM)
    skv = (B, L, N_KV_B, HEAD_DIM)
    return (qa.reshape(sa), ka.reshape(sa), va.reshape(sa),
            qb.reshape(B, L, N_HEADS_B, HEAD_DIM), kb.reshape(skv), vb.reshape(skv))

def att_mixer_ctx(h, w_in, w_out, sink):
    B, L, _ = h.shape
    qa, ka, va, qb, kb, vb = att_project(h, w_in)
    oa = dense_ctx_attention(qa[:, :, :, None, :], ka, va, None)
    ob = dense_ctx_attention(qb.reshape(B, L, N_KV_B, G_B, HEAD_DIM), kb, vb, sink)
    o = jnp.concatenate([oa.reshape(B, L, QA_W), ob.reshape(B, L, QB_W)], axis=-1) @ w_out
    return o, ka, va, kb, vb

def att_mixer_lat(h, w_in, w_out, sink, rpb, ak, av, bk, bv):
    B, T, _ = h.shape
    qa, ka, va, qb, kb, vb = att_project(h, w_in)
    qb = rope_2d(qb)
    kb = rope_2d(kb)
    oa = neighbourhood_attention(qa, ka, va, ak, av, rpb)
    ob = window_attention(qb.reshape(B, T, N_KV_B, G_B, HEAD_DIM), kb, vb, bk, bv, sink)
    return jnp.concatenate([oa.reshape(B, T, QA_W), ob.reshape(B, T, QB_W)], axis=-1) @ w_out

def depthwise_conv(x, w, b):
    y = lax.conv_general_dilated(x, w[:, None, :].astype(x.dtype), window_strides=(1,),
                                 padding=[(CONV_PAD_L, CONV_W - 1 - CONV_PAD_L)],
                                 dimension_numbers=('NWC', 'WIO', 'NWC'),
                                 feature_group_count=x.shape[-1])
    return y + b

def _lin_combine(left, right):
    a_l, b_l = left
    a_r, b_r = right
    return a_l * a_r, a_r * b_l + b_r

def rglru(x, w_a, b_a, w_x, b_x, lam, h0, reverse):
    B, T, _ = x.shape
    xb = x.reshape(B, T, N_RG_BLOCKS, RG_BLOCK)
    gate_a = jnp.einsum('btnk,nkj->btnj', xb, w_a).reshape(B, T, D_RNN) + b_a
    gate_x = jnp.einsum('btnk,nkj->btnj', xb, w_x).reshape(B, T, D_RNN) + b_x
    r = jax.nn.sigmoid(gate_a.astype(jnp.float32))
    i = jax.nn.sigmoid(gate_x.astype(jnp.float32))
    log_a = -RG_C * r * jax.nn.softplus(-lam.astype(jnp.float32))
    a = jnp.exp(log_a)
    bcoef = jnp.sqrt(-jnp.expm1(2.0 * log_a)) * i * x.astype(jnp.float32)
    h0 = h0.astype(jnp.float32)
    if reverse:
        bcoef = bcoef.at[:, -1].add(a[:, -1] * h0)
    else:
        bcoef = bcoef.at[:, 0].add(a[:, 0] * h0)
    _, h = lax.associative_scan(_lin_combine, (a, bcoef), reverse=reverse, axis=1)
    return h

def rec_mixer(h, w_in, cw, cb, w_a, b_a, w_x, b_x, lam, w_out, h0f, h0b):
    xr, g = jnp.split(h @ w_in, 2, axis=-1)
    xr = depthwise_conv(xr, cw, cb)
    hf = rglru(xr, w_a[0], b_a[0], w_x[0], b_x[0], lam[0], h0f, False)
    hb = rglru(xr, w_a[1], b_a[1], w_x[1], b_x[1], lam[1], h0b, True)
    y = ((hf + hb) * jax.nn.gelu(g.astype(jnp.float32))).astype(h.dtype)
    return y @ w_out, hf, hb

def ffn(h, w1, w2):
    a = jnp.maximum(h @ w1, 0)
    return (a * a) @ w2

def setup_inputs(seed: int = 0) -> dict:
    key = jax.random.key(seed)
    ks = iter(jax.random.split(key, 40))

    def nrm(shape, scale):
        return jax.random.normal(next(ks), shape, jnp.float32) * scale

    u = jax.random.uniform(next(ks), (N_REC_LAYERS, 2, D_RNN), jnp.float32, minval=0.9, maxval=0.999)
    a0 = u ** (1.0 / RG_C)
    rg_lambda = jnp.log(a0) - jnp.log1p(-a0)
    return {
        'x_prompt': nrm((BATCH, SEQ, D_MODEL), 1.0),
        'x_sample': nrm((DEC_BATCH, DEC_SEQ, D_MODEL), 1.0),
        'c': nrm((DEC_BATCH, D_MODEL), 1.0),
        'cache_a_k': nrm((DEC_BATCH, N_ATT_LAYERS, PAST_LEN, N_HEADS_A, HEAD_DIM), 1.0),
        'cache_a_v': nrm((DEC_BATCH, N_ATT_LAYERS, PAST_LEN, N_HEADS_A, HEAD_DIM), 1.0),
        'cache_b_k': nrm((DEC_BATCH, N_ATT_LAYERS, PAST_LEN, N_KV_B, HEAD_DIM), 1.0),
        'cache_b_v': nrm((DEC_BATCH, N_ATT_LAYERS, PAST_LEN, N_KV_B, HEAD_DIM), 1.0),
        'state_rg_fwd': nrm((DEC_BATCH, N_REC_LAYERS, D_RNN), 0.5),
        'state_rg_bwd': nrm((DEC_BATCH, N_REC_LAYERS, D_RNN), 0.5),
        'c_ctx': nrm((D_MODEL,), 1.0),
        'w_ada': nrm((DEPTH, D_MODEL, 6 * D_MODEL), 0.5 * D_MODEL ** -0.5),
        'b_ada': nrm((DEPTH, 6 * D_MODEL), 0.02),
        'g_pre_mix': 1.0 + nrm((DEPTH, D_MODEL), 0.05),
        'g_post_mix': 1.0 + nrm((DEPTH, D_MODEL), 0.05),
        'g_pre_ffn': 1.0 + nrm((DEPTH, D_MODEL), 0.05),
        'g_post_ffn': 1.0 + nrm((DEPTH, D_MODEL), 0.05),
        'w_att_in': nrm((N_ATT_LAYERS, D_MODEL, D_ATT_IN), D_MODEL ** -0.5),
        'w_att_out': nrm((N_ATT_LAYERS, D_ATT_OUT, D_MODEL), D_ATT_OUT ** -0.5),
        'sink_b': nrm((N_ATT_LAYERS, N_KV_B, G_B), 0.5),
        'rpb_a': nrm((N_ATT_LAYERS, N_HEADS_A, 2 * NA_ROWS - 1, 2 * NA_COLS - 1), 0.1),
        'w_rec_in': nrm((N_REC_LAYERS, D_MODEL, 2 * D_RNN), D_MODEL ** -0.5),
        'conv_w': nrm((N_REC_LAYERS, CONV_W, D_RNN), CONV_W ** -0.5),
        'conv_b': nrm((N_REC_LAYERS, D_RNN), 0.02),
        'w_rg_a': nrm((N_REC_LAYERS, 2, N_RG_BLOCKS, RG_BLOCK, RG_BLOCK), RG_BLOCK ** -0.5),
        'b_rg_a': nrm((N_REC_LAYERS, 2, D_RNN), 0.02),
        'w_rg_x': nrm((N_REC_LAYERS, 2, N_RG_BLOCKS, RG_BLOCK, RG_BLOCK), RG_BLOCK ** -0.5),
        'b_rg_x': nrm((N_REC_LAYERS, 2, D_RNN), 0.02),
        'rg_lambda': rg_lambda,
        'w_rec_out': nrm((N_REC_LAYERS, D_RNN, D_MODEL), D_RNN ** -0.5),
        'w_ff1': nrm((DEPTH, D_MODEL, D_FF), D_MODEL ** -0.5),
        'w_ff2': nrm((DEPTH, D_FF, D_MODEL), D_FF ** -0.5),
    }

def reference(x_prompt, x_sample, c, cache_a_k, cache_a_v, cache_b_k, cache_b_v, state_rg_fwd,
              state_rg_bwd, c_ctx, w_ada, b_ada, g_pre_mix, g_post_mix, g_pre_ffn, g_post_ffn,
              w_att_in, w_att_out, sink_b, rpb_a, w_rec_in, conv_w, conv_b, w_rg_a, b_rg_a,
              w_rg_x, b_rg_x, rg_lambda, w_rec_out, w_ff1, w_ff2):
    yp, ys = x_prompt, x_sample
    ctx_cond = c_ctx[None, :]
    ak_l, av_l, bk_l, bv_l, sf_l, sb_l = [], [], [], [], [], []
    for layer in range(DEPTH):
        shm_p, scm_p, gm_p, shf_p, scf_p, gf_p = adaln(ctx_cond, w_ada[layer], b_ada[layer])
        shm_s, scm_s, gm_s, shf_s, scf_s, gf_s = adaln(c, w_ada[layer], b_ada[layer])
        hp = rmsnorm(yp, g_pre_mix[layer]) * (1 + scm_p) + shm_p
        hs = rmsnorm(ys, g_pre_mix[layer]) * (1 + scm_s) + shm_s
        li = layer // 2
        if layer % 2 == 0:
            op, ka, va, kb, vb = att_mixer_ctx(hp, w_att_in[li], w_att_out[li], sink_b[li])
            os_ = att_mixer_lat(hs, w_att_in[li], w_att_out[li], sink_b[li], rpb_a[li],
                                cache_a_k[:, li], cache_a_v[:, li], cache_b_k[:, li], cache_b_v[:, li])
            ak_l.append(ka)
            av_l.append(va)
            bk_l.append(kb)
            bv_l.append(vb)
        else:
            zeros = jnp.zeros((yp.shape[0], D_RNN), yp.dtype)
            op, hf, hb = rec_mixer(hp, w_rec_in[li], conv_w[li], conv_b[li], w_rg_a[li], b_rg_a[li],
                                   w_rg_x[li], b_rg_x[li], rg_lambda[li], w_rec_out[li], zeros, zeros)
            os_, _, _ = rec_mixer(hs, w_rec_in[li], conv_w[li], conv_b[li], w_rg_a[li], b_rg_a[li],
                                  w_rg_x[li], b_rg_x[li], rg_lambda[li], w_rec_out[li],
                                  state_rg_fwd[:, li], state_rg_bwd[:, li])
            sf_l.append(hf[:, -1].astype(yp.dtype))
            sb_l.append(hb[:, 0].astype(yp.dtype))
        yp = yp + gm_p * rmsnorm(op, g_post_mix[layer])
        ys = ys + gm_s * rmsnorm(os_, g_post_mix[layer])
        hp = rmsnorm(yp, g_pre_ffn[layer]) * (1 + scf_p) + shf_p
        hs = rmsnorm(ys, g_pre_ffn[layer]) * (1 + scf_s) + shf_s
        yp = yp + gf_p * rmsnorm(ffn(hp, w_ff1[layer], w_ff2[layer]), g_post_ffn[layer])
        ys = ys + gf_s * rmsnorm(ffn(hs, w_ff1[layer], w_ff2[layer]), g_post_ffn[layer])
    return (yp, ys, jnp.stack(ak_l, axis=1), jnp.stack(av_l, axis=1), jnp.stack(bk_l, axis=1),
            jnp.stack(bv_l, axis=1), jnp.stack(sf_l, axis=1), jnp.stack(sb_l, axis=1))


_drawn_inputs = setup_inputs


def setup_inputs(seed=0):
    import zlib

    import numpy as np

    out = dict(_drawn_inputs(seed))
    spreads = {}
    factors = {'g_pre_ffn': 2.689,
     'g_post_ffn': 2.945,
     'sink_b': 8.0,
     'rpb_a': 6.752,
     'b_rg_a': 8.0,
     'b_rg_x': 7.031,
     'state_rg_fwd': 2.679}
    for name, (base, spread) in spreads.items():
        noise = np.random.default_rng([zlib.crc32(name.encode()), seed]).standard_normal(out[name].shape)
        drawn = base * np.exp(spread * noise) if base else spread * noise
        out[name] = jnp.asarray(drawn.astype(out[name].dtype))
    for name, factor in factors.items():
        out[name] = (out[name] * factor).astype(out[name].dtype)
    return out
```

```python
import concourse.bass as bass
from concourse import mybir
from contextlib import ExitStack

D = 2048
T = 128
NG = 2
P = 128
KC = D // P
FF = 4 * D
HD = 128
NA = 8
NKV = 2
QKV_W = 3 * NA * HD + NA * HD + 2 * NKV * HD
QA0, KA0, VA0, QB0, KB0, VB0 = 0, 1024, 2048, 3072, 4096, 4352
GRID_W = 64
RPB_ROWS, RPB_COLS = 15, 31
EPS = 1e-6
SCALE = float(HD) ** -0.5
BLK = 512
QKV_BLOCKS = QKV_W // BLK
TILE = 4
NRAW = 4
NSPLIT = 4
GELU_C = 0.7978845608028654


class Sweep:

    def __init__(self, name, n, mode, weight, col0, tiles, blocks, ada, ada_at, order, out, skew=True):
        self.name, self.n, self.mode = name, n, mode
        self.weight, self.col0 = weight, col0
        self.tiles, self.blocks = tiles, blocks
        self.ada, self.ada_at = ada, ada_at
        self.order = order
        self.out = out
        self.skew = skew
        self.halves = 2 * order.count("M")
        assert order.count("M") == tiles * blocks and len(order) % NRAW == 0


def plan(w):
    ma = "MA" * 4
    sweeps = [
        Sweep("ada0", 8, None, None, 0, 0, 0, "cols", (0, 0), "AAAA", None),
        Sweep("att_in_a", 4, "token", w["att_in"], 0, 4, 1, "gate", (0, 8), ma, "qkv"),
        Sweep("att_in_b", 5, "token", w["att_in"], 4, 4, 1, "cols", (0, 12), ma, "qkv"),
        Sweep("att_out_a", 3, "token", w["att_out"], 0, 4, 1, "cols", (0, 17), ma, "op"),
        Sweep("att_out_b", 1, "token", w["att_out"], 3, 4, 1, None, None, "MMMM", "op"),
        Sweep("ff1_0", 8, "feature", w["ff1_0"], 0, 4, 2, "cols", (1, 0), "MMA" * 4, "hidden"),
        Sweep("ff2_0", 4, "token", w["ff2_0"], 0, 16, 1, "gate", (0, 20), "MMA" * 4 + "M" * 8, "op", False),
        Sweep("rec_in_a", 4, "feature", w["rec_in"], 0, 4, 1, "gate", (1, 8), ma, "xr"),
        Sweep("rec_in_b", 4, "feature", w["rec_in"], 4, 4, 1, "cols", (1, 12), ma, "gr"),
        Sweep("rec_out", 4, "token", w["rec_out"], 0, 4, 1, "cols", (1, 16), ma, "op"),
        Sweep("ff1_1", 8, "feature", w["ff1_1"], 0, 4, 2, None, None, "M" * 8, "hidden"),
        Sweep("ff2_1", 4, "token", w["ff2_1"], 0, 16, 1, "gate", (1, 20), "MMA" * 4 + "M" * 8, "op", False),
    ]
    pos = half = ada = token = feature = gate = main = 0
    for s in sweeps:
        s.pos0, s.main0, s.half0, s.ada0, s.token0, s.feature0, s.gate0 = pos, main, half, ada, token, feature, gate
        pos += s.n * len(s.order)
        main += s.n * s.order.count("M")
        half += s.n * s.halves
        ada += s.n * bool(s.ada)
        gate += s.n * (s.ada == "gate")
        if s.mode == "token":
            token += s.n * s.blocks
        if s.mode == "feature":
            feature += s.n * s.blocks
    return sweeps


def hybrid_step(nc, A, out):
    fp32 = mybir.dt.float32
    fp32r = mybir.dt.float32r
    ALU = mybir.AluOpType
    ACT = mybir.ActivationFunctionType
    AX = mybir.AxisListType.X

    def tiles_of(w):
        return w.rearrange("(t c p) n -> t p c n", c=TILE, p=P)

    W = {
        "att_in": tiles_of(A["w_att_in"][0]), "att_out": tiles_of(A["w_att_out"][0]),
        "rec_in": tiles_of(A["w_rec_in"][0]), "rec_out": tiles_of(A["w_rec_out"][0]),
        "ff1_0": tiles_of(A["w_ff1"][0]), "ff1_1": tiles_of(A["w_ff1"][1]),
        "ff2_0": tiles_of(A["w_ff2"][0]), "ff2_1": tiles_of(A["w_ff2"][1]),
    }
    W_ada = [tiles_of(A["w_ada"][layer]) for layer in range(2)]
    S = {s.name: s for s in plan(W)}
    sweeps = list(S.values())

    def after(name):
        s = S[name]
        return s.half0 + s.n * s.halves

    ctx = ExitStack()
    with ctx:
        def sb(name, shape, dt=fp32):
            return ctx.enter_context(nc.sbuf_tensor(name, shape, dt))

        def sem(name):
            return ctx.enter_context(nc.semaphore(name))

        raw = sb("raw", [P, NRAW, TILE, BLK])
        w_hi = sb("w_hi", [P, NSPLIT, 2, BLK], fp32r)
        w_lo = sb("w_lo", [P, NSPLIT, 2, BLK], fp32r)
        xt = sb("xt", [P, KC, 2 * NG * T], fp32r)
        x = sb("x", [P, NG, D])
        gate = sb("gate", [P, NG, D])
        R = sb("R", [P, 16384])
        cond = sb("cond", [P, KC, 32])
        ada_rows = sb("ada_rows", [P, BLK])
        bias_rows = sb("bias_rows", [P, BLK])
        gain_rows = sb("gain_rows", [P, BLK])
        ada_cols = sb("ada_cols", [P, 2, KC, NG])
        ident = sb("ident", [P, P])
        flip = sb("flip", [P, P])
        sel = sb("sel", [P, 2])
        vec_a = sb("vec_a", [P, 96])
        vec_r = sb("vec_r", [P, 13 * KC])
        window = sb("window", [P, T])
        rope_cos = sb("rope_cos", [P, 64])
        rope_sin = sb("rope_sin", [P, 64])
        rpb = sb("rpb", [P, 4, T])
        small = sb("small", [P, 128])
        hidden = R[:, :].rearrange("p (c t) -> p c t", t=NG * T)
        qkv = R[:, 0:NG * QKV_W].rearrange("p (g n) -> p g n", g=NG)
        o = NG * QKV_W
        ctx_k = R[:, o:o + 1280].rearrange("p (h d) -> p h d", d=HD)
        ctx_v = R[:, o + 1280:o + 2560].rearrange("p (h d) -> p h d", d=HD)
        o += 2560
        q_t = R[:, o:o + 1024].rearrange("p (g h t) -> p g h t", g=NG, h=4)
        k_t = R[:, o + 1024:o + 2048].rearrange("p (g h t) -> p g h t", g=NG, h=4)
        ck_t = R[:, o + 2048:o + 2560].rearrange("p (h t) -> p h t", h=4)
        prob_s = R[:, o + 2560:o + 3584].rearrange("p (h t) -> p h t", h=4)
        prob_p = R[:, o + 3584:o + 4096].rearrange("p (h t) -> p h t", h=4)
        pc_t = R[:, o + 4096:o + 4608].rearrange("p (h t) -> p h t", h=4)
        rope_a = R[:, o + 2560:o + 3200].rearrange("p (h a f) -> p h a f", h=10, a=2)
        rope_b = R[:, o + 3200:o + 3840].rearrange("p (h a f) -> p h a f", h=10, a=2)
        xr = R[:, 0:4096].rearrange("p (c g t) -> p c g t", g=NG, t=T)
        gr = R[:, 4096:8192].rearrange("p (c t) -> p c t", t=NG * T)
        w_rg = R[:, 8192:10240].rearrange("p (s c k j) -> p s c k j", s=2, c=2, k=4)
        xc = R[:, 10240:10752].rearrange("p (c g t) -> p c g t", c=2, g=NG)
        tt = R[:, 10752:11776].rearrange("p (c d n) -> p c d n", c=2, d=2)
        th_i = R[:, 11776:12800].rearrange("p (c d n) -> p c d n", c=2, d=2)
        root = R[:, 12800:13824].rearrange("p (c d n) -> p c d n", c=2, d=2)
        inv = R[:, 13824:14848].rearrange("p (c d n) -> p c d n", c=2, d=2)
        th_a = R[:, 14848:15360].rearrange("p (d n) -> p d n", d=2)
        gel = R[:, 15360:15872].rearrange("p (c n) -> p c n", c=2)
        diag = R[:, 0:256].rearrange("p (g t) -> p g t", g=NG)
        h_mod = R[:, 256:1280].rearrange("p (s c g t) -> p s c g t", s=2, c=2, g=NG)
        junk = R[:, 4096:8192].rearrange("p (a n) -> p a n", a=4)
        stage = R[:, 2048:2048 + 3 * P].rearrange("p (a k) -> p a k", a=3)
        lam_t = R[:, 3072:3072 + 6 * 2 * KC].rearrange("p (a k) -> p a k", a=6)
        silu_t = R[:, 3584:3584 + 2 * NG * KC].rearrange("p (a k) -> p a k", a=2)
        ssq = small[:, 0:8].rearrange("p (g b) -> p g b", g=NG)
        ssq_x = small[:, 8:12].rearrange("p (g b) -> p g b", g=NG)
        mean = small[:, 12:14]
        rstd = small[:, 14:16]
        half_neg = small[:, 16:18]
        gs = small[:, 32:64].rearrange("p (c g) -> p c g", g=NG)
        mx = small[:, 64:72].rearrange("p (g h) -> p g h", g=NG)
        den = small[:, 72:80].rearrange("p (g h) -> p g h", g=NG)
        sink = small[:, 80:88]
        sink_e = small[:, 88:96].rearrange("p (g h) -> p g h", g=NG)
        states = small[:, 96:96 + 2 * KC]
        state_rows = rpb[0:2 * KC, 0, :]
        CONV_W, CONV_B, B_A, B_X, LAM, H0 = 0, 64, 80, 112, 144, 176

        ps = [ctx.enter_context(nc.psum_tensor(f"bank{i}", [P, BLK], fp32)) for i in range(8)]

        raw_landed = [sem(f"raw_landed{i}") for i in range(NRAW)]
        hi_ready = sem("hi_ready")
        lo_ready = sem("lo_ready")
        half_used = sem("half_used")
        ada_used = sem("ada_used")
        g0_done = sem("g0_done")
        chunk_done = sem("chunk_done")
        out_read_act = sem("out_read_act")
        out_read_dve = sem("out_read_dve")
        lo_copied = sem("lo_copied")
        chunk_read = sem("chunk_read")
        hidden_ready = sem("hidden_ready")
        bias_landed = sem("bias_landed")
        gain_landed = sem("gain_landed")
        ada_row = sem("ada_row")
        ada_small = sem("ada_small")
        ada_fin = sem("ada_fin")
        x_landed = sem("x_landed")
        id_landed = sem("id_landed")
        const_landed = sem("const_landed")
        vec_a_landed = sem("vec_a_landed")
        vec_r_landed = sem("vec_r_landed")
        cache_landed = sem("cache_landed")
        rpb_landed = sem("rpb_landed")
        rg_landed = [sem("rg_landed0"), sem("rg_landed1")]
        stored = sem("stored")
        cleared = sem("cleared")
        dve_step = sem("dve_step")
        vec_turned = sem("vec_turned")
        vec_ready = sem("vec_ready")
        cond_tanh = sem("cond_tanh")
        cond_ready = sem("cond_ready")
        lam_abs = sem("lam_abs")
        lam_exp = sem("lam_exp")
        rg_ready = sem("rg_ready")
        x_ready = sem("x_ready")
        ssq_ready = sem("ssq_ready")
        mean_ready = sem("mean_ready")
        rstd_ready = sem("rstd_ready")
        diag_ready = sem("diag_ready")
        turned = sem("turned")
        mod_ready = sem("mod_ready")
        mod_hi = sem("mod_hi")
        xt_ready = sem("xt_ready")
        qk_turned = sem("qk_turned")
        qk_copied_act = sem("qk_copied_act")
        qk_copied_dve = sem("qk_copied_dve")
        roped = sem("roped")
        scores_done = sem("scores_done")
        scores_scaled = sem("scores_scaled")
        bias_used = sem("bias_used")
        max_ready = sem("max_ready")
        exp_done = sem("exp_done")
        probs_ready = sem("probs_ready")
        probs_turned = sem("probs_turned")
        probs_copied_act = sem("probs_copied_act")
        probs_copied_dve = sem("probs_copied_dve")
        pv_done = sem("pv_done")
        heads_hi = sem("heads_hi")
        heads_ready = sem("heads_ready")
        conv_ready = sem("conv_ready")
        gates_done = sem("gates_done")
        gates_read = sem("gates_read")
        act_step = sem("act_step")
        gelu_arg = sem("gelu_arg")
        gelu_tanh = sem("gelu_tanh")
        y_ready = sem("y_ready")
        y_hi = sem("y_hi")
        y_split = sem("y_split")
        states_turned = sem("states_turned")
        state_rows_ready = sem("state_rows_ready")

        block = ctx.enter_context(nc.Block())

        def first(it):
            return isinstance(it, int) and it == 0

        def stream(s, it, p):
            return p % NRAW, 16 * (s.pos0 // NRAW + it * (len(s.order) // NRAW) + p // NRAW + 1)

        def released(s, it, p):
            if p >= NRAW:
                at, upto = (s, it), p - NRAW + 1
            elif first(it):
                k = sweeps.index(s)
                if k == 0:
                    return None
                b = sweeps[k - 1]
                at, upto = (b, b.n - 1), len(b.order) - NRAW + p + 1
            else:
                at, upto = (s, it - 1), len(s.order) - NRAW + p + 1
            b, i = at
            if b.order[upto - 1] == "M":
                return lo_ready, 2 * (b.main0 + i * b.order.count("M") + b.order[:upto].count("M"))
            return ada_used, TILE * b.ada0 + i * b.order.count("A") + b.order[:upto].count("A")

        def iterations(eng, s, body, before):
            body(s, 0, before)
            if s.n == 2:
                body(s, 1, (s, 0))
            elif s.n > 2:
                with eng.Fori(1, s.n) as it:
                    body(s, it, (s, it - 1))
            return s, s.n - 1

        class Steps:

            def __init__(self, eng, sem):
                self.eng, self.sem, self.n, self.ahead = eng, sem, 0, 0

            def __call__(self, ins):
                self.n += 1
                ins.then_inc(self.sem, 1)
                self.eng.wait_ge(self.sem, self.n + self.ahead)

        @block.sync
        def _(sp):
            def tiles(s, it, before):
                m = a = 0
                for p, kind in enumerate(s.order):
                    if kind == "M":
                        b, t = divmod(m, s.tiles)
                        w, col = s.weight[t], (s.col0 + it * s.blocks + b) * BLK
                        m += 1
                    else:
                        layer, col0 = s.ada_at
                        w, col = W_ada[layer][a], (col0 + it) * BLK
                        a += 1
                    if not isinstance(it, int):
                        col = sp.snap(col)
                    free = released(s, it, p)
                    if free:
                        sp.wait_ge(*free)
                    sp.dma_start(raw[:, p % NRAW, :, :], w[:, :, bass.ds(col, BLK)]).then_inc(raw_landed[p % NRAW], 16)

            sp.dma_start(stage[0:96, 0, :], A["vectors"][0:96, :]).then_inc(vec_a_landed, 16)
            sp.dma_start(ident[:, :], A["ident"]).then_inc(id_landed, 16)
            sp.dma_start(sel[:, :], A["sel"]).then_inc(id_landed, 16)
            for s in sweeps:
                iterations(sp, s, tiles, None)

        @block.gpsimd
        def _(pool):
            def ada_loads(s, it, before):
                b = s.ada0 + it
                layer, col = s.ada_at
                if not isinstance(b, int) or b > 0:
                    pool.wait_ge(ada_row, b)
                src = A["b_ada"][layer:layer + 1, bass.ds((col + it) * BLK, BLK)]
                pool.dma_start(bias_rows[0:NG, :], src.broadcast_to([NG, BLK])).then_inc(bias_landed, 16)
                if s.ada == "gate":
                    name = "g_post_ffn" if col >= 20 else "g_post_mix"
                    pool.wait_ge(ada_fin, b)
                    src = A[name][layer:layer + 1, bass.ds(it * BLK, BLK)]
                    pool.dma_start(gain_rows[:, :], src.broadcast_to([P, BLK])).then_inc(gain_landed, 16)

            def rsqrt(n):
                pool.wait_ge(mean_ready, n)
                nc.gpsimd.tensor_tensor(rstd, mean, half_neg, ALU.pow).then_inc(rstd_ready, 1)

            pool.wait_ge(cleared, 1)
            pool.dma_start(stage[0:112, 1, :], A["vectors"][96:208, :]).then_inc(vec_r_landed, 16)
            pool.dma_start(stage[0:96, 2, :], A["vectors"][208:304, :]).then_inc(vec_r_landed, 16)
            pool.dma_start(x[:, 0, :], A["x_prompt"][0]).then_inc(x_landed, 16)
            pool.dma_start(x[:, 1, :], A["x_sample"][0]).then_inc(x_landed, 16)
            pool.dma_start(flip[:, :], A["flip"]).then_inc(const_landed, 16)
            pool.dma_start(window[:, :], A["window"]).then_inc(const_landed, 16)
            pool.dma_start(rope_cos[:, :], A["rope_cos"]).then_inc(const_landed, 16)
            pool.dma_start(rope_sin[:, :], A["rope_sin"]).then_inc(const_landed, 16)
            pool.dma_start(sink, A["sink_b"].rearrange("a k g -> a (k g)").broadcast_to([P, 8])).then_inc(const_landed, 16)

            def load_rpb(quad):
                for r in range(2):
                    for rk in range(2):
                        at = 4 * quad * RPB_ROWS * RPB_COLS + (rk - r + 7) * RPB_COLS - 48
                        src = bass.AP(tensor=A["rpb_a"].tensor, offset=at,
                                      ap=[[1, GRID_W], [RPB_ROWS * RPB_COLS, 4], [1, GRID_W]])
                        pool.dma_start(rpb[GRID_W * r:GRID_W * (r + 1), :, GRID_W * rk:GRID_W * (rk + 1)], src)\
                            .then_inc(rpb_landed, 16)

            load_rpb(0)
            iterations(pool, S["ada0"], ada_loads, None)
            rsqrt(1)
            iterations(pool, S["att_in_a"], ada_loads, None)
            pool.wait_ge(xt_ready, KC // 2)
            pool.dma_start(ctx_k[:, 0:NA, :], A["cache_a_k"][0, 0]).then_inc(cache_landed, 16)
            pool.dma_start(ctx_k[:, NA:NA + NKV, :], A["cache_b_k"][0, 0]).then_inc(cache_landed, 16)
            pool.dma_start(ctx_v[:, 0:NA, :], A["cache_a_v"][0, 0]).then_inc(cache_landed, 16)
            pool.dma_start(ctx_v[:, NA:NA + NKV, :], A["cache_b_v"][0, 0]).then_inc(cache_landed, 16)
            iterations(pool, S["att_in_b"], ada_loads, None)
            pool.wait_ge(out_read_act, NG * QKV_BLOCKS)
            for a, c0, c1 in (("new_a_k", KA0, VA0), ("new_a_v", VA0, QB0), ("new_b_k", KB0, VB0),
                              ("new_b_v", VB0, QKV_W)):
                pool.dma_start(out[a][0, 0].rearrange("t h d -> t (h d)"), qkv[:, 0, c0:c1]).then_inc(stored, 16)
            pool.wait_ge(bias_used, 1)
            load_rpb(1)
            iterations(pool, S["att_out_a"], ada_loads, None)
            rsqrt(2)
            rsqrt(3)
            pool.wait_ge(stored, 16 * 4)
            iterations(pool, S["ff1_0"], ada_loads, None)
            iterations(pool, S["ff2_0"], ada_loads, None)
            rsqrt(4)
            rsqrt(5)
            iterations(pool, S["rec_in_a"], ada_loads, None)

            def rg_loads(pair, s):
                for c in range(2):
                    for k, (name, d) in enumerate((("w_rg_a", 0), ("w_rg_a", 1), ("w_rg_x", 0), ("w_rg_x", 1))):
                        src = A[name][0, d, bass.ds(pair * 2 + c, 1), :, :].rearrange("o k j -> k (o j)")
                        pool.dma_start(w_rg[:, s, c, k, :], src).then_inc(rg_landed[s], 16)

            pool.wait_ge(xt_ready, 3 * KC // 2)
            rg_loads(0, 0)
            rg_loads(1, 1)
            iterations(pool, S["rec_in_b"], ada_loads, None)
            with pool.Fori(1, KC // 4) as it:
                for s in range(2):
                    pool.wait_ge(gates_done, 2 * it - 1 + s)
                    rg_loads(2 * it + s, s)
            pool.wait_ge(state_rows_ready, 1)
            pool.dma_start(out["new_rg_fwd"].rearrange("a b (n k) -> (a b n) k", k=P), state_rows[0:KC, :]).then_inc(stored, 16)
            pool.dma_start(out["new_rg_bwd"].rearrange("a b (n k) -> (a b n) k", k=P), state_rows[KC:2 * KC, :]).then_inc(stored, 16)
            iterations(pool, S["rec_out"], ada_loads, None)
            rsqrt(6)
            rsqrt(7)
            iterations(pool, S["ff2_1"], ada_loads, None)
            rsqrt(8)
            for k in range(4):
                pool.wait_ge(x_ready, 12 + k + 1)
                g, c = divmod(k, 2)
                pool.dma_start(out["y_prompt" if g == 0 else "y_sample"][0][:, c * 1024:(c + 1) * 1024],
                               x[:, g, c * 1024:(c + 1) * 1024]).then_inc(stored, 16)
            pool.wait_ge(stored, 16 * 10)

        @block.tensor
        def _(pe):
            def ada_tile(s, it, p, a):
                slot, landed = stream(s, it, p)
                b = s.ada0 + it
                pe.wait_ge(raw_landed[slot], landed)
                if a == 0 and not (isinstance(b, int) and b == 0):
                    pe.wait_ge(ada_row, b)
                for j in range(TILE):
                    mm = nc.tensor.matmul(ps[4][32 * j:32 * j + 32, :], cond[:, TILE * a + j, :],
                                          raw[:, slot, j, :], start=(a == 0), stop=(a == TILE - 1))
                mm.then_inc(ada_used, 1)

            def ada_end(s, it):
                b = s.ada0 + it
                pe.wait_ge(ada_row, b + 1)
                if not (isinstance(b, int) and b == 0):
                    pe.wait_ge(ada_fin, b)
                if s.ada == "cols":
                    for m in range(BLK // P):
                        mm = nc.tensor.matmul(ps[5][:, NG * m:NG * m + NG], ada_rows[:, m * P:(m + 1) * P],
                                              sel[:, :], start=True, stop=True)
                else:
                    for g in range(NG):
                        mm = nc.tensor.matmul(ps[5 + g][:, :], sel[:, g:g + 1].broadcast_to([P, P]),
                                              ada_rows[:, :], start=True, stop=True)
                mm.then_inc(ada_small, 1)

            def token_half(s, h, g, hh, begin, end):
                for k in range(2):
                    c = (2 * hh + k) % KC
                    hi = xt[:, c, g * T:(g + 1) * T]
                    lo = xt[:, c, (NG + g) * T:(NG + g + 1) * T]
                    o = ps[g][:, :]
                    nc.tensor.matmul(o, hi, w_hi[:, h, k, :], start=(begin and k == 0), stop=False)
                    nc.tensor.matmul(o, hi, w_lo[:, h, k, :], start=False, stop=False)
                    mm = nc.tensor.matmul(o, lo, w_hi[:, h, k, :], start=False, stop=(end and k == 1))
                return mm

            def feature_half(s, h, m, hh, begin, end):
                for k in range(2):
                    c = (2 * hh + k) % KC
                    nc.tensor.matmul(ps[m][:, :], w_hi[:, h, k, m * P:(m + 1) * P], xt[:, c, :],
                                     start=(begin and k == 0), stop=False)
                    mm = nc.tensor.matmul(ps[m][:, 0:NG * T], w_lo[:, h, k, m * P:(m + 1) * P],
                                          xt[:, c, 0:NG * T], start=False, stop=(end and k == 1))
                return mm

            def body(s, it, before):
                lanes = NG if s.mode == "token" else BLK // P
                m = a = 0
                for p, kind in enumerate(s.order):
                    if kind == "A":
                        ada_tile(s, it, p, a)
                        a += 1
                        if s.mode is None and a == 1 and before and before[0].ada:
                            ada_end(*before)
                        continue
                    b, t = divmod(m, s.tiles)
                    blk = it * s.blocks + b
                    for q in range(2):
                        hh = 2 * t + q
                        h = 2 * m + q
                        n = s.half0 + it * s.halves + h
                        if first(it) and b == 0 and s.xt_ready is not None:
                            s_, base, per = s.xt_ready
                            pe.wait_ge(s_, base + hh // per + 1)
                        pe.wait_ge(lo_ready, n + 1)
                        if t == s.tiles - 1:
                            continue
                        for lane in range(lanes):
                            if hh == 0:
                                bank_free(s, blk, lane)
                            if s.mode == "token":
                                mm = token_half(s, h % NSPLIT, lane, hh, hh == 0, False)
                            else:
                                mm = feature_half(s, h % NSPLIT, lane, hh, hh == 0, False)
                        mm.then_inc(half_used, 1)
                    if t == s.tiles - 1:
                        for lane in range(lanes):
                            for q in range(2):
                                hh, h = 2 * t + q, 2 * m + q
                                if s.mode == "token":
                                    mm = token_half(s, h % NSPLIT, lane, hh, False, q == 1)
                                else:
                                    mm = feature_half(s, h % NSPLIT, lane, hh, False, q == 1)
                                if lane == lanes - 1:
                                    mm.then_inc(half_used, 1)
                                elif q == 1:
                                    mm.then_inc(g0_done if s.mode == "token" else chunk_done, 1)
                    m += 1
                    if m == 2 and before and before[0].ada and before[0].skew:
                        ada_end(*before)
                    if not s.skew and m == 11:
                        ada_end(s, it)

            def bank_free(s, blk, lane):
                if s.mode == "token":
                    n = NG * (s.token0 + blk) - NG + lane + 1
                    if s.out == "qkv":
                        if not (first(blk) and s.token0 == 0):
                            pe.wait_ge(out_read_act, n)
                    elif not (first(blk) and s.name == "att_out_a"):
                        pe.wait_ge(out_read_dve, n - NG * QKV_BLOCKS)
                    if first(blk) and lane == 0 and s.feature0:
                        pe.wait_ge(chunk_read, 4 * s.feature0)
                else:
                    if not (first(blk) and s.feature0 == 0):
                        pe.wait_ge(chunk_read, 4 * (s.feature0 + blk) - 4 + lane + 1)
                    if first(blk) and lane == 0:
                        pe.wait_ge(out_read_dve, NG * (s.token0 - QKV_BLOCKS))

            def turn_normed(n):
                pe.wait_ge(diag_ready, n + 1)
                for j in range(KC // 2):
                    if n * KC // 2 + j >= 4:
                        pe.wait_ge(mod_ready, n * KC // 2 + j - 3)
                    for c in range(2):
                        for g in range(NG):
                            at = (c * NG + g) * T
                            mm = nc.tensor.matmul(ps[4 + j % 4][:, at:at + T], x[:, g, (2 * j + c) * P:(2 * j + c + 1) * P],
                                                  diag[:, g, :], start=True, stop=True)
                    mm.then_inc(turned, 1)

            def attention(i):
                near = i < 2
                q0 = QA0 + i * BLK if near else QB0 + (i - 2) * BLK
                k0 = KA0 + i * BLK if near else KB0 + (i - 2) * HD
                v0 = VA0 + i * BLK if near else VB0 + (i - 2) * HD
                h0 = 4 * i if near else NA + i - 2
                nk = 4 if near else 1
                if i == 0:
                    pe.wait_ge(out_read_act, NG * QKV_BLOCKS)
                    pe.wait_ge(cache_landed, 16 * 4)
                    pe.wait_ge(const_landed, 16 * 5)
                else:
                    pe.wait_ge(heads_ready, i)
                if i == 2:
                    pe.wait_ge(roped, 1)
                for g in range(NG):
                    for j in range(4):
                        nc.tensor.transpose(ps[g][:, j * T:(j + 1) * T], qkv[:, g, q0 + j * HD:q0 + (j + 1) * HD], ident[:, :])
                for j in range(nk):
                    for g in range(NG):
                        o = ps[2 + g][:, j * T:(j + 1) * T]
                        nc.tensor.transpose(o, qkv[:, g, k0 + j * HD:k0 + (j + 1) * HD], ident[:, :])
                    mm = nc.tensor.transpose(ps[4][:, j * T:(j + 1) * T], ctx_k[:, h0 + j, :], ident[:, :])
                mm.then_inc(qk_turned, 1)
                pe.wait_ge(qk_copied_act, i + 1)
                pe.wait_ge(qk_copied_dve, i + 1)
                for j in range(4):
                    kj = j if near else 0
                    for bank, g, keys in ((5, 0, k_t[:, 0, kj, :]), (6, 1, k_t[:, 1, kj, :]), (7, 1, ck_t[:, kj, :])):
                        mm = nc.tensor.matmul(ps[bank][:, j * T:(j + 1) * T], q_t[:, g, j, :], keys, start=True, stop=True)
                if near:
                    pe.wait_ge(rpb_landed, 16 * 4 * (i + 1))
                    mm = nc.tensor.matmul(ps[4][:, :], flip[:, :], rpb[:, :, :], start=True, stop=True)
                mm.then_inc(scores_done, 1)
                pe.wait_ge(probs_ready, i + 1)
                for j in range(4):
                    nc.tensor.transpose(ps[0][:, j * T:(j + 1) * T], prob_p[:, j, :], ident[:, :])
                    nc.tensor.transpose(ps[1][:, j * T:(j + 1) * T], prob_s[:, j, 0:T], ident[:, :])
                    mm = nc.tensor.transpose(ps[2][:, j * T:(j + 1) * T], prob_s[:, j, T:2 * T], ident[:, :])
                mm.then_inc(probs_turned, 1)
                pe.wait_ge(probs_copied_act, i + 1)
                pe.wait_ge(probs_copied_dve, i + 1)
                for j in range(nk):
                    n = 4 * T // nk
                    cols = slice(j * n, (j + 1) * n)
                    keys = slice(q0 + j * n, q0 + (j + 1) * n)
                    vj = slice(v0 + j * HD, v0 + (j + 1) * HD)
                    nc.tensor.matmul(ps[3][:, cols], qkv[:, 0, vj], qkv[:, 0, keys], start=True, stop=True)
                    nc.tensor.matmul(ps[4][:, cols], qkv[:, 1, vj], qkv[:, 1, keys], start=True, stop=False)
                    mm = nc.tensor.matmul(ps[4][:, cols], ctx_v[:, h0 + j, :],
                                          pc_t[:, j * (4 // nk):(j + 1) * (4 // nk), :], start=False, stop=True)
                mm.then_inc(pv_done, 1)

            for s in sweeps:
                s.xt_ready = None
            S["att_in_a"].xt_ready = (xt_ready, 0, 1)
            S["att_out_a"].xt_ready = (heads_ready, 0, 2)
            S["ff1_0"].xt_ready = (xt_ready, KC // 2, 1)
            S["rec_in_a"].xt_ready = (xt_ready, 2 * KC // 2, 1)
            S["rec_out"].xt_ready = (y_split, 0, 1)
            S["ff1_1"].xt_ready = (xt_ready, 3 * KC // 2, 1)

            pe.wait_ge(vec_a_landed, 16)
            pe.wait_ge(id_landed, 32)
            nc.tensor.transpose(ps[5][:, 0:96], stage[0:96, 0, :], ident[0:96, 0:96]).then_inc(vec_turned, 1)
            pe.wait_ge(vec_r_landed, 32)
            nc.tensor.transpose(ps[6][:, 0:112], stage[0:112, 1, :], ident[0:112, 0:112])
            nc.tensor.transpose(ps[6][:, 112:208], stage[0:96, 2, :], ident[0:96, 0:96]).then_inc(vec_turned, 1)
            pe.wait_ge(vec_ready, 2)
            pe.wait_ge(cond_ready, 1)
            last = iterations(pe, S["ada0"], body, None)
            ada_end(*last)
            turn_normed(0)
            last = iterations(pe, S["att_in_a"], body, None)
            last = iterations(pe, S["att_in_b"], body, last)
            ada_end(*last)
            for i in range(4):
                attention(i)
            last = iterations(pe, S["att_out_a"], body, None)
            last = iterations(pe, S["att_out_b"], body, last)
            turn_normed(1)
            last = iterations(pe, S["ff1_0"], body, None)
            last = iterations(pe, S["ff2_0"], body, last)
            turn_normed(2)
            last = iterations(pe, S["rec_in_a"], body, None)
            last = iterations(pe, S["rec_in_b"], body, last)
            ada_end(*last)
            with pe.Fori(0, KC // 4) as it:
                for s in range(2):
                    pe.wait_ge(rg_landed[s], 128 * (it + 1))
                    pe.wait_ge(conv_ready, 2 * it + s + 1)
                    pe.wait_ge(gates_read, 2 * it + s + 1)
                    for c in range(2):
                        for k in range(4):
                            at = (k % 2) * NG * T
                            mm = nc.tensor.matmul(ps[4 + 2 * c + k // 2][:, at:at + NG * T],
                                                  w_rg[:, s, c, k, :], xc[:, c, :, :], start=True, stop=True)
                    mm.then_inc(gates_done, 1)
            pe.wait_ge(y_split, KC // 2)
            nc.tensor.matmul(ps[7][0:2 * KC, 0:P], states, ident[:, :], start=True, stop=True).then_inc(states_turned, 1)
            last = iterations(pe, S["rec_out"], body, None)
            ada_end(*last)
            turn_normed(3)
            last = iterations(pe, S["ff1_1"], body, None)
            last = iterations(pe, S["ff2_1"], body, last)

        @block.scalar
        def _(act):
            def split(s, it, h):
                n = s.half0 + it * s.halves + h
                t, q = divmod(h, 2)
                p = [i for i, k in enumerate(s.order) if k == "M"][t]
                slot, landed = stream(s, it, p)
                if s.tiles == 16:
                    if first(it):
                        act.wait_ge(hidden_ready, hidden0[s.name] + 2 * h + 2)
                if q == 0:
                    act.wait_ge(raw_landed[slot], landed)
                if not isinstance(n, int) or n >= NSPLIT:
                    act.wait_ge(half_used, n - NSPLIT + 1)
                if s.tiles == 16:
                    c = 2 * h % KC
                    nc.scalar.activation(xt[:, c:c + 2, 0:NG * T], hidden[:, 2 * h:2 * h + 2, :], ACT.Copy)
                nc.scalar.activation(w_hi[:, h % NSPLIT, :, :], raw[:, slot, 2 * q:2 * q + 2, :], ACT.Copy)\
                    .then_inc(hi_ready, 1)

            def out_ready(s, blk, g):
                if g == 0:
                    act.wait_ge(g0_done, s.token0 + blk + 1)
                else:
                    act.wait_ge(half_used, s.half0 + (blk + 1) * 2 * s.tiles)

            def token_out(s, blk, g):
                out_ready(s, blk, g)
                if s.out == "qkv":
                    nc.scalar.activation(qkv[:, g, bass.ds((s.col0 + blk) * BLK, BLK)], ps[g][:, :], ACT.Copy)\
                        .then_inc(out_read_act, 1)
                else:
                    act.wait_ge(out_read_act, NG * (s.token0 + blk) + g)
                    nc.scalar.activation(ps[7][:, :], ps[g][:, :], ACT.Square,
                                         accum_out=ssq[:, g, bass.ds(s.col0 + blk, 1)]).then_inc(out_read_act, 1)

            def feature_out(s, blk, m):
                if m < 3:
                    act.wait_ge(chunk_done, 3 * (s.feature0 + blk) + m + 1)
                else:
                    act.wait_ge(half_used, s.half0 + (blk + 1) * 2 * s.tiles)
                dst = hidden[:, bass.ds(4 * (s.col0 + blk) + m, 1), :]
                nc.scalar.activation(dst, ps[m][:, NG * T:2 * NG * T].rearrange("p (o t) -> p o t", o=1), ACT.Copy)\
                    .then_inc(lo_copied, 1)

            def body(s, it, before):
                for b in range(s.blocks):
                    last = (s, it * s.blocks + b - 1) if b else (before and (before[0], before[1] * before[0].blocks + before[0].blocks - 1))
                    for hh in range(2 * s.tiles):
                        h = b * 2 * s.tiles + hh
                        split(s, it, h)
                        if last and last[0].mode == "token" and hh in (1, 2):
                            token_out(*last, hh - 1)
                        if last and last[0].mode == "feature" and hh == 1:
                            for m in range(4):
                                feature_out(*last, m)

            def flush(last):
                s, it = last
                blk = it * s.blocks + s.blocks - 1
                if s.mode == "token":
                    for g in range(NG):
                        token_out(s, blk, g)
                else:
                    for m in range(4):
                        feature_out(s, blk, m)

            def squares_of_x(n):
                for k in range(4):
                    g, c = divmod(k, 2)
                    if n == 0:
                        act.wait_ge(x_landed, 32)
                    else:
                        act.wait_ge(x_ready, 4 * (n - 1) + k + 1)
                    nc.scalar.activation(junk[:, k, :], x[:, g, c * 1024:(c + 1) * 1024], ACT.Square,
                                         accum_out=ssq_x[:, g, c:c + 1]).then_inc(ssq_ready, 1)

            def norm(n):
                for j in range(KC // 2):
                    act.wait_ge(mod_ready, n * KC // 2 + j + 1)
                    nc.scalar.activation(xt[:, 2 * j:2 * j + 2, 0:NG * T],
                                         h_mod[:, j % 2].rearrange("p c g t -> p c (g t)"), ACT.Copy).then_inc(mod_hi, 1)

            def attention(i):
                near = i < 2
                q0 = QA0 + i * BLK if near else QB0 + (i - 2) * BLK
                act.wait_ge(qk_turned, i + 1)
                nc.scalar.activation(q_t[:, 0].rearrange("p h t -> p (h t)"), ps[0][:, :], ACT.Copy)
                n = BLK if near else T
                nc.scalar.activation(k_t[:, 0].rearrange("p h t -> p (h t)")[:, 0:n], ps[2][:, 0:n], ACT.Copy)\
                    .then_inc(qk_copied_act, 1)
                act.wait_ge(scores_done, i + 1)
                nc.scalar.activation(prob_s[:, :, T:2 * T], ps[7][:, :].rearrange("p (h t) -> p h t", h=4), ACT.Copy, scale=SCALE)
                if not near:
                    nc.scalar.activation(prob_s[:, :, 0:T], ps[6][:, :].rearrange("p (h t) -> p h t", h=4), ACT.Copy, scale=SCALE)
                nc.scalar.activation(prob_p.rearrange("p h t -> p (h t)"), ps[5][:, :], ACT.Copy, scale=SCALE).then_inc(scores_scaled, 1)
                act.wait_ge(max_ready, i + 1)
                if not near:
                    nc.scalar.activation(sink_e, sink_e, ACT.Exp)
                for g, pr in ((0, prob_p), (1, prob_s)):
                    for j in range(4):
                        e = nc.scalar.activation(pr[:, j, :], pr[:, j, :], ACT.Exp, bias=mx[:, g, j:j + 1],
                                                 accum_out=den[:, g, j:j + 1])
                e.then_inc(exp_done, 1)
                act.wait_ge(probs_turned, i + 1)
                nc.scalar.activation(qkv[:, 0, q0:q0 + BLK], ps[0][:, :], ACT.Copy).then_inc(probs_copied_act, 1)
                act.wait_ge(pv_done, i + 1)
                for g in range(NG):
                    e = nc.scalar.activation(xt[:, 4 * i:4 * i + 4, g * T:(g + 1) * T],
                                             ps[3 + g][:, :].rearrange("p (h t) -> p h t", h=4), ACT.Copy)
                e.then_inc(heads_hi, 1)

            steps = Steps(act, act_step)

            hidden0 = {"ff2_0": 0, "ff2_1": 4 * FF // BLK}

            act.wait_ge(vec_ready, 1)
            nc.scalar.activation(silu_t[:, 0, :], vec_a[:, 0:2 * KC], ACT.Tanh, scale=0.5).then_inc(cond_tanh, 1)
            act.wait_ge(lam_abs, 1)
            nc.scalar.activation(lam_t[:, 1, :], lam_t[:, 0, :], ACT.Exp, scale=-1.0).then_inc(lam_exp, 1)
            squares_of_x(0)
            norm(0)
            last = iterations(act, S["att_in_a"], body, None)
            last = iterations(act, S["att_in_b"], body, last)
            flush(last)
            for i in range(4):
                attention(i)
            last = iterations(act, S["att_out_a"], body, None)
            last = iterations(act, S["att_out_b"], body, last)
            flush(last)
            squares_of_x(1)
            norm(1)
            last = iterations(act, S["ff1_0"], body, None)
            last = iterations(act, S["ff2_0"], body, last)
            flush(last)
            squares_of_x(2)
            norm(2)
            last = iterations(act, S["rec_in_a"], body, None)
            last = iterations(act, S["rec_in_b"], body, last)
            flush(last)
            with act.Fori(0, KC // 4) as it:
                steps.n, steps.ahead = 0, it * (2 * 5)
                for s in range(2):
                    pair = 2 * it + s
                    act.wait_ge(gates_done, pair + 1)
                    for c in range(2):
                        for d in range(2):
                            cols = [vec_r[:, bass.ds(base + d * KC + pair * 2 + c, 1)] for base in (B_A, LAM, B_X)]
                            steps(nc.scalar.activation(th_a[:, d, :], ps[4 + 2 * c][:, d * NG * T:(d + 1) * NG * T],
                                                       ACT.Tanh, scale=0.5, bias=cols[0]))
                            nc.scalar.activation(tt[:, c, d, :], th_a[:, d, :], ACT.Tanh, scale=cols[1], bias=cols[1])
                            e = nc.scalar.activation(th_i[:, c, d, :], ps[5 + 2 * c][:, d * NG * T:(d + 1) * NG * T],
                                                     ACT.Tanh, scale=0.5, bias=cols[2])
                    steps(e)
                    nc.scalar.activation(root.rearrange("p c d n -> p (c d n)"), tt.rearrange("p c d n -> p (c d n)"),
                                         ACT.Sqrt).then_inc(gates_read, 1)
                    act.wait_ge(gelu_arg, pair + 1)
                    nc.scalar.activation(gel, gel, ACT.Tanh).then_inc(gelu_tanh, 1)
                    act.wait_ge(y_ready, pair + 1)
                    nc.scalar.activation(xt[:, bass.ds(2 * pair, 2), 0:NG * T],
                                         xr[:, bass.ds(2 * pair, 2)].rearrange("p c g t -> p c (g t)"), ACT.Copy)\
                        .then_inc(y_hi, 1)
            last = iterations(act, S["rec_out"], body, None)
            flush(last)
            squares_of_x(3)
            norm(3)
            last = iterations(act, S["ff1_1"], body, None)
            last = iterations(act, S["ff2_1"], body, last)
            flush(last)

        @block.vector
        def _(dve):
            steps = Steps(dve, dve_step)
            V = nc.vector

            def split(s, it, h):
                n = s.half0 + it * s.halves + h
                t, q = divmod(h, 2)
                slot = [i for i, k in enumerate(s.order) if k == "M"][t] % NRAW
                dve.wait_ge(hi_ready, n + 1)
                if s.tiles == 16:
                    c = 2 * h % KC
                    V.tensor_tensor(xt[:, c:c + 2, NG * T:2 * NG * T], hidden[:, 2 * h:2 * h + 2, :],
                                    xt[:, c:c + 2, 0:NG * T].bitcast(fp32), ALU.subtract)
                V.tensor_tensor(w_lo[:, h % NSPLIT, :, :], raw[:, slot, 2 * q:2 * q + 2, :],
                                w_hi[:, h % NSPLIT, :, :].bitcast(fp32), ALU.subtract).then_inc(lo_ready, 1)

            def token_out(s, blk, g):
                if s.out == "op":
                    dve.wait_ge(out_read_act, NG * (s.token0 + blk) + g + 1)
                    dst = gate[:, g, bass.ds((s.col0 + blk) * BLK, BLK)]
                    V.tensor_tensor(dst, ps[g][:, :], dst, ALU.mult).then_inc(out_read_dve, 1)

            def feature_out(s, blk, m):
                n = 4 * (s.feature0 + blk) + m
                dve.wait_ge(lo_copied, n + 1)
                dst = hidden[:, bass.ds(4 * (s.col0 + blk) + m, 1), :].rearrange("p o t -> p (o t)")
                V.tensor_tensor(dst, ps[m][:, 0:NG * T], dst, ALU.add).then_inc(chunk_read, 1)
                if s.out == "hidden":
                    dve.wait_ge(chunk_read, n + 1)
                    V.scalar_tensor_tensor(out=dst, in0=dst, scalar=0.0, in1=dst, op0=ALU.max, op1=ALU.mult)\
                        .then_inc(hidden_ready, 1)

            def ada_rows_out(s, it):
                b = s.ada0 + it
                dve.wait_ge(ada_used, TILE * (b + 1))
                dve.wait_ge(bias_landed, 16 * (b + 1))
                if not (isinstance(b, int) and b == 0):
                    dve.wait_ge(ada_small, b)
                V.tensor_tensor(ada_rows[:, :], ps[4][:, :], bias_rows[:, :], ALU.add).then_inc(ada_row, 1)

            def ada_store(s, it):
                b = s.ada0 + it
                dve.wait_ge(ada_small, b + 1)
                if s.ada == "cols":
                    base = s.ada_at[1] - (12 if s.ada_at[1] >= 12 else 0)
                    flat = ada_cols[:, :, :, :].rearrange("p a c g -> p (a c g)")
                    V.tensor_copy(flat[:, bass.ds((base + it) * 4 * NG, 4 * NG)], ps[5][:, 0:4 * NG]).then_inc(ada_fin, 1)
                else:
                    dve.wait_ge(gain_landed, 16 * (s.gate0 + it + 1))
                    for g in range(NG):
                        e = V.tensor_tensor(gate[:, g, bass.ds(it * BLK, BLK)], ps[5 + g][:, :], gain_rows[:, :], ALU.mult)
                    e.then_inc(ada_fin, 1)

            def body(s, it, before):
                if s.mode is None:
                    if before:
                        ada_store(*before)
                    ada_rows_out(s, it)
                    return
                for b in range(s.blocks):
                    last = (s, it * s.blocks + b - 1) if b else (before and (before[0], before[1] * before[0].blocks + before[0].blocks - 1))
                    for hh in range(2 * s.tiles):
                        h = b * 2 * s.tiles + hh
                        split(s, it, h)
                        if last and last[0].mode == "token" and hh in (1, 2):
                            if last[0].out == "op" and hh == 1:
                                dve.wait_ge(ada_fin, gate_of(*last))
                            token_out(*last, hh - 1)
                        if last and last[0].mode == "feature" and hh == 1:
                            for m in range(4):
                                feature_out(*last, m)
                        if before and before[0].ada and before[0].skew and b == 0:
                            if hh == 2:
                                ada_rows_out(*before)
                            if hh == 7:
                                ada_store(*before)
                        if not s.skew and hh == 19:
                            ada_rows_out(s, it)
                        if not s.skew and hh == 25:
                            ada_store(s, it)

            def gate_of(s, blk):
                return {"att_out_a": 12, "att_out_b": 12, "ff2_0": S["ff2_0"].ada0 + blk + 1,
                        "rec_out": S["rec_in_a"].ada0 + 4, "ff2_1": S["ff2_1"].ada0 + blk + 1}[s.name]

            def flush(last):
                s, it = last
                blk = it * s.blocks + s.blocks - 1
                if s.mode == "token":
                    if s.out == "op":
                        dve.wait_ge(ada_fin, gate_of(s, blk))
                    for g in range(NG):
                        token_out(s, blk, g)
                else:
                    for m in range(4):
                        feature_out(s, blk, m)

            def mean_of(sums, b):
                steps(V.tensor_reduce(mean, sums, AX, ALU.add))
                V.tensor_scalar(mean, mean, 1.0 / D, EPS, ALU.mult, ALU.add).then_inc(mean_ready, 1)

            def residual(n):
                dve.wait_ge(out_read_dve, NG * (blocks_done[n] - QKV_BLOCKS))
                mean_of(ssq, 4)
                dve.wait_ge(rstd_ready, 2 * n)
                for k in range(4):
                    g, c = divmod(k, 2)
                    cols = slice(c * 1024, (c + 1) * 1024)
                    V.scalar_tensor_tensor(out=x[:, g, cols], in0=gate[:, g, cols], scalar=rstd[:, g:g + 1],
                                           in1=x[:, g, cols], op0=ALU.mult, op1=ALU.add).then_inc(x_ready, 1)

            def norm(n, gain):
                dve.wait_ge(ssq_ready, 4 * (n + 1))
                mean_of(ssq_x, 2)
                dve.wait_ge(ada_fin, norm_ada[n])
                steps(V.scalar_tensor_tensor(out=gs, in0=ada_cols[:, 1], scalar=1.0,
                                             in1=vec_a[:, gain:gain + KC].unsqueeze(2).broadcast_to([P, KC, NG]),
                                             op0=ALU.add, op1=ALU.mult))
                dve.wait_ge(rstd_ready, 2 * n + 1)
                for g in range(NG):
                    e = V.tensor_scalar(diag[:, g, :], ident[:, :], rstd[:, g:g + 1], None, ALU.mult)
                e.then_inc(diag_ready, 1)

                def rest(j):
                    dve.wait_ge(mod_hi, n * KC // 2 + j + 1)
                    V.tensor_tensor(xt[:, 2 * j:2 * j + 2, NG * T:2 * NG * T],
                                    h_mod[:, j % 2].rearrange("p c g t -> p c (g t)"),
                                    xt[:, 2 * j:2 * j + 2, 0:NG * T].bitcast(fp32), ALU.subtract).then_inc(xt_ready, 1)

                for j in range(KC // 2):
                    dve.wait_ge(turned, n * KC // 2 + j + 1)
                    if j >= 2:
                        dve.wait_ge(xt_ready, n * KC // 2 + j - 1)
                    for c in range(2):
                        for g in range(NG):
                            at = (c * NG + g) * T
                            e = V.tensor_scalar(h_mod[:, j % 2, c, g, :], ps[4 + j % 4][:, at:at + T],
                                                gs[:, 2 * j + c, g:g + 1], ada_cols[:, 0, 2 * j + c, g:g + 1],
                                                ALU.mult, ALU.add)
                    e.then_inc(mod_ready, 1)
                    if j:
                        rest(j - 1)
                rest(KC // 2 - 1)

            def rope():
                dve.wait_ge(const_landed, 16 * 5)
                dve.wait_ge(out_read_act, NG * QKV_BLOCKS)
                qk = qkv[:, 1, QB0:VB0].rearrange("p (h a f) -> p h a f", h=10, a=2)
                x1, x2 = qk[:, :, :, 0:32], qk[:, :, :, 32:64]
                cos = rope_cos[:, :].rearrange("p (a f) -> p a f", a=2).unsqueeze(1).broadcast_to([P, 10, 2, 32])
                sin = rope_sin[:, :].rearrange("p (a f) -> p a f", a=2).unsqueeze(1).broadcast_to([P, 10, 2, 32])
                V.tensor_tensor(rope_a, x2, sin, ALU.mult)
                steps(V.tensor_tensor(rope_b, x1, sin, ALU.mult))
                V.tensor_tensor(x1, x1, cos, ALU.mult)
                steps(V.tensor_tensor(x2, x2, cos, ALU.mult))
                V.tensor_tensor(x1, x1, rope_a, ALU.subtract)
                V.tensor_tensor(x2, x2, rope_b, ALU.add).then_inc(roped, 1)

            def attention(i):
                near = i < 2
                q0 = QA0 + i * BLK if near else QB0 + (i - 2) * BLK
                n = BLK if near else T
                dve.wait_ge(qk_turned, i + 1)
                V.tensor_copy(q_t[:, 1].rearrange("p h t -> p (h t)"), ps[1][:, :])
                V.tensor_copy(k_t[:, 1].rearrange("p h t -> p (h t)")[:, 0:n], ps[3][:, 0:n])
                V.tensor_copy(ck_t.rearrange("p h t -> p (h t)")[:, 0:n], ps[4][:, 0:n]).then_inc(qk_copied_dve, 1)
                dve.wait_ge(scores_done, i + 1)
                if near:
                    steps(V.tensor_tensor(rpb[:, :, :], ps[4][:, :].rearrange("p (h t) -> p h t", h=4),
                                          window[:, :].unsqueeze(1).broadcast_to([P, 4, T]), ALU.add))
                    V.scalar_tensor_tensor(out=prob_s[:, :, 0:T], in0=ps[6][:, :].rearrange("p (h t) -> p h t", h=4),
                                           scalar=SCALE, in1=rpb[:, :, :], op0=ALU.mult, op1=ALU.add).then_inc(bias_used, 1)
                    dve.wait_ge(bias_used, i + 1)
                dve.wait_ge(scores_scaled, i + 1)
                V.tensor_reduce(mx[:, 0, :], prob_p, AX, ALU.max)
                steps(V.tensor_reduce(mx[:, 1, :], prob_s, AX, ALU.max))
                if not near:
                    sinks = sink[:, 4 * (i - 2):4 * (i - 1)].unsqueeze(1).broadcast_to([P, NG, 4])
                    steps(V.tensor_tensor(mx, mx, sinks, ALU.max))
                    steps(V.tensor_tensor(sink_e, sinks, mx, ALU.subtract))
                m = V.tensor_scalar(mx, mx, -1.0, None, ALU.mult)
                m.then_inc(max_ready, 1)
                dve.wait_ge(exp_done, i + 1)
                if not near:
                    steps(V.tensor_tensor(den, den, sink_e, ALU.add))
                steps(V.reciprocal(den, den))
                V.tensor_tensor(prob_p, prob_p, den[:, 0, :].unsqueeze(2).broadcast_to([P, 4, T]), ALU.mult)
                V.tensor_tensor(prob_s, prob_s, den[:, 1, :].unsqueeze(2).broadcast_to([P, 4, 2 * T]), ALU.mult)\
                    .then_inc(probs_ready, 1)
                dve.wait_ge(probs_turned, i + 1)
                V.tensor_copy(qkv[:, 1, q0:q0 + BLK], ps[1][:, :])
                V.tensor_copy(pc_t.rearrange("p h t -> p (h t)"), ps[2][:, :]).then_inc(probs_copied_dve, 1)
                dve.wait_ge(heads_hi, i + 1)
                for g in range(NG):
                    e = V.tensor_tensor(xt[:, 4 * i:4 * i + 4, (NG + g) * T:(NG + g + 1) * T],
                                        ps[3 + g][:, :].rearrange("p (h t) -> p h t", h=4),
                                        xt[:, 4 * i:4 * i + 4, g * T:(g + 1) * T].bitcast(fp32), ALU.subtract)
                e.then_inc(heads_ready, 1)

            def decay_rates():
                lam = vec_r[:, LAM:LAM + 2 * KC]
                L = [lam_t[:, a, :] for a in range(6)]
                V.tensor_scalar(vec_r[:, B_A:B_A + 4 * KC], vec_r[:, B_A:B_A + 4 * KC], 0.5, None, ALU.mult)
                V.scalar_tensor_tensor(out=L[0], in0=lam, scalar=-1.0, in1=lam, op0=ALU.mult, op1=ALU.max)\
                    .then_inc(lam_abs, 1)
                dve.wait_ge(lam_exp, 1)
                steps(V.tensor_scalar(L[2], L[1], 2.0, None, ALU.add))
                steps(V.reciprocal(L[2], L[2]))
                steps(V.tensor_tensor(L[2], L[1], L[2], ALU.mult))
                steps(V.tensor_tensor(L[3], L[2], L[2], ALU.mult))
                steps(V.tensor_scalar(L[4], L[3], 1.0 / 17, None, ALU.mult))
                for k in range(15, 1, -2):
                    steps(V.scalar_tensor_tensor(out=L[4], in0=L[4], scalar=1.0 / k, in1=L[3], op0=ALU.add, op1=ALU.mult))
                steps(V.scalar_tensor_tensor(out=L[4], in0=L[4], scalar=1.0, in1=L[2], op0=ALU.add, op1=ALU.mult))
                steps(V.tensor_scalar(L[5], lam, -1.0, 0.0, ALU.mult, ALU.max))
                steps(V.scalar_tensor_tensor(out=L[5], in0=L[4], scalar=2.0, in1=L[5], op0=ALU.mult, op1=ALU.add))
                V.tensor_scalar(lam, L[5], 2.0, None, ALU.mult).then_inc(rg_ready, 1)

            def rg_pair(pair):
                def param(base, c):
                    return vec_r[:, bass.ds(base + 2 * pair + c, 1)]

                xs = [xr[:, bass.ds(2 * pair + c, 1)].rearrange("p o g t -> p (o g) t") for c in range(2)]
                two = xr[:, bass.ds(2 * pair, 2)].rearrange("p c g t -> p c (g t)")
                g2 = gr[:, bass.ds(2 * pair, 2), :]
                for c in range(2):
                    e = V.tensor_scalar(xc[:, c], xs[c], param(CONV_W + 2 * KC, c), param(CONV_B, c), ALU.mult, ALU.add)
                steps(e)
                for tap, back in ((0, 2), (1, 1)):
                    for c in range(2):
                        e = V.scalar_tensor_tensor(out=xc[:, c, :, back:], in0=xs[c][:, :, 0:T - back],
                                                   scalar=param(CONV_W + tap * KC, c), in1=xc[:, c, :, back:],
                                                   op0=ALU.mult, op1=ALU.add)
                    steps(e)
                for c in range(2):
                    e = V.scalar_tensor_tensor(out=xc[:, c, :, 0:T - 1], in0=xs[c][:, :, 1:T],
                                               scalar=param(CONV_W + 3 * KC, c), in1=xc[:, c, :, 0:T - 1],
                                               op0=ALU.mult, op1=ALU.add)
                e.then_inc(conv_ready, 1)
                steps(V.tensor_tensor(gel, g2, g2, ALU.mult))
                steps(V.tensor_scalar(gel, gel, 0.044715 * GELU_C, GELU_C, ALU.mult, ALU.add))
                V.tensor_tensor(gel, gel, g2, ALU.mult).then_inc(gelu_arg, 1)
                dve.wait_ge(gates_read, pair + 2)
                t_, i_, r_, v_ = (z.rearrange("p c d n -> p (c d n)") for z in (tt, inv, root, th_i))
                steps(V.tensor_scalar(i_, t_, 1.0, None, ALU.add))
                V.tensor_scalar(t_, t_, -1.0, 1.0, ALU.mult, ALU.add)
                steps(V.reciprocal(i_, i_))
                V.tensor_tensor(t_, t_, i_, ALU.mult)
                steps(V.tensor_tensor(r_, r_, i_, ALU.mult))
                for c in range(2):
                    xcb = xc[:, c].rearrange("p g t -> p (g t)").unsqueeze(1).broadcast_to([P, 2, NG * T])
                    e = V.scalar_tensor_tensor(out=th_i[:, c], in0=th_i[:, c], scalar=1.0, in1=xcb,
                                               op0=ALU.add, op1=ALU.mult)
                steps(e)
                steps(V.tensor_tensor(v_, v_, r_, ALU.mult))
                for c in range(2):
                    for d in range(2):
                        for g in range(NG):
                            way = slice(None, None, -1) if d else slice(None)
                            a, b, h = (z[:, c, d, g * T:(g + 1) * T][:, way] for z in (tt, th_i, root))
                            e = V.tensor_tensor_scan(h, a, b, 0.0 if g == 0 else param(H0 + d * KC, c), ALU.mult, ALU.add)
                steps(e)
                for d in range(2):
                    end = 0 if d else T - 1
                    V.tensor_copy(states[:, bass.ds(d * KC + 2 * pair, 2)], root[:, :, d, end])
                steps(V.tensor_tensor(two, root[:, :, 0, :], root[:, :, 1, :], ALU.add))
                dve.wait_ge(gelu_tanh, pair + 1)
                steps(V.scalar_tensor_tensor(out=gel, in0=gel, scalar=1.0, in1=g2, op0=ALU.add, op1=ALU.mult))
                V.scalar_tensor_tensor(out=two, in0=gel, scalar=0.5, in1=two, op0=ALU.mult, op1=ALU.mult)\
                    .then_inc(y_ready, 1)
                dve.wait_ge(y_hi, pair + 1)
                V.tensor_tensor(xt[:, bass.ds(2 * pair, 2), NG * T:2 * NG * T], two,
                                xt[:, bass.ds(2 * pair, 2), 0:NG * T].bitcast(fp32), ALU.subtract).then_inc(y_split, 1)

            blocks_done = {1: 13, 2: 17, 3: 21, 4: 25}
            norm_ada = {0: 8, 1: 20, 2: 28, 3: 44}

            V.memset(bias_rows[:, :], 0.0)
            V.memset(half_neg, -0.5)
            steps(V.memset(cond[:, :, :], 0.0))
            V.memset(ssq_x, 0.0).then_inc(cleared, 1)
            dve.wait_ge(vec_turned, 1)
            V.tensor_copy(vec_a[:, :], ps[5][:, 0:96]).then_inc(vec_ready, 1)
            dve.wait_ge(cond_tanh, 1)
            steps(V.scalar_tensor_tensor(out=silu_t[:, 1, :], in0=silu_t[:, 0, :], scalar=1.0, in1=vec_a[:, 0:2 * KC],
                                         op0=ALU.add, op1=ALU.mult))
            V.tensor_scalar(cond[:, :, 0:NG].rearrange("p c g -> p g c"),
                            silu_t[:, 1, :].rearrange("p (g c) -> p g c", g=NG), 0.5, None, ALU.mult).then_inc(cond_ready, 1)
            dve.wait_ge(vec_turned, 2)
            V.tensor_copy(vec_r[:, :], ps[6][:, 0:208]).then_inc(vec_ready, 1)
            dve.wait_ge(vec_ready, 2)
            decay_rates()
            last = iterations(dve, S["ada0"], body, None)
            ada_store(*last)
            norm(0, 2 * KC)
            last = iterations(dve, S["att_in_a"], body, None)
            last = iterations(dve, S["att_in_b"], body, last)
            flush(last)
            ada_rows_out(*last)
            ada_store(*last)
            rope()
            for i in range(4):
                attention(i)
            last = iterations(dve, S["att_out_a"], body, None)
            last = iterations(dve, S["att_out_b"], body, last)
            flush(last)
            residual(1)
            norm(1, 4 * KC)
            last = iterations(dve, S["ff1_0"], body, None)
            last = iterations(dve, S["ff2_0"], body, last)
            flush(last)
            residual(2)
            norm(2, 3 * KC)
            last = iterations(dve, S["rec_in_a"], body, None)
            last = iterations(dve, S["rec_in_b"], body, last)
            flush(last)
            ada_rows_out(*last)
            ada_store(*last)
            dve.wait_ge(chunk_read, 4 * (S["rec_in_b"].feature0 + 4))
            V.memset(mean, 0.0).then_inc(gates_read, 1)
            base = steps.n
            PER = 2 * 13
            with dve.Fori(0, KC // 4) as it:
                steps.n, steps.ahead = base, it * PER
                for s in range(2):
                    rg_pair(2 * it + s)
                assert steps.n - base == PER, steps.n - base
            steps.n, steps.ahead = base + PER * (KC // 4), 0
            dve.wait_ge(states_turned, 1)
            V.tensor_copy(state_rows, ps[7][0:2 * KC, 0:P]).then_inc(state_rows_ready, 1)
            last = iterations(dve, S["rec_out"], body, None)
            flush(last)
            ada_rows_out(*last)
            ada_store(*last)
            residual(3)
            norm(3, 5 * KC)
            last = iterations(dve, S["ff1_1"], body, None)
            last = iterations(dve, S["ff2_1"], body, last)
            flush(last)
            residual(4)


_OUTS = [("y_prompt", (1, T, D)), ("y_sample", (1, T, D)),
         ("new_a_k", (1, 1, T, NA, HD)), ("new_a_v", (1, 1, T, NA, HD)),
         ("new_b_k", (1, 1, T, NKV, HD)), ("new_b_v", (1, 1, T, NKV, HD)),
         ("new_rg_fwd", (1, 1, D)), ("new_rg_bwd", (1, 1, D))]
_WHOLE = ["x_prompt", "x_sample", "cache_a_k", "cache_a_v", "cache_b_k", "cache_b_v", "w_ada", "b_ada",
          "g_post_mix", "g_post_ffn", "w_att_in", "w_att_out", "sink_b", "rpb_a", "w_rec_in", "w_rg_a",
          "w_rg_x", "w_rec_out", "w_ff1", "w_ff2"]


def tables(np):
    t = np.arange(T)
    flip = np.zeros((P, P), np.float32)
    flip[(t // GRID_W) * GRID_W + GRID_W - 1 - t % GRID_W, t] = 1
    sel = np.zeros((P, NG), np.float32)
    for j in range(TILE):
        for g in range(NG):
            sel[32 * j + g, g] = 1
    col = t % GRID_W
    start = np.clip(col - 8, 0, GRID_W - 16)[:, None]
    window = np.where((col[None, :] >= start) & (col[None, :] < start + 16), 0.0, -1e30).astype(np.float32)
    inv = np.float32(10000.0) ** (-np.arange(0, 64, 2, dtype=np.float32) / np.float32(64))
    ang = np.concatenate([(t // GRID_W).astype(np.float32)[:, None] * inv,
                          (t % GRID_W).astype(np.float32)[:, None] * inv], axis=1).astype(np.float32)
    return {"ident": np.eye(P, dtype=np.float32), "flip": flip, "sel": sel, "window": window,
            "rope_cos": np.cos(ang), "rope_sin": np.sin(ang)}


def kernel(**inputs):
    import numpy as np
    import concourse.bacc as bacc
    from concourse.bass_utils import run_bass_kernel_spmd

    nc = bacc.Bacc("TRN2", target_bir_lowering=False, num_devices=1)
    given = {k: np.ascontiguousarray(v) for k, v in inputs.items()}
    rows = [given[k].reshape(-1, P) for k in ("c_ctx", "c", "g_pre_mix", "g_pre_ffn", "conv_w", "conv_b",
                                              "b_rg_a", "b_rg_x", "rg_lambda", "state_rg_fwd", "state_rg_bwd")]
    host = {k: given[k] for k in _WHOLE}
    host["vectors"] = np.concatenate(rows, axis=0)
    host.update(tables(np))
    arrays, A, out = {}, {}, {}
    for name, a in host.items():
        arrays[f"in_{name}"] = a
        A[name] = nc.dram_tensor(f"in_{name}", a.shape, mybir.dt.from_np(a.dtype), kind="ExternalInput").ap()
    for name, shape in _OUTS:
        out[name] = nc.dram_tensor(f"out_{name}", shape, mybir.dt.float32, kind="ExternalOutput").ap()
    hybrid_step(nc, A, out)
    r = run_bass_kernel_spmd(nc, [arrays], core_ids=[0])
    return tuple(r.results[0][f"out_{name}"] for name, _ in _OUTS)
```

```python
import concourse.bass as bass
from concourse import mybir
from contextlib import ExitStack

D = 2048
T = 128
NG = 2
P = 128
KC = D // P
FF = 4 * D
HD = 128
NA = 8
NKV = 2
QKV_W = 3 * NA * HD + NA * HD + 2 * NKV * HD
QA0, KA0, VA0, QB0, KB0, VB0 = 0, 1024, 2048, 3072, 4096, 4352
GRID_W = 64
RPB_ROWS, RPB_COLS = 15, 31
EPS = 1e-6
SCALE = float(HD) ** -0.5
BLK = 512
QKV_BLOCKS = QKV_W // BLK
TILE = 4
NRAW = 4
NSPLIT = 4
GELU_C = 0.7978845608028654


class Sweep:

    def __init__(self, name, n, mode, weight, col0, tiles, blocks, ada, ada_at, order, out, skew=True):
        self.name, self.n, self.mode = name, n, mode
        self.weight, self.col0 = weight, col0
        self.tiles, self.blocks = tiles, blocks
        self.ada, self.ada_at = ada, ada_at
        self.order = order
        self.out = out
        self.skew = skew
        self.halves = 2 * order.count("M")
        assert order.count("M") == tiles * blocks and len(order) % NRAW == 0


def plan(w):
    ma = "MA" * 4
    sweeps = [
        Sweep("ada0", 8, None, None, 0, 0, 0, "cols", (0, 0), "AAAA", None),
        Sweep("att_in_a", 4, "token", w["att_in"], 0, 4, 1, "gate", (0, 8), ma, "qkv"),
        Sweep("att_in_b", 5, "token", w["att_in"], 4, 4, 1, "cols", (0, 12), ma, "qkv"),
        Sweep("att_out_a", 3, "token", w["att_out"], 0, 4, 1, "cols", (0, 17), ma, "op"),
        Sweep("att_out_b", 1, "token", w["att_out"], 3, 4, 1, None, None, "MMMM", "op"),
        Sweep("ff1_0", 8, "feature", w["ff1_0"], 0, 4, 2, "cols", (1, 0), "MMA" * 4, "hidden"),
        Sweep("ff2_0", 4, "token", w["ff2_0"], 0, 16, 1, "gate", (0, 20), "MMA" * 4 + "M" * 8, "op", False),
        Sweep("rec_in_a", 4, "feature", w["rec_in"], 0, 4, 1, "gate", (1, 8), ma, "xr"),
        Sweep("rec_in_b", 4, "feature", w["rec_in"], 4, 4, 1, "cols", (1, 12), ma, "gr"),
        Sweep("rec_out", 4, "token", w["rec_out"], 0, 4, 1, "cols", (1, 16), ma, "op"),
        Sweep("ff1_1", 8, "feature", w["ff1_1"], 0, 4, 2, None, None, "M" * 8, "hidden"),
        Sweep("ff2_1", 4, "token", w["ff2_1"], 0, 16, 1, "gate", (1, 20), "MMA" * 4 + "M" * 8, "op", False),
    ]
    pos = half = ada = token = feature = gate = main = 0
    for s in sweeps:
        s.pos0, s.main0, s.half0, s.ada0, s.token0, s.feature0, s.gate0 = pos, main, half, ada, token, feature, gate
        pos += s.n * len(s.order)
        main += s.n * s.order.count("M")
        half += s.n * s.halves
        ada += s.n * bool(s.ada)
        gate += s.n * (s.ada == "gate")
        if s.mode == "token":
            token += s.n * s.blocks
        if s.mode == "feature":
            feature += s.n * s.blocks
    return sweeps


def hybrid_step(nc, A, out):
    fp32 = mybir.dt.float32
    fp32r = mybir.dt.float32r
    ALU = mybir.AluOpType
    ACT = mybir.ActivationFunctionType
    AX = mybir.AxisListType.X

    def tiles_of(w):
        return w.rearrange("(t c p) n -> t p c n", c=TILE, p=P)

    W = {
        "att_in": tiles_of(A["w_att_in"][0]), "att_out": tiles_of(A["w_att_out"][0]),
        "rec_in": tiles_of(A["w_rec_in"][0]), "rec_out": tiles_of(A["w_rec_out"][0]),
        "ff1_0": tiles_of(A["w_ff1"][0]), "ff1_1": tiles_of(A["w_ff1"][1]),
        "ff2_0": tiles_of(A["w_ff2"][0]), "ff2_1": tiles_of(A["w_ff2"][1]),
    }
    W_ada = [tiles_of(A["w_ada"][layer]) for layer in range(2)]
    S = {s.name: s for s in plan(W)}
    sweeps = list(S.values())
    for s in sweeps:
        s.early = {"att_in_a": 2, "att_out_a": 4, "ff1_0": 4, "rec_in_a": 4, "rec_out": 4, "ff1_1": 4}.get(s.name, 0)

    ctx = ExitStack()
    with ctx:
        def sb(name, shape, dt=fp32):
            return ctx.enter_context(nc.sbuf_tensor(name, shape, dt))

        def sem(name):
            return ctx.enter_context(nc.semaphore(name))

        raw = sb("raw", [P, NRAW, TILE, BLK])
        w_hi = sb("w_hi", [P, NSPLIT, 2, BLK], fp32r)
        w_lo = sb("w_lo", [P, NSPLIT, 2, BLK], fp32r)
        xt = sb("xt", [P, KC, 2 * NG * T], fp32r)
        x = sb("x", [P, NG, D])
        gate = sb("gate", [P, NG, D])
        R = sb("R", [P, 16384])
        cond = sb("cond", [P, KC, 32])
        ada_rows = sb("ada_rows", [P, BLK])
        bias_rows = sb("bias_rows", [P, BLK])
        gain_rows = sb("gain_rows", [P, BLK])
        ada_cols = sb("ada_cols", [P, 2, KC, NG])
        ident = sb("ident", [P, P])
        flip = sb("flip", [P, P])
        sel = sb("sel", [P, 2])
        vec_a = sb("vec_a", [P, 96])
        vec_r = sb("vec_r", [P, 13 * KC])
        window = sb("window", [P, T])
        rope_cos = sb("rope_cos", [P, 64])
        rope_sin = sb("rope_sin", [P, 64])
        rpb = sb("rpb", [P, 4, T])
        th_a = rpb[:, :, :].rearrange("p (d h) t -> p d (h t)", d=2)
        small = sb("small", [P, 128])
        lam_exp2 = sb("lam_exp2", [P, 2 * KC])
        hidden = R[:, :].rearrange("p (c t) -> p c t", t=NG * T)
        qkv = R[:, 0:NG * QKV_W].rearrange("p (g n) -> p g n", g=NG)
        o = NG * QKV_W
        ctx_k = R[:, o:o + 1280].rearrange("p (h d) -> p h d", d=HD)
        ctx_v = R[:, o + 1280:o + 2560].rearrange("p (h d) -> p h d", d=HD)
        o += 2560
        q_t = R[:, o:o + 1024].rearrange("p (g h t) -> p g h t", g=NG, h=4)
        k_t = R[:, o + 1024:o + 2048].rearrange("p (g h t) -> p g h t", g=NG, h=4)
        ck_t = R[:, o + 2048:o + 2560].rearrange("p (h t) -> p h t", h=4)
        prob_s = R[:, o + 2560:o + 3584].rearrange("p (h t) -> p h t", h=4)
        prob_p = R[:, o + 3584:o + 4096].rearrange("p (h t) -> p h t", h=4)
        pc_t = R[:, o + 4096:o + 4608].rearrange("p (h t) -> p h t", h=4)
        rope_a = R[:, o + 2560:o + 3200].rearrange("p (h a f) -> p h a f", h=10, a=2)
        rope_b = R[:, o + 3200:o + 3840].rearrange("p (h a f) -> p h a f", h=10, a=2)
        xc = R[:, 0:4096].rearrange("p (c g t) -> p c g t", g=NG, t=T)
        gr = R[:, 4096:8192].rearrange("p (c t) -> p c t", t=NG * T)
        w_rg = R[:, 8192:9216].rearrange("p (s k j) -> p s k j", s=2, k=4)
        xr = R[:, 9216:10240].rearrange("p (c g t) -> p c g t", c=4, g=NG)
        gel = R[:, 9216:10240].rearrange("p (c n) -> p c n", c=4)
        decay = R[:, 10240:12288].rearrange("p (c d n) -> p c d n", c=4, d=2)
        drive = R[:, 12288:14336].rearrange("p (c d n) -> p c d n", c=4, d=2)
        root = R[:, 14336:16384].rearrange("p (c d n) -> p c d n", c=4, d=2)
        diag = R[:, 0:256].rearrange("p (g t) -> p g t", g=NG)
        h_mod = R[:, 256:1280].rearrange("p (s c g t) -> p s c g t", s=2, c=2, g=NG)
        junk = R[:, 4096:8192].rearrange("p (a n) -> p a n", a=4)
        stage = R[:, 2048:2048 + 3 * P].rearrange("p (a k) -> p a k", a=3)
        lam_t = R[:, 3072:3072 + 6 * 2 * KC].rearrange("p (a k) -> p a k", a=6)
        silu_t = R[:, 3584:3584 + 2 * NG * KC].rearrange("p (a k) -> p a k", a=2)
        ssq = small[:, 0:8].rearrange("p (g b) -> p g b", g=NG)
        ssq_x = small[:, 8:12].rearrange("p (g b) -> p g b", g=NG)
        mean = small[:, 12:14]
        rstd = small[:, 14:16]
        half_neg = small[:, 16:18]
        gs = small[:, 32:64].rearrange("p (c g) -> p c g", g=NG)
        mx = small[:, 64:72].rearrange("p (g h) -> p g h", g=NG)
        den = small[:, 72:80].rearrange("p (g h) -> p g h", g=NG)
        sink = small[:, 80:88]
        sink_e = small[:, 88:96].rearrange("p (g h) -> p g h", g=NG)
        states = small[:, 96:96 + 2 * KC]
        state_rows = rpb[0:2 * KC, 0, :]
        CONV_W, CONV_B, B_A, B_X, LAM, H0 = 0, 64, 80, 112, 144, 176

        ps = [ctx.enter_context(nc.psum_tensor(f"bank{i}", [P, BLK], fp32)) for i in range(8)]

        raw_landed = [sem(f"raw_landed{i}") for i in range(NRAW)]
        hi_ready = sem("hi_ready")
        lo_ready = sem("lo_ready")
        half_used = sem("half_used")
        ada_used = sem("ada_used")
        g0_done = sem("g0_done")
        chunk_done = sem("chunk_done")
        out_read_act = sem("out_read_act")
        out_read_dve = sem("out_read_dve")
        lo_copied = sem("lo_copied")
        chunk_read = sem("chunk_read")
        hidden_ready = sem("hidden_ready")
        bias_landed = sem("bias_landed")
        gain_landed = sem("gain_landed")
        ada_row = sem("ada_row")
        ada_small = sem("ada_small")
        ada_fin = sem("ada_fin")
        x_landed = sem("x_landed")
        id_landed = sem("id_landed")
        const_landed = sem("const_landed")
        vec_a_landed = sem("vec_a_landed")
        vec_r_landed = sem("vec_r_landed")
        cache_landed = sem("cache_landed")
        rpb_landed = sem("rpb_landed")
        rg_landed = [sem("rg_landed0"), sem("rg_landed1")]
        stored = sem("stored")
        cleared = sem("cleared")
        dve_step = sem("dve_step")
        vec_turned = sem("vec_turned")
        vec_ready = sem("vec_ready")
        cond_tanh = sem("cond_tanh")
        cond_ready = sem("cond_ready")
        lam_abs = sem("lam_abs")
        lam_exp = sem("lam_exp")
        rg_ready = sem("rg_ready")
        x_ready = sem("x_ready")
        ssq_ready = sem("ssq_ready")
        mean_ready = sem("mean_ready")
        rstd_ready = sem("rstd_ready")
        diag_ready = sem("diag_ready")
        turned = sem("turned")
        mod_ready = sem("mod_ready")
        mod_hi = sem("mod_hi")
        xt_ready = sem("xt_ready")
        qk_turned = sem("qk_turned")
        qk_copied_act = sem("qk_copied_act")
        qk_copied_dve = sem("qk_copied_dve")
        roped = sem("roped")
        scores_done = sem("scores_done")
        scores_scaled = sem("scores_scaled")
        bias_used = sem("bias_used")
        max_ready = sem("max_ready")
        exp_done = sem("exp_done")
        probs_ready = sem("probs_ready")
        probs_turned = sem("probs_turned")
        probs_copied_act = sem("probs_copied_act")
        probs_copied_dve = sem("probs_copied_dve")
        pv_done = sem("pv_done")
        heads_hi = sem("heads_hi")
        heads_ready = sem("heads_ready")
        conv_step = sem("conv_step")
        conv_ready = sem("conv_ready")
        gates_done = sem("gates_done")
        gates_read = sem("gates_read")
        roots_ready = sem("roots_ready")
        rg_step = sem("rg_step")
        scanned = sem("scanned")
        act_step = sem("act_step")
        gelu_square = sem("gelu_square")
        gelu_arg = sem("gelu_arg")
        gelu_tanh = sem("gelu_tanh")
        gelu_ready = sem("gelu_ready")
        y_ready = sem("y_ready")
        y_hi = sem("y_hi")
        y_split = sem("y_split")
        states_turned = sem("states_turned")
        state_rows_ready = sem("state_rows_ready")

        block = ctx.enter_context(nc.Block())

        def first(it):
            return isinstance(it, int) and it == 0

        def stream(s, it, p):
            return p % NRAW, 16 * (s.pos0 // NRAW + it * (len(s.order) // NRAW) + p // NRAW + 1)

        def released(s, it, p):
            if p >= NRAW:
                at, upto = (s, it), p - NRAW + 1
            elif first(it):
                k = sweeps.index(s)
                if k == 0:
                    return None
                b = sweeps[k - 1]
                at, upto = (b, b.n - 1), len(b.order) - NRAW + p + 1
            else:
                at, upto = (s, it - 1), len(s.order) - NRAW + p + 1
            b, i = at
            if b.order[upto - 1] == "M":
                return lo_ready, 2 * (b.main0 + i * b.order.count("M") + b.order[:upto].count("M"))
            return ada_used, TILE * b.ada0 + i * b.order.count("A") + b.order[:upto].count("A")

        def iterations(eng, s, body, before):
            body(s, 0, before)
            if s.n == 2:
                body(s, 1, (s, 0))
            elif s.n > 2:
                with eng.Fori(1, s.n) as it:
                    body(s, it, (s, it - 1))
            return s, s.n - 1

        class Steps:

            def __init__(self, eng, sem):
                self.eng, self.sem, self.n, self.ahead = eng, sem, 0, 0

            def __call__(self, ins):
                self.n += 1
                ins.then_inc(self.sem, 1)
                self.eng.wait_ge(self.sem, self.n + self.ahead)

        @block.sync
        def _(sp):
            def tiles(s, it, before):
                m = a = 0
                for p, kind in enumerate(s.order):
                    if kind == "M":
                        b, t = divmod(m, s.tiles)
                        w, col = s.weight[t], (s.col0 + it * s.blocks + b) * BLK
                        m += 1
                    else:
                        layer, col0 = s.ada_at
                        w, col = W_ada[layer][a], (col0 + it) * BLK
                        a += 1
                    if not isinstance(it, int):
                        col = sp.snap(col)
                    free = released(s, it, p)
                    if free:
                        sp.wait_ge(*free)
                    sp.dma_start(raw[:, p % NRAW, :, :], w[:, :, bass.ds(col, BLK)]).then_inc(raw_landed[p % NRAW], 16)

            sp.dma_start(stage[0:96, 0, :], A["vectors"][0:96, :]).then_inc(vec_a_landed, 16)
            sp.dma_start(ident[:, :], A["ident"]).then_inc(id_landed, 16)
            sp.dma_start(sel[:, :], A["sel"]).then_inc(id_landed, 16)
            for s in sweeps:
                iterations(sp, s, tiles, None)

        @block.gpsimd
        def _(pool):
            def ada_loads(s, it, before):
                b = s.ada0 + it
                layer, col = s.ada_at
                if not isinstance(b, int) or b > 0:
                    pool.wait_ge(ada_row, b)
                src = A["b_ada"][layer:layer + 1, bass.ds((col + it) * BLK, BLK)]
                pool.dma_start(bias_rows[0:NG, :], src.broadcast_to([NG, BLK])).then_inc(bias_landed, 16)
                if s.ada == "gate":
                    name = "g_post_ffn" if col >= 20 else "g_post_mix"
                    pool.wait_ge(ada_fin, b)
                    src = A[name][layer:layer + 1, bass.ds(it * BLK, BLK)]
                    pool.dma_start(gain_rows[:, :], src.broadcast_to([P, BLK])).then_inc(gain_landed, 16)

            def rsqrt(n):
                pool.wait_ge(mean_ready, n)
                nc.gpsimd.tensor_tensor(rstd, mean, half_neg, ALU.pow).then_inc(rstd_ready, 1)

            pool.wait_ge(cleared, 1)
            pool.dma_start(stage[0:112, 1, :], A["vectors"][96:208, :]).then_inc(vec_r_landed, 16)
            pool.dma_start(stage[0:96, 2, :], A["vectors"][208:304, :]).then_inc(vec_r_landed, 16)
            pool.dma_start(x[:, 0, :], A["x_prompt"][0]).then_inc(x_landed, 16)
            pool.dma_start(x[:, 1, :], A["x_sample"][0]).then_inc(x_landed, 16)
            pool.dma_start(flip[:, :], A["flip"]).then_inc(const_landed, 16)
            pool.dma_start(window[:, :], A["window"]).then_inc(const_landed, 16)
            pool.dma_start(rope_cos[:, :], A["rope_cos"]).then_inc(const_landed, 16)
            pool.dma_start(rope_sin[:, :], A["rope_sin"]).then_inc(const_landed, 16)
            pool.dma_start(sink, A["sink_b"].rearrange("a k g -> a (k g)").broadcast_to([P, 8])).then_inc(const_landed, 16)

            def load_rpb(quad):
                for r in range(2):
                    for rk in range(2):
                        at = 4 * quad * RPB_ROWS * RPB_COLS + (rk - r + 7) * RPB_COLS - 48
                        src = bass.AP(tensor=A["rpb_a"].tensor, offset=at,
                                      ap=[[1, GRID_W], [RPB_ROWS * RPB_COLS, 4], [1, GRID_W]])
                        pool.dma_start(rpb[GRID_W * r:GRID_W * (r + 1), :, GRID_W * rk:GRID_W * (rk + 1)], src)\
                            .then_inc(rpb_landed, 16)

            load_rpb(0)
            iterations(pool, S["ada0"], ada_loads, None)
            rsqrt(1)
            iterations(pool, S["att_in_a"], ada_loads, None)
            pool.wait_ge(xt_ready, KC // 2)
            pool.dma_start(ctx_k[:, 0:NA, :], A["cache_a_k"][0, 0]).then_inc(cache_landed, 16)
            pool.dma_start(ctx_k[:, NA:NA + NKV, :], A["cache_b_k"][0, 0]).then_inc(cache_landed, 16)
            pool.dma_start(ctx_v[:, 0:NA, :], A["cache_a_v"][0, 0]).then_inc(cache_landed, 16)
            pool.dma_start(ctx_v[:, NA:NA + NKV, :], A["cache_b_v"][0, 0]).then_inc(cache_landed, 16)
            iterations(pool, S["att_in_b"], ada_loads, None)
            pool.wait_ge(out_read_act, NG * QKV_BLOCKS)
            for a, c0, c1 in (("new_a_k", KA0, VA0), ("new_a_v", VA0, QB0), ("new_b_k", KB0, VB0),
                              ("new_b_v", VB0, QKV_W)):
                pool.dma_start(out[a][0, 0].rearrange("t h d -> t (h d)"), qkv[:, 0, c0:c1]).then_inc(stored, 16)
            pool.wait_ge(bias_used, 1)
            load_rpb(1)
            iterations(pool, S["att_out_a"], ada_loads, None)
            rsqrt(2)
            rsqrt(3)
            pool.wait_ge(stored, 16 * 4)
            iterations(pool, S["ff1_0"], ada_loads, None)
            iterations(pool, S["ff2_0"], ada_loads, None)
            rsqrt(4)
            rsqrt(5)
            iterations(pool, S["rec_in_a"], ada_loads, None)

            def rg_loads(s, it, before):
                for j in range(4):
                    if not (first(it) and j < 2):
                        pool.wait_ge(gates_done, 4 * it + j - 1)
                    for k, name in enumerate(("w_rg_a", "w_rg_x")):
                        src = A[name][0, :, bass.ds(4 * it + j, 1), :, :].rearrange("d o k j -> k d (o j)")
                        pool.dma_start(w_rg[:, j % 2, 2 * k:2 * k + 2, :], src).then_inc(rg_landed[j % 2], 16)
                ada_loads(s, it, before)

            pool.wait_ge(xt_ready, 3 * KC // 2)
            iterations(pool, S["rec_in_b"], rg_loads, None)
            pool.wait_ge(state_rows_ready, 1)
            pool.dma_start(out["new_rg_fwd"].rearrange("a b (n k) -> (a b n) k", k=P), state_rows[0:KC, :]).then_inc(stored, 16)
            pool.dma_start(out["new_rg_bwd"].rearrange("a b (n k) -> (a b n) k", k=P), state_rows[KC:2 * KC, :]).then_inc(stored, 16)
            iterations(pool, S["rec_out"], ada_loads, None)
            rsqrt(6)
            rsqrt(7)
            iterations(pool, S["ff2_1"], ada_loads, None)
            rsqrt(8)
            for k in range(4):
                pool.wait_ge(x_ready, 12 + k + 1)
                g, c = divmod(k, 2)
                pool.dma_start(out["y_prompt" if g == 0 else "y_sample"][0][:, c * 1024:(c + 1) * 1024],
                               x[:, g, c * 1024:(c + 1) * 1024]).then_inc(stored, 16)
            pool.wait_ge(stored, 16 * 10)

        @block.tensor
        def _(pe):
            def ada_tile(s, it, p, a):
                slot, landed = stream(s, it, p)
                b = s.ada0 + it
                pe.wait_ge(raw_landed[slot], landed)
                if a == 0 and not (isinstance(b, int) and b == 0):
                    pe.wait_ge(ada_row, b)
                if a == 0 and first(it) and s.name == "att_out_a":
                    pe.wait_ge(heads_ready, 4)
                for j in range(TILE):
                    mm = nc.tensor.matmul(ps[4][32 * j:32 * j + 32, :], cond[:, TILE * a + j, :],
                                          raw[:, slot, j, :], start=(a == 0), stop=(a == TILE - 1))
                mm.then_inc(ada_used, 1)

            def ada_end(s, it):
                b = s.ada0 + it
                pe.wait_ge(ada_row, b + 1)
                if not (isinstance(b, int) and b == 0):
                    pe.wait_ge(ada_fin, b)
                if s.name == "rec_in_a" and isinstance(it, int) and it == s.n - 1:
                    pe.wait_ge(gates_read, 4)
                if s.ada == "cols":
                    for m in range(BLK // P):
                        mm = nc.tensor.matmul(ps[5][:, NG * m:NG * m + NG], ada_rows[:, m * P:(m + 1) * P],
                                              sel[:, :], start=True, stop=True)
                else:
                    for g in range(NG):
                        mm = nc.tensor.matmul(ps[5 + g][:, :], sel[:, g:g + 1].broadcast_to([P, P]),
                                              ada_rows[:, :], start=True, stop=True)
                mm.then_inc(ada_small, 1)

            def token_half(s, h, g, hh, begin, end):
                for k in range(2):
                    c = (2 * hh + k) % KC
                    hi = xt[:, c, g * T:(g + 1) * T]
                    lo = xt[:, c, (NG + g) * T:(NG + g + 1) * T]
                    o = ps[g][:, :]
                    nc.tensor.matmul(o, hi, w_hi[:, h, k, :], start=(begin and k == 0), stop=False)
                    nc.tensor.matmul(o, hi, w_lo[:, h, k, :], start=False, stop=False)
                    mm = nc.tensor.matmul(o, lo, w_hi[:, h, k, :], start=False, stop=(end and k == 1))
                return mm

            def feature_half(s, h, m, hh, begin, end):
                for k in range(2):
                    c = (2 * hh + k) % KC
                    nc.tensor.matmul(ps[m][:, :], w_hi[:, h, k, m * P:(m + 1) * P], xt[:, c, :],
                                     start=(begin and k == 0), stop=False)
                    mm = nc.tensor.matmul(ps[m][:, 0:NG * T], w_lo[:, h, k, m * P:(m + 1) * P],
                                          xt[:, c, 0:NG * T], start=False, stop=(end and k == 1))
                return mm

            def rg_gates(it, j):
                n = 4 * it + j
                pe.wait_ge(rg_landed[j % 2], 32 * (2 * it + j // 2 + 1))
                pe.wait_ge(conv_ready, n + 1)
                if not (first(it) and j == 0):
                    pe.wait_ge(gates_read, n)
                if not first(it) and j == 0:
                    pe.wait_ge(ada_fin, S["rec_in_b"].ada0)
                for k in range(4):
                    at = (k % 2) * NG * T
                    mm = nc.tensor.matmul(ps[6 + k // 2][:, at:at + NG * T], w_rg[:, j % 2, k, :],
                                          xc[:, bass.ds(n, 1), :, :].rearrange("p o g t -> p (o g) t"), start=True, stop=True)
                mm.then_inc(gates_done, 1)

            def body(s, it, before):
                lanes = NG if s.mode == "token" else BLK // P
                m = a = 0
                for p, kind in enumerate(s.order):
                    if kind == "A":
                        ada_tile(s, it, p, a)
                        a += 1
                        if s.mode is None and a == 1 and before and before[0].ada:
                            ada_end(*before)
                        continue
                    b, t = divmod(m, s.tiles)
                    blk = it * s.blocks + b
                    for q in range(2):
                        hh = 2 * t + q
                        h = 2 * m + q
                        n = s.half0 + it * s.halves + h
                        if first(it) and b == 0 and s.xt_ready is not None:
                            s_, base, per = s.xt_ready
                            pe.wait_ge(s_, base + hh // per + 1)
                        if s.out == "gr" and hh < 4:
                            rg_gates(it, hh)
                        pe.wait_ge(lo_ready, n + 1)
                        if t == s.tiles - 1:
                            continue
                        for lane in range(lanes):
                            if hh == 0:
                                bank_free(s, blk, lane)
                            if s.mode == "token":
                                mm = token_half(s, h % NSPLIT, lane, hh, hh == 0, False)
                            else:
                                mm = feature_half(s, h % NSPLIT, lane, hh, hh == 0, False)
                        mm.then_inc(half_used, 1)
                    if t == s.tiles - 1:
                        for lane in range(lanes):
                            for q in range(2):
                                hh, h = 2 * t + q, 2 * m + q
                                if s.mode == "token":
                                    mm = token_half(s, h % NSPLIT, lane, hh, False, q == 1)
                                else:
                                    mm = feature_half(s, h % NSPLIT, lane, hh, False, q == 1)
                                if lane == lanes - 1:
                                    mm.then_inc(half_used, 1)
                                elif q == 1:
                                    mm.then_inc(g0_done if s.mode == "token" else chunk_done, 1)
                    m += 1
                    if m == 2 and before and before[0].ada and before[0].skew:
                        ada_end(*before)
                    if not s.skew and m == 11:
                        ada_end(s, it)

            def bank_free(s, blk, lane):
                if s.mode == "token":
                    n = NG * (s.token0 + blk) - NG + lane + 1
                    if s.out == "qkv":
                        if not (first(blk) and s.token0 == 0):
                            pe.wait_ge(out_read_act, n)
                    elif not (first(blk) and s.name == "att_out_a"):
                        pe.wait_ge(out_read_dve, n - NG * QKV_BLOCKS)
                    if first(blk) and lane == 0 and s.feature0:
                        pe.wait_ge(chunk_read, 4 * s.feature0)
                else:
                    if not (first(blk) and s.feature0 == 0):
                        pe.wait_ge(chunk_read, 4 * (s.feature0 + blk) - 4 + lane + 1)
                    if first(blk) and lane == 0:
                        pe.wait_ge(out_read_dve, NG * (s.token0 - QKV_BLOCKS))

            def turn_normed(n):
                pe.wait_ge(diag_ready, n + 1)
                for j in range(KC // 2):
                    if j >= 3:
                        pe.wait_ge(mod_ready, n * KC // 2 + j - 2)
                    for c in range(2):
                        for g in range(NG):
                            at = (c * NG + g) * T
                            mm = nc.tensor.matmul(ps[5 + j % 3][:, at:at + T], x[:, g, (2 * j + c) * P:(2 * j + c + 1) * P],
                                                  diag[:, g, :], start=True, stop=True)
                    mm.then_inc(turned, 1)

            def attention(i):
                near = i < 2
                q0 = QA0 + i * BLK if near else QB0 + (i - 2) * BLK
                k0 = KA0 + i * BLK if near else KB0 + (i - 2) * HD
                v0 = VA0 + i * BLK if near else VB0 + (i - 2) * HD
                h0 = 4 * i if near else NA + i - 2
                nk = 4 if near else 1
                if i == 0:
                    pe.wait_ge(out_read_act, NG * QKV_BLOCKS)
                    pe.wait_ge(cache_landed, 16 * 4)
                    pe.wait_ge(const_landed, 16 * 5)
                else:
                    pe.wait_ge(heads_ready, i)
                if i == 2:
                    pe.wait_ge(roped, 1)
                for g in range(NG):
                    for j in range(4):
                        nc.tensor.transpose(ps[g][:, j * T:(j + 1) * T], qkv[:, g, q0 + j * HD:q0 + (j + 1) * HD], ident[:, :])
                for j in range(nk):
                    for g in range(NG):
                        o = ps[2 + g][:, j * T:(j + 1) * T]
                        nc.tensor.transpose(o, qkv[:, g, k0 + j * HD:k0 + (j + 1) * HD], ident[:, :])
                    mm = nc.tensor.transpose(ps[4][:, j * T:(j + 1) * T], ctx_k[:, h0 + j, :], ident[:, :])
                mm.then_inc(qk_turned, 1)
                pe.wait_ge(qk_copied_act, i + 1)
                pe.wait_ge(qk_copied_dve, i + 1)
                for j in range(4):
                    kj = j if near else 0
                    for bank, g, keys in ((5, 0, k_t[:, 0, kj, :]), (6, 1, k_t[:, 1, kj, :]), (7, 1, ck_t[:, kj, :])):
                        mm = nc.tensor.matmul(ps[bank][:, j * T:(j + 1) * T], q_t[:, g, j, :], keys, start=True, stop=True)
                if near:
                    pe.wait_ge(rpb_landed, 16 * 4 * (i + 1))
                    mm = nc.tensor.matmul(ps[4][:, :], flip[:, :], rpb[:, :, :], start=True, stop=True)
                mm.then_inc(scores_done, 1)
                pe.wait_ge(probs_ready, i + 1)
                for j in range(4):
                    nc.tensor.transpose(ps[0][:, j * T:(j + 1) * T], prob_p[:, j, :], ident[:, :])
                    nc.tensor.transpose(ps[1][:, j * T:(j + 1) * T], prob_s[:, j, 0:T], ident[:, :])
                    mm = nc.tensor.transpose(ps[2][:, j * T:(j + 1) * T], prob_s[:, j, T:2 * T], ident[:, :])
                mm.then_inc(probs_turned, 1)
                pe.wait_ge(probs_copied_act, i + 1)
                pe.wait_ge(probs_copied_dve, i + 1)
                for j in range(nk):
                    n = 4 * T // nk
                    cols = slice(j * n, (j + 1) * n)
                    keys = slice(q0 + j * n, q0 + (j + 1) * n)
                    vj = slice(v0 + j * HD, v0 + (j + 1) * HD)
                    nc.tensor.matmul(ps[3][:, cols], qkv[:, 0, vj], qkv[:, 0, keys], start=True, stop=True)
                    nc.tensor.matmul(ps[4][:, cols], qkv[:, 1, vj], qkv[:, 1, keys], start=True, stop=False)
                    mm = nc.tensor.matmul(ps[4][:, cols], ctx_v[:, h0 + j, :],
                                          pc_t[:, j * (4 // nk):(j + 1) * (4 // nk), :], start=False, stop=True)
                mm.then_inc(pv_done, 1)

            for s in sweeps:
                s.xt_ready = None
            S["att_in_a"].xt_ready = (xt_ready, 0, 1)
            S["att_out_a"].xt_ready = (heads_ready, 0, 2)
            S["ff1_0"].xt_ready = (xt_ready, KC // 2, 1)
            S["rec_in_a"].xt_ready = (xt_ready, 2 * KC // 2, 1)
            S["rec_out"].xt_ready = (y_split, 0, 1)
            S["ff1_1"].xt_ready = (xt_ready, 3 * KC // 2, 1)

            pe.wait_ge(vec_a_landed, 16)
            pe.wait_ge(id_landed, 32)
            nc.tensor.transpose(ps[5][:, 0:96], stage[0:96, 0, :], ident[0:96, 0:96]).then_inc(vec_turned, 1)
            pe.wait_ge(vec_r_landed, 32)
            nc.tensor.transpose(ps[6][:, 0:112], stage[0:112, 1, :], ident[0:112, 0:112])
            nc.tensor.transpose(ps[6][:, 112:208], stage[0:96, 2, :], ident[0:96, 0:96]).then_inc(vec_turned, 1)
            pe.wait_ge(vec_ready, 2)
            pe.wait_ge(cond_ready, 1)
            last = iterations(pe, S["ada0"], body, None)
            ada_end(*last)
            turn_normed(0)
            last = iterations(pe, S["att_in_a"], body, None)
            last = iterations(pe, S["att_in_b"], body, last)
            ada_end(*last)
            for i in range(4):
                attention(i)
            last = iterations(pe, S["att_out_a"], body, None)
            last = iterations(pe, S["att_out_b"], body, last)
            turn_normed(1)
            last = iterations(pe, S["ff1_0"], body, None)
            last = iterations(pe, S["ff2_0"], body, last)
            turn_normed(2)
            last = iterations(pe, S["rec_in_a"], body, None)
            last = iterations(pe, S["rec_in_b"], body, last)
            ada_end(*last)
            pe.wait_ge(scanned, KC)
            pe.wait_ge(gates_read, KC)
            nc.tensor.matmul(ps[7][0:2 * KC, 0:P], states, ident[:, :], start=True, stop=True).then_inc(states_turned, 1)
            last = iterations(pe, S["rec_out"], body, None)
            ada_end(*last)
            turn_normed(3)
            last = iterations(pe, S["ff1_1"], body, None)
            last = iterations(pe, S["ff2_1"], body, last)

        @block.scalar
        def _(act):
            def split(s, it, h):
                n = s.half0 + it * s.halves + h
                t, q = divmod(h, 2)
                p = [i for i, k in enumerate(s.order) if k == "M"][t]
                slot, landed = stream(s, it, p)
                if s.tiles == 16:
                    if first(it):
                        act.wait_ge(hidden_ready, hidden0[s.name] + 2 * h + 2)
                if q == 0:
                    act.wait_ge(raw_landed[slot], landed)
                if not isinstance(n, int) or n >= NSPLIT:
                    act.wait_ge(half_used, n - NSPLIT + 1)
                if s.tiles == 16:
                    c = 2 * h % KC
                    nc.scalar.activation(xt[:, c:c + 2, 0:NG * T], hidden[:, 2 * h:2 * h + 2, :], ACT.Copy)
                nc.scalar.activation(w_hi[:, h % NSPLIT, :, :], raw[:, slot, 2 * q:2 * q + 2, :], ACT.Copy)\
                    .then_inc(hi_ready, 1)

            def split_early(name, h0, h1):
                for h in range(h0, h1):
                    split(S[name], 0, h)

            def out_ready(s, blk, g):
                if g == 0:
                    act.wait_ge(g0_done, s.token0 + blk + 1)
                else:
                    act.wait_ge(half_used, s.half0 + (blk + 1) * 2 * s.tiles)

            def token_out(s, blk, g):
                out_ready(s, blk, g)
                if s.out == "qkv":
                    nc.scalar.activation(qkv[:, g, bass.ds((s.col0 + blk) * BLK, BLK)], ps[g][:, :], ACT.Copy)\
                        .then_inc(out_read_act, 1)
                else:
                    act.wait_ge(out_read_act, NG * (s.token0 + blk) + g)
                    nc.scalar.activation(ps[7][:, :], ps[g][:, :], ACT.Square,
                                         accum_out=ssq[:, g, bass.ds(s.col0 + blk, 1)]).then_inc(out_read_act, 1)

            def feature_out(s, blk, m):
                if m < 3:
                    act.wait_ge(chunk_done, 3 * (s.feature0 + blk) + m + 1)
                else:
                    act.wait_ge(half_used, s.half0 + (blk + 1) * 2 * s.tiles)
                dst = hidden[:, bass.ds(4 * (s.col0 + blk) + m, 1), :]
                if s.out == "xr":
                    dst = gel[:, m:m + 1, :]
                    if m == 0 and not first(blk):
                        act.wait_ge(conv_ready, 4 * blk)
                nc.scalar.activation(dst, ps[m][:, NG * T:2 * NG * T].rearrange("p (o t) -> p o t", o=1), ACT.Copy)\
                    .then_inc(lo_copied, 1)

            def rg_tanhs(it, j):
                n = 4 * it + j
                steps.n, steps.ahead = 0, n * 2
                act.wait_ge(gates_done, n + 1)
                if not first(it):
                    act.wait_ge(scanned, n - 3)
                for d in range(2):
                    cols = [vec_r[:, bass.ds(base + d * KC + n, 1)] for base in (B_A, LAM, B_X)]
                    fast = lam_exp2[:, bass.ds(d * KC + n, 1)]
                    steps(nc.scalar.activation(th_a[:, d, :], ps[6][:, d * NG * T:(d + 1) * NG * T],
                                               ACT.Tanh, scale=0.5, bias=cols[0]))
                    nc.scalar.activation(root[:, j, d, :], th_a[:, d, :], ACT.Tanh, scale=cols[1], bias=cols[1])
                    nc.scalar.activation(decay[:, j, d, :], th_a[:, d, :], ACT.Exp, scale=fast, bias=fast)
                    e = nc.scalar.activation(drive[:, j, d, :], ps[7][:, d * NG * T:(d + 1) * NG * T],
                                             ACT.Tanh, scale=0.5, bias=cols[2])
                e.then_inc(gates_read, 1)

            def rg_roots(it):
                act.wait_ge(gates_read, 4 * it + 4)
                flat = root.rearrange("p c d n -> p (c d n)")
                nc.scalar.activation(flat, flat, ACT.Sqrt).then_inc(roots_ready, 1)

            def gelu_squares(blk):
                act.wait_ge(chunk_read, 4 * (S["rec_in_b"].feature0 + blk) + 4)
                if first(blk):
                    act.wait_ge(conv_ready, KC)
                else:
                    act.wait_ge(y_ready, blk)
                nc.scalar.activation(gel, gr[:, bass.ds(4 * blk, 4), :], ACT.Square,
                                     scale=(0.044715 * GELU_C) ** 0.5).then_inc(gelu_square, 1)

            def gelu_tanhs(blk):
                act.wait_ge(gelu_arg, blk + 1)
                nc.scalar.activation(gel, gel, ACT.Tanh).then_inc(gelu_tanh, 1)

            def body(s, it, before):
                for b in range(s.blocks):
                    last = (s, it * s.blocks + b - 1) if b else (before and (before[0], before[1] * before[0].blocks + before[0].blocks - 1))
                    for hh in range(2 * s.tiles):
                        h = b * 2 * s.tiles + hh
                        if not (first(it) and h < s.early):
                            split(s, it, h)
                        if last and last[0].mode == "token" and hh == 1:
                            for g in range(NG):
                                token_out(*last, g)
                        if last and last[0].mode == "feature" and hh == 1:
                            for m in range(4):
                                feature_out(*last, m)
                        if s.out == "gr":
                            if last[0] is s and hh == 3:
                                gelu_squares(last[1])
                            if last[0] is s and hh == 5:
                                gelu_tanhs(last[1])
                            if 1 <= hh <= 4:
                                rg_tanhs(it, hh - 1)
                            if hh == 5:
                                rg_roots(it)

            def flush(last):
                s, it = last
                blk = it * s.blocks + s.blocks - 1
                if s.mode == "token":
                    for g in range(NG):
                        token_out(s, blk, g)
                else:
                    for m in range(4):
                        feature_out(s, blk, m)

            def squares_of_x(n):
                for k in range(4):
                    g, c = divmod(k, 2)
                    if n == 0:
                        act.wait_ge(x_landed, 32)
                    else:
                        act.wait_ge(x_ready, 4 * (n - 1) + k + 1)
                    nc.scalar.activation(junk[:, k, :], x[:, g, c * 1024:(c + 1) * 1024], ACT.Square,
                                         accum_out=ssq_x[:, g, c:c + 1]).then_inc(ssq_ready, 1)

            def norm(n):
                for j in range(KC // 2):
                    act.wait_ge(mod_ready, n * KC // 2 + j + 1)
                    nc.scalar.activation(xt[:, 2 * j:2 * j + 2, 0:NG * T],
                                         h_mod[:, j % 2].rearrange("p c g t -> p c (g t)"), ACT.Copy).then_inc(mod_hi, 1)

            def attention(i):
                near = i < 2
                q0 = QA0 + i * BLK if near else QB0 + (i - 2) * BLK
                act.wait_ge(qk_turned, i + 1)
                nc.scalar.activation(q_t[:, 0].rearrange("p h t -> p (h t)"), ps[0][:, :], ACT.Copy)
                n = BLK if near else T
                nc.scalar.activation(k_t[:, 0].rearrange("p h t -> p (h t)")[:, 0:n], ps[2][:, 0:n], ACT.Copy)\
                    .then_inc(qk_copied_act, 1)
                act.wait_ge(scores_done, i + 1)
                nc.scalar.activation(prob_s[:, :, T:2 * T], ps[7][:, :].rearrange("p (h t) -> p h t", h=4), ACT.Copy, scale=SCALE)
                if not near:
                    nc.scalar.activation(prob_s[:, :, 0:T], ps[6][:, :].rearrange("p (h t) -> p h t", h=4), ACT.Copy, scale=SCALE)
                nc.scalar.activation(prob_p.rearrange("p h t -> p (h t)"), ps[5][:, :], ACT.Copy, scale=SCALE).then_inc(scores_scaled, 1)
                act.wait_ge(max_ready, i + 1)
                if not near:
                    nc.scalar.activation(sink_e, sink_e, ACT.Exp)
                for g, pr in ((0, prob_p), (1, prob_s)):
                    for j in range(4):
                        e = nc.scalar.activation(pr[:, j, :], pr[:, j, :], ACT.Exp, bias=mx[:, g, j:j + 1],
                                                 accum_out=den[:, g, j:j + 1])
                e.then_inc(exp_done, 1)
                act.wait_ge(probs_turned, i + 1)
                nc.scalar.activation(qkv[:, 0, q0:q0 + BLK], ps[0][:, :], ACT.Copy).then_inc(probs_copied_act, 1)
                act.wait_ge(pv_done, i + 1)
                for g in range(NG):
                    e = nc.scalar.activation(xt[:, 4 * i:4 * i + 4, g * T:(g + 1) * T],
                                             ps[3 + g][:, :].rearrange("p (h t) -> p h t", h=4), ACT.Copy)
                e.then_inc(heads_hi, 1)

            steps = Steps(act, act_step)

            hidden0 = {"ff2_0": 0, "ff2_1": 4 * FF // BLK}

            act.wait_ge(vec_ready, 1)
            nc.scalar.activation(silu_t[:, 0, :], vec_a[:, 0:2 * KC], ACT.Tanh, scale=0.5).then_inc(cond_tanh, 1)
            act.wait_ge(lam_abs, 1)
            nc.scalar.activation(lam_t[:, 1, :], lam_t[:, 0, :], ACT.Exp, scale=-1.0).then_inc(lam_exp, 1)
            squares_of_x(0)
            split_early("att_in_a", 0, 2)
            norm(0)
            last = iterations(act, S["att_in_a"], body, None)
            last = iterations(act, S["att_in_b"], body, last)
            split_early("att_out_a", 0, 2)
            flush(last)
            split_early("att_out_a", 2, 4)
            for i in range(4):
                attention(i)
            last = iterations(act, S["att_out_a"], body, None)
            last = iterations(act, S["att_out_b"], body, last)
            split_early("ff1_0", 0, 2)
            flush(last)
            split_early("ff1_0", 2, 4)
            squares_of_x(1)
            norm(1)
            last = iterations(act, S["ff1_0"], body, None)
            last = iterations(act, S["ff2_0"], body, last)
            split_early("rec_in_a", 0, 2)
            flush(last)
            split_early("rec_in_a", 2, 4)
            squares_of_x(2)
            norm(2)
            last = iterations(act, S["rec_in_a"], body, None)
            last = iterations(act, S["rec_in_b"], body, last)
            split_early("rec_out", 0, 2)
            flush(last)
            split_early("rec_out", 2, 4)
            gelu_squares(3)
            for pair in range(KC // 2):
                if pair == 6:
                    gelu_tanhs(3)
                act.wait_ge(y_ready, pair // 2 + 1)
                nc.scalar.activation(xt[:, 2 * pair:2 * pair + 2, 0:NG * T],
                                     xc[:, 2 * pair:2 * pair + 2].rearrange("p c g t -> p c (g t)"), ACT.Copy)\
                    .then_inc(y_hi, 1)
            last = iterations(act, S["rec_out"], body, None)
            split_early("ff1_1", 0, 2)
            flush(last)
            split_early("ff1_1", 2, 4)
            squares_of_x(3)
            norm(3)
            last = iterations(act, S["ff1_1"], body, None)
            last = iterations(act, S["ff2_1"], body, last)
            flush(last)

        @block.vector
        def _(dve):
            steps = Steps(dve, dve_step)
            V = nc.vector

            def split(s, it, h):
                n = s.half0 + it * s.halves + h
                t, q = divmod(h, 2)
                slot = [i for i, k in enumerate(s.order) if k == "M"][t] % NRAW
                dve.wait_ge(hi_ready, n + 1)
                if s.tiles == 16:
                    c = 2 * h % KC
                    V.tensor_tensor(xt[:, c:c + 2, NG * T:2 * NG * T], hidden[:, 2 * h:2 * h + 2, :],
                                    xt[:, c:c + 2, 0:NG * T].bitcast(fp32), ALU.subtract)
                V.tensor_tensor(w_lo[:, h % NSPLIT, :, :], raw[:, slot, 2 * q:2 * q + 2, :],
                                w_hi[:, h % NSPLIT, :, :].bitcast(fp32), ALU.subtract).then_inc(lo_ready, 1)

            def split_early(name, h0, h1):
                for h in range(h0, h1):
                    split(S[name], 0, h)

            def token_out(s, blk, g):
                if s.out == "op":
                    dve.wait_ge(out_read_act, NG * (s.token0 + blk) + g + 1)
                    dst = gate[:, g, bass.ds((s.col0 + blk) * BLK, BLK)]
                    V.tensor_tensor(dst, ps[g][:, :], dst, ALU.mult).then_inc(out_read_dve, 1)

            def feature_out(s, blk, m):
                n = 4 * (s.feature0 + blk) + m
                dve.wait_ge(lo_copied, n + 1)
                dst = hidden[:, bass.ds(4 * (s.col0 + blk) + m, 1), :].rearrange("p o t -> p (o t)")
                if s.out == "xr":
                    dst = gel[:, m, :]
                V.tensor_tensor(dst, ps[m][:, 0:NG * T], dst, ALU.add).then_inc(chunk_read, 1)
                if s.out == "hidden":
                    dve.wait_ge(chunk_read, n + 1)
                    V.scalar_tensor_tensor(out=dst, in0=dst, scalar=0.0, in1=dst, op0=ALU.max, op1=ALU.mult)\
                        .then_inc(hidden_ready, 1)

            def ada_rows_out(s, it):
                b = s.ada0 + it
                dve.wait_ge(ada_used, TILE * (b + 1))
                dve.wait_ge(bias_landed, 16 * (b + 1))
                if not (isinstance(b, int) and b == 0):
                    dve.wait_ge(ada_small, b)
                V.tensor_tensor(ada_rows[:, :], ps[4][:, :], bias_rows[:, :], ALU.add).then_inc(ada_row, 1)

            def ada_store(s, it):
                b = s.ada0 + it
                dve.wait_ge(ada_small, b + 1)
                if s.ada == "cols":
                    base = s.ada_at[1] - (12 if s.ada_at[1] >= 12 else 0)
                    flat = ada_cols[:, :, :, :].rearrange("p a c g -> p (a c g)")
                    V.tensor_copy(flat[:, bass.ds((base + it) * 4 * NG, 4 * NG)], ps[5][:, 0:4 * NG]).then_inc(ada_fin, 1)
                else:
                    dve.wait_ge(gain_landed, 16 * (s.gate0 + it + 1))
                    for g in range(NG):
                        e = V.tensor_tensor(gate[:, g, bass.ds(it * BLK, BLK)], ps[5 + g][:, :], gain_rows[:, :], ALU.mult)
                    e.then_inc(ada_fin, 1)

            def body(s, it, before):
                if s.mode is None:
                    if before:
                        ada_store(*before)
                    ada_rows_out(s, it)
                    return
                for b in range(s.blocks):
                    last = (s, it * s.blocks + b - 1) if b else (before and (before[0], before[1] * before[0].blocks + before[0].blocks - 1))
                    for hh in range(2 * s.tiles):
                        h = b * 2 * s.tiles + hh
                        if not (first(it) and h < s.early):
                            split(s, it, h)
                        if last and last[0].mode == "token" and hh == 1:
                            if last[0].out == "op":
                                dve.wait_ge(ada_fin, gate_of(*last))
                            for g in range(NG):
                                token_out(*last, g)
                        if last and last[0].mode == "feature" and hh == 1:
                            for m in range(4):
                                feature_out(*last, m)
                        if last and last[0].out == "xr" and hh == 3:
                            convolve(last[1])
                        if s.out == "gr":
                            if 2 <= hh <= 5:
                                rg_drive(it, hh - 2)
                            if last[0] is s and hh == 3:
                                gelu_arguments(last[1])
                            if last[0] is s and hh == 6:
                                outputs(last[1])
                            if hh >= 6:
                                rg_scan(it, 2 * (hh - 6))
                                rg_scan(it, 2 * (hh - 6) + 1)
                        if before and before[0].ada and before[0].skew and b == 0:
                            if hh == 2:
                                ada_rows_out(*before)
                            if hh == 7:
                                ada_store(*before)
                        if not s.skew and hh == 19:
                            ada_rows_out(s, it)
                        if not s.skew and hh == 25:
                            ada_store(s, it)

            def gate_of(s, blk):
                return {"att_out_a": 12, "att_out_b": 12, "ff2_0": S["ff2_0"].ada0 + blk + 1,
                        "rec_out": S["rec_in_a"].ada0 + 4, "ff2_1": S["ff2_1"].ada0 + blk + 1}[s.name]

            def flush(last):
                s, it = last
                blk = it * s.blocks + s.blocks - 1
                if s.mode == "token":
                    if s.out == "op":
                        dve.wait_ge(ada_fin, gate_of(s, blk))
                    for g in range(NG):
                        token_out(s, blk, g)
                else:
                    for m in range(4):
                        feature_out(s, blk, m)

            def mean_of(sums, b):
                steps(V.tensor_reduce(mean, sums, AX, ALU.add))
                V.tensor_scalar(mean, mean, 1.0 / D, EPS, ALU.mult, ALU.add).then_inc(mean_ready, 1)

            def residual(n, ahead=None):
                dve.wait_ge(out_read_dve, NG * (blocks_done[n] - QKV_BLOCKS))
                mean_of(ssq, 4)
                if ahead:
                    split_early(ahead, 2, 3)
                dve.wait_ge(rstd_ready, 2 * n)
                for k in range(4):
                    g, c = divmod(k, 2)
                    cols = slice(c * 1024, (c + 1) * 1024)
                    V.scalar_tensor_tensor(out=x[:, g, cols], in0=gate[:, g, cols], scalar=rstd[:, g:g + 1],
                                           in1=x[:, g, cols], op0=ALU.mult, op1=ALU.add).then_inc(x_ready, 1)
                if ahead:
                    split_early(ahead, 3, 4)

            def norm(n, gain):
                dve.wait_ge(ssq_ready, 4 * (n + 1))
                mean_of(ssq_x, 2)
                dve.wait_ge(ada_fin, norm_ada[n])
                steps(V.scalar_tensor_tensor(out=gs, in0=ada_cols[:, 1], scalar=1.0,
                                             in1=vec_a[:, gain:gain + KC].unsqueeze(2).broadcast_to([P, KC, NG]),
                                             op0=ALU.add, op1=ALU.mult))
                dve.wait_ge(rstd_ready, 2 * n + 1)
                for g in range(NG):
                    e = V.tensor_scalar(diag[:, g, :], ident[:, :], rstd[:, g:g + 1], None, ALU.mult)
                e.then_inc(diag_ready, 1)

                def rest(j):
                    dve.wait_ge(mod_hi, n * KC // 2 + j + 1)
                    V.tensor_tensor(xt[:, 2 * j:2 * j + 2, NG * T:2 * NG * T],
                                    h_mod[:, j % 2].rearrange("p c g t -> p c (g t)"),
                                    xt[:, 2 * j:2 * j + 2, 0:NG * T].bitcast(fp32), ALU.subtract).then_inc(xt_ready, 1)

                for j in range(KC // 2):
                    dve.wait_ge(turned, n * KC // 2 + j + 1)
                    if j >= 2:
                        dve.wait_ge(xt_ready, n * KC // 2 + j - 1)
                    for c in range(2):
                        for g in range(NG):
                            at = (c * NG + g) * T
                            e = V.tensor_scalar(h_mod[:, j % 2, c, g, :], ps[5 + j % 3][:, at:at + T],
                                                gs[:, 2 * j + c, g:g + 1], ada_cols[:, 0, 2 * j + c, g:g + 1],
                                                ALU.mult, ALU.add)
                    e.then_inc(mod_ready, 1)
                    if j:
                        rest(j - 1)
                rest(KC // 2 - 1)

            def rope():
                dve.wait_ge(const_landed, 16 * 5)
                dve.wait_ge(out_read_act, NG * QKV_BLOCKS)
                qk = qkv[:, 1, QB0:VB0].rearrange("p (h a f) -> p h a f", h=10, a=2)
                x1, x2 = qk[:, :, :, 0:32], qk[:, :, :, 32:64]
                cos = rope_cos[:, :].rearrange("p (a f) -> p a f", a=2).unsqueeze(1).broadcast_to([P, 10, 2, 32])
                sin = rope_sin[:, :].rearrange("p (a f) -> p a f", a=2).unsqueeze(1).broadcast_to([P, 10, 2, 32])
                V.tensor_tensor(rope_a, x2, sin, ALU.mult)
                steps(V.tensor_tensor(rope_b, x1, sin, ALU.mult))
                V.tensor_tensor(x1, x1, cos, ALU.mult)
                steps(V.tensor_tensor(x2, x2, cos, ALU.mult))
                V.tensor_tensor(x1, x1, rope_a, ALU.subtract)
                V.tensor_tensor(x2, x2, rope_b, ALU.add).then_inc(roped, 1)

            def attention(i):
                near = i < 2
                q0 = QA0 + i * BLK if near else QB0 + (i - 2) * BLK
                n = BLK if near else T
                dve.wait_ge(qk_turned, i + 1)
                V.tensor_copy(q_t[:, 1].rearrange("p h t -> p (h t)"), ps[1][:, :])
                V.tensor_copy(k_t[:, 1].rearrange("p h t -> p (h t)")[:, 0:n], ps[3][:, 0:n])
                V.tensor_copy(ck_t.rearrange("p h t -> p (h t)")[:, 0:n], ps[4][:, 0:n]).then_inc(qk_copied_dve, 1)
                dve.wait_ge(scores_done, i + 1)
                if near:
                    steps(V.tensor_tensor(rpb[:, :, :], ps[4][:, :].rearrange("p (h t) -> p h t", h=4),
                                          window[:, :].unsqueeze(1).broadcast_to([P, 4, T]), ALU.add))
                    V.scalar_tensor_tensor(out=prob_s[:, :, 0:T], in0=ps[6][:, :].rearrange("p (h t) -> p h t", h=4),
                                           scalar=SCALE, in1=rpb[:, :, :], op0=ALU.mult, op1=ALU.add).then_inc(bias_used, 1)
                    dve.wait_ge(bias_used, i + 1)
                dve.wait_ge(scores_scaled, i + 1)
                V.tensor_reduce(mx[:, 0, :], prob_p, AX, ALU.max)
                steps(V.tensor_reduce(mx[:, 1, :], prob_s, AX, ALU.max))
                if not near:
                    sinks = sink[:, 4 * (i - 2):4 * (i - 1)].unsqueeze(1).broadcast_to([P, NG, 4])
                    steps(V.tensor_tensor(mx, mx, sinks, ALU.max))
                    steps(V.tensor_tensor(sink_e, sinks, mx, ALU.subtract))
                m = V.tensor_scalar(mx, mx, -1.0, None, ALU.mult)
                m.then_inc(max_ready, 1)
                dve.wait_ge(exp_done, i + 1)
                if not near:
                    steps(V.tensor_tensor(den, den, sink_e, ALU.add))
                steps(V.reciprocal(den, den))
                V.tensor_tensor(prob_p, prob_p, den[:, 0, :].unsqueeze(2).broadcast_to([P, 4, T]), ALU.mult)
                V.tensor_tensor(prob_s, prob_s, den[:, 1, :].unsqueeze(2).broadcast_to([P, 4, 2 * T]), ALU.mult)\
                    .then_inc(probs_ready, 1)
                dve.wait_ge(probs_turned, i + 1)
                V.tensor_copy(qkv[:, 1, q0:q0 + BLK], ps[1][:, :])
                V.tensor_copy(pc_t.rearrange("p h t -> p (h t)"), ps[2][:, :]).then_inc(probs_copied_dve, 1)
                dve.wait_ge(heads_hi, i + 1)
                for g in range(NG):
                    e = V.tensor_tensor(xt[:, 4 * i:4 * i + 4, (NG + g) * T:(NG + g + 1) * T],
                                        ps[3 + g][:, :].rearrange("p (h t) -> p h t", h=4),
                                        xt[:, 4 * i:4 * i + 4, g * T:(g + 1) * T].bitcast(fp32), ALU.subtract)
                e.then_inc(heads_ready, 1)

            def decay_rates():
                lam = vec_r[:, LAM:LAM + 2 * KC]
                L = [lam_t[:, a, :] for a in range(6)]
                V.tensor_scalar(vec_r[:, B_A:B_A + 4 * KC], vec_r[:, B_A:B_A + 4 * KC], 0.5, None, ALU.mult)
                V.scalar_tensor_tensor(out=L[0], in0=lam, scalar=-1.0, in1=lam, op0=ALU.mult, op1=ALU.max)\
                    .then_inc(lam_abs, 1)
                dve.wait_ge(lam_exp, 1)
                steps(V.tensor_scalar(L[2], L[1], 2.0, None, ALU.add))
                steps(V.reciprocal(L[2], L[2]))
                steps(V.tensor_tensor(L[2], L[1], L[2], ALU.mult))
                steps(V.tensor_tensor(L[3], L[2], L[2], ALU.mult))
                steps(V.tensor_scalar(L[4], L[3], 1.0 / 17, None, ALU.mult))
                for k in range(15, 1, -2):
                    steps(V.scalar_tensor_tensor(out=L[4], in0=L[4], scalar=1.0 / k, in1=L[3], op0=ALU.add, op1=ALU.mult))
                steps(V.scalar_tensor_tensor(out=L[4], in0=L[4], scalar=1.0, in1=L[2], op0=ALU.add, op1=ALU.mult))
                steps(V.tensor_scalar(L[5], lam, -1.0, 0.0, ALU.mult, ALU.max))
                steps(V.scalar_tensor_tensor(out=L[5], in0=L[4], scalar=2.0, in1=L[5], op0=ALU.mult, op1=ALU.add))
                V.tensor_scalar(lam_exp2[:, :], L[5], -4.0, None, ALU.mult)
                V.tensor_scalar(vec_r[:, H0:H0 + 2 * KC], vec_r[:, H0:H0 + 2 * KC], 2.0, None, ALU.mult)
                V.tensor_scalar(lam, L[5], 2.0, None, ALU.mult).then_inc(rg_ready, 1)

            def convolve(blk):
                def param(base, m):
                    return vec_r[:, bass.ds(base + 4 * blk + m, 1)]

                def wait_taps(k):
                    dve.wait_ge(conv_step, 3 * blk + k)

                dve.wait_ge(chunk_read, 4 * (S["rec_in_a"].feature0 + blk) + 4)
                xs = [xr[:, m] for m in range(4)]
                ys = [xc[:, bass.ds(4 * blk + m, 1)].rearrange("p o g t -> p (o g) t") for m in range(4)]
                for m in range(4):
                    e = V.tensor_scalar(ys[m], xs[m], param(CONV_W + 2 * KC, m), param(CONV_B, m), ALU.mult, ALU.add)
                e.then_inc(conv_step, 1)
                for k, (tap, back) in enumerate(((0, 2), (1, 1))):
                    wait_taps(k + 1)
                    for m in range(4):
                        e = V.scalar_tensor_tensor(out=ys[m][:, :, back:], in0=xs[m][:, :, 0:T - back],
                                                   scalar=param(CONV_W + tap * KC, m), in1=ys[m][:, :, back:],
                                                   op0=ALU.mult, op1=ALU.add)
                    e.then_inc(conv_step, 1)
                wait_taps(3)
                for m in range(4):
                    V.scalar_tensor_tensor(out=ys[m][:, :, 0:T - 1], in0=xs[m][:, :, 1:T],
                                           scalar=param(CONV_W + 3 * KC, m), in1=ys[m][:, :, 0:T - 1],
                                           op0=ALU.mult, op1=ALU.add).then_inc(conv_ready, 1)

            rg = Steps(dve, rg_step)
            RG_STEPS = 4

            def rg_drive(it, j):
                n = 4 * it + j
                rg.n, rg.ahead = 2 * j, it * 4 * RG_STEPS
                dve.wait_ge(gates_read, n + 1)
                x_c = xc[:, bass.ds(n, 1)].rearrange("p o g t -> p o (g t)").broadcast_to([P, 2, NG * T])
                v = drive[:, j]
                rg(V.scalar_tensor_tensor(out=v, in0=v, scalar=1.0, in1=x_c, op0=ALU.add, op1=ALU.mult))
                rg(V.scalar_tensor_tensor(out=v, in0=decay[:, j], scalar=1.0, in1=v, op0=ALU.add, op1=ALU.mult))

            def rg_scan(it, j):
                n = 4 * it + j
                rg.n, rg.ahead = 8 + 2 * j, it * 4 * RG_STEPS
                dve.wait_ge(roots_ready, it + 1)
                rg(V.tensor_tensor(drive[:, j], drive[:, j], root[:, j], ALU.mult))
                for d in range(2):
                    for g in range(NG):
                        way = slice(None, None, -1) if d else slice(None)
                        a, b, h = (z[:, j, d, g * T:(g + 1) * T][:, way] for z in (decay, drive, root))
                        h0 = 0.0 if g == 0 else vec_r[:, bass.ds(H0 + d * KC + n, 1)]
                        e = V.tensor_tensor_scan(h, a, b, h0, ALU.mult, ALU.add)
                rg(e)
                for d in range(2):
                    end = 0 if d else T - 1
                    V.tensor_scalar(states[:, bass.ds(d * KC + n, 1)], root[:, j, d, end:end + 1], 0.5, None, ALU.mult)
                V.tensor_tensor(xc[:, bass.ds(n, 1)].rearrange("p o g t -> p (o g t)"), root[:, j, 0, :],
                                root[:, j, 1, :], ALU.add).then_inc(scanned, 1)

            def gelu_arguments(blk):
                dve.wait_ge(gelu_square, blk + 1)
                V.scalar_tensor_tensor(out=gel, in0=gel, scalar=GELU_C, in1=gr[:, bass.ds(4 * blk, 4), :],
                                       op0=ALU.add, op1=ALU.mult).then_inc(gelu_arg, 1)

            def outputs(blk):
                dve.wait_ge(gelu_tanh, blk + 1)
                V.scalar_tensor_tensor(out=gel, in0=gel, scalar=1.0, in1=gr[:, bass.ds(4 * blk, 4), :],
                                       op0=ALU.add, op1=ALU.mult).then_inc(gelu_ready, 1)
                dve.wait_ge(gelu_ready, blk + 1)
                dve.wait_ge(scanned, 4 * blk + 4)
                y = xc[:, bass.ds(4 * blk, 4)].rearrange("p c g t -> p c (g t)")
                V.scalar_tensor_tensor(out=y, in0=gel, scalar=0.25, in1=y, op0=ALU.mult, op1=ALU.mult)\
                    .then_inc(y_ready, 1)

            blocks_done = {1: 13, 2: 17, 3: 21, 4: 25}
            norm_ada = {0: 8, 1: 20, 2: 28, 3: 44}

            V.memset(bias_rows[:, :], 0.0)
            V.memset(half_neg, -0.5)
            steps(V.memset(cond[:, :, :], 0.0))
            V.memset(ssq_x, 0.0).then_inc(cleared, 1)
            dve.wait_ge(vec_turned, 1)
            V.tensor_copy(vec_a[:, :], ps[5][:, 0:96]).then_inc(vec_ready, 1)
            dve.wait_ge(cond_tanh, 1)
            steps(V.scalar_tensor_tensor(out=silu_t[:, 1, :], in0=silu_t[:, 0, :], scalar=1.0, in1=vec_a[:, 0:2 * KC],
                                         op0=ALU.add, op1=ALU.mult))
            V.tensor_scalar(cond[:, :, 0:NG].rearrange("p c g -> p g c"),
                            silu_t[:, 1, :].rearrange("p (g c) -> p g c", g=NG), 0.5, None, ALU.mult).then_inc(cond_ready, 1)
            dve.wait_ge(vec_turned, 2)
            V.tensor_copy(vec_r[:, :], ps[6][:, 0:208]).then_inc(vec_ready, 1)
            dve.wait_ge(vec_ready, 2)
            decay_rates()
            last = iterations(dve, S["ada0"], body, None)
            ada_store(*last)
            split_early("att_in_a", 0, 2)
            norm(0, 2 * KC)
            last = iterations(dve, S["att_in_a"], body, None)
            last = iterations(dve, S["att_in_b"], body, last)
            split_early("att_out_a", 0, 2)
            flush(last)
            ada_rows_out(*last)
            split_early("att_out_a", 2, 3)
            ada_store(*last)
            rope()
            split_early("att_out_a", 3, 4)
            for i in range(4):
                attention(i)
            last = iterations(dve, S["att_out_a"], body, None)
            last = iterations(dve, S["att_out_b"], body, last)
            split_early("ff1_0", 0, 2)
            flush(last)
            residual(1, "ff1_0")
            norm(1, 4 * KC)
            last = iterations(dve, S["ff1_0"], body, None)
            last = iterations(dve, S["ff2_0"], body, last)
            split_early("rec_in_a", 0, 2)
            flush(last)
            residual(2, "rec_in_a")
            norm(2, 3 * KC)
            last = iterations(dve, S["rec_in_a"], body, None)
            last = iterations(dve, S["rec_in_b"], body, last)
            split_early("rec_out", 0, 2)
            flush(last)
            split_early("rec_out", 2, 4)
            gelu_arguments(3)
            for pair in range(KC // 2):
                if pair == 6:
                    outputs(3)
                dve.wait_ge(y_hi, pair + 1)
                V.tensor_tensor(xt[:, 2 * pair:2 * pair + 2, NG * T:2 * NG * T],
                                xc[:, 2 * pair:2 * pair + 2].rearrange("p c g t -> p c (g t)"),
                                xt[:, 2 * pair:2 * pair + 2, 0:NG * T].bitcast(fp32), ALU.subtract).then_inc(y_split, 1)
            ada_rows_out(*last)
            ada_store(*last)
            dve.wait_ge(states_turned, 1)
            V.tensor_copy(state_rows, ps[7][0:2 * KC, 0:P]).then_inc(state_rows_ready, 1)
            last = iterations(dve, S["rec_out"], body, None)
            split_early("ff1_1", 0, 2)
            flush(last)
            ada_rows_out(*last)
            ada_store(*last)
            residual(3, "ff1_1")
            norm(3, 5 * KC)
            last = iterations(dve, S["ff1_1"], body, None)
            last = iterations(dve, S["ff2_1"], body, last)
            flush(last)
            residual(4)


_OUTS = [("y_prompt", (1, T, D)), ("y_sample", (1, T, D)),
         ("new_a_k", (1, 1, T, NA, HD)), ("new_a_v", (1, 1, T, NA, HD)),
         ("new_b_k", (1, 1, T, NKV, HD)), ("new_b_v", (1, 1, T, NKV, HD)),
         ("new_rg_fwd", (1, 1, D)), ("new_rg_bwd", (1, 1, D))]
_WHOLE = ["x_prompt", "x_sample", "cache_a_k", "cache_a_v", "cache_b_k", "cache_b_v", "w_ada", "b_ada",
          "g_post_mix", "g_post_ffn", "w_att_in", "w_att_out", "sink_b", "rpb_a", "w_rec_in", "w_rg_a",
          "w_rg_x", "w_rec_out", "w_ff1", "w_ff2"]


def tables(np):
    t = np.arange(T)
    flip = np.zeros((P, P), np.float32)
    flip[(t // GRID_W) * GRID_W + GRID_W - 1 - t % GRID_W, t] = 1
    sel = np.zeros((P, NG), np.float32)
    for j in range(TILE):
        for g in range(NG):
            sel[32 * j + g, g] = 1
    col = t % GRID_W
    start = np.clip(col - 8, 0, GRID_W - 16)[:, None]
    window = np.where((col[None, :] >= start) & (col[None, :] < start + 16), 0.0, -1e30).astype(np.float32)
    inv = np.float32(10000.0) ** (-np.arange(0, 64, 2, dtype=np.float32) / np.float32(64))
    ang = np.concatenate([(t // GRID_W).astype(np.float32)[:, None] * inv,
                          (t % GRID_W).astype(np.float32)[:, None] * inv], axis=1).astype(np.float32)
    return {"ident": np.eye(P, dtype=np.float32), "flip": flip, "sel": sel, "window": window,
            "rope_cos": np.cos(ang), "rope_sin": np.sin(ang)}


def kernel(**inputs):
    import numpy as np
    import concourse.bacc as bacc
    from concourse.bass_utils import run_bass_kernel_spmd

    nc = bacc.Bacc("TRN2", target_bir_lowering=False, num_devices=1)
    given = {k: np.ascontiguousarray(v) for k, v in inputs.items()}
    rows = [given[k].reshape(-1, P) for k in ("c_ctx", "c", "g_pre_mix", "g_pre_ffn", "conv_w", "conv_b",
                                              "b_rg_a", "b_rg_x", "rg_lambda", "state_rg_fwd", "state_rg_bwd")]
    host = {k: given[k] for k in _WHOLE}
    host["vectors"] = np.concatenate(rows, axis=0)
    host.update(tables(np))
    arrays, A, out = {}, {}, {}
    for name, a in host.items():
        arrays[f"in_{name}"] = a
        A[name] = nc.dram_tensor(f"in_{name}", a.shape, mybir.dt.from_np(a.dtype), kind="ExternalInput").ap()
    for name, shape in _OUTS:
        out[name] = nc.dram_tensor(f"out_{name}", shape, mybir.dt.float32, kind="ExternalOutput").ap()
    hybrid_step(nc, A, out)
    r = run_bass_kernel_spmd(nc, [arrays], core_ids=[0])
    return tuple(r.results[0][f"out_{name}"] for name, _ in _OUTS)
```

```python
import concourse.bass as bass
from concourse import mybir
from contextlib import ExitStack

D = 2048
T = 128
NG = 2
P = 128
KC = D // P
FF = 4 * D
HD = 128
NA = 8
NKV = 2
QKV_W = 3 * NA * HD + NA * HD + 2 * NKV * HD
QA0, KA0, VA0, QB0, KB0, VB0 = 0, 1024, 2048, 3072, 4096, 4352
GRID_W = 64
RPB_ROWS, RPB_COLS = 15, 31
EPS = 1e-6
SCALE = float(HD) ** -0.5
BLK = 512
QKV_BLOCKS = QKV_W // BLK
TILE = 4
NRAW = 4
NSPLIT = 4
GELU_C = 0.7978845608028654


class Sweep:

    def __init__(self, name, n, mode, weight, col0, tiles, blocks, ada, ada_at, order, out, skew=True):
        self.name, self.n, self.mode = name, n, mode
        self.weight, self.col0 = weight, col0
        self.tiles, self.blocks = tiles, blocks
        self.ada, self.ada_at = ada, ada_at
        self.order = order
        self.out = out
        self.skew = skew
        self.halves = 2 * order.count("M")
        assert order.count("M") == tiles * blocks and len(order) % NRAW == 0


def plan(w):
    ma = "MA" * 4
    sweeps = [
        Sweep("ada0", 8, None, None, 0, 0, 0, "cols", (0, 0), "AAAA", None),
        Sweep("att_in_a", 4, "token", w["att_in"], 0, 4, 1, "gate", (0, 8), ma, "qkv"),
        Sweep("att_in_b", 5, "token", w["att_in"], 4, 4, 1, "cols", (0, 12), ma, "qkv"),
        Sweep("att_out_a", 3, "token", w["att_out"], 0, 4, 1, "cols", (0, 17), ma, "op"),
        Sweep("att_out_b", 1, "token", w["att_out"], 3, 4, 1, None, None, "MMMM", "op"),
        Sweep("ff1_0", 8, "feature", w["ff1_0"], 0, 4, 2, "cols", (1, 0), "MMA" * 4, "hidden"),
        Sweep("ff2_0", 4, "token", w["ff2_0"], 0, 16, 1, "gate", (0, 20), "MMA" * 4 + "M" * 8, "op", False),
        Sweep("rec_in_a", 4, "feature", w["rec_in"], 0, 4, 1, "gate", (1, 8), ma, "xr"),
        Sweep("rec_in_b", 4, "feature", w["rec_in"], 4, 4, 1, "cols", (1, 12), ma, "gr"),
        Sweep("rec_out", 4, "token", w["rec_out"], 0, 4, 1, "cols", (1, 16), ma, "op"),
        Sweep("ff1_1", 8, "feature", w["ff1_1"], 0, 4, 2, None, None, "M" * 8, "hidden"),
        Sweep("ff2_1", 4, "token", w["ff2_1"], 0, 16, 1, "gate", (1, 20), "MMA" * 4 + "M" * 8, "op", False),
    ]
    pos = half = ada = token = feature = gate = main = 0
    for s in sweeps:
        s.pos0, s.main0, s.half0, s.ada0, s.token0, s.feature0, s.gate0 = pos, main, half, ada, token, feature, gate
        pos += s.n * len(s.order)
        main += s.n * s.order.count("M")
        half += s.n * s.halves
        ada += s.n * bool(s.ada)
        gate += s.n * (s.ada == "gate")
        if s.mode == "token":
            token += s.n * s.blocks
        if s.mode == "feature":
            feature += s.n * s.blocks
    return sweeps


def hybrid_step(nc, A, out):
    fp32 = mybir.dt.float32
    fp32r = mybir.dt.float32r
    ALU = mybir.AluOpType
    ACT = mybir.ActivationFunctionType
    AX = mybir.AxisListType.X

    def tiles_of(w):
        return w.rearrange("(t c p) n -> t p c n", c=TILE, p=P)

    W = {
        "att_in": tiles_of(A["w_att_in"][0]), "att_out": tiles_of(A["w_att_out"][0]),
        "rec_in": tiles_of(A["w_rec_in"][0]), "rec_out": tiles_of(A["w_rec_out"][0]),
        "ff1_0": tiles_of(A["w_ff1"][0]), "ff1_1": tiles_of(A["w_ff1"][1]),
        "ff2_0": tiles_of(A["w_ff2"][0]), "ff2_1": tiles_of(A["w_ff2"][1]),
    }
    W_ada = [tiles_of(A["w_ada"][layer]) for layer in range(2)]
    S = {s.name: s for s in plan(W)}
    sweeps = list(S.values())
    for s in sweeps:
        s.ada_early = NRAW if s.name in ("ff1_0", "rec_in_a") else 0
        s.early = {"att_in_a": 8, "att_out_a": 4, "ff1_0": 8, "rec_in_a": 8, "rec_out": 6, "ff1_1": 8}.get(s.name, 0)

    ctx = ExitStack()
    with ctx:
        def sb(name, shape, dt=fp32):
            return ctx.enter_context(nc.sbuf_tensor(name, shape, dt))

        def sem(name):
            return ctx.enter_context(nc.semaphore(name))

        raw = sb("raw", [P, NRAW, TILE, BLK])
        w_hi = sb("w_hi", [P, NSPLIT, 2, BLK], fp32r)
        w_lo = sb("w_lo", [P, NSPLIT, 2, BLK], fp32r)
        xt = sb("xt", [P, KC, 2 * NG * T], fp32r)
        x = sb("x", [P, NG, D])
        gate = sb("gate", [P, NG, D])
        R = sb("R", [P, 16384])
        cond = sb("cond", [P, KC, 32])
        ada_sum = sb("ada_sum", [P, BLK])
        ada_rows = sb("ada_rows", [P, BLK], fp32r)
        bias_rows = sb("bias_rows", [P, BLK])
        gain_rows = sb("gain_rows", [P, BLK])
        ada_cols = sb("ada_cols", [P, 2, KC, NG])
        ident = sb("ident", [P, P])
        flip = sb("flip", [P, P])
        sel = sb("sel", [P, 4])
        sel_r = sb("sel_r", [P, 2], fp32r)
        vec_a = sb("vec_a", [P, 96])
        vec_r = sb("vec_r", [P, 13 * KC])
        window = sb("window", [P, T])
        rope_cos = sb("rope_cos", [P, 64])
        rope_sin = sb("rope_sin", [P, 64])
        rpb = sb("rpb", [P, 4, T])
        th_a = rpb[:, :, :].rearrange("p (d h) t -> p d (h t)", d=2)
        small = sb("small", [P, 82])
        decay_cols = vec_a[:, 0:2 * KC]
        hidden = R[:, :].rearrange("p (c t) -> p c t", t=NG * T)
        qkv = R[:, 0:NG * QKV_W].rearrange("p (g n) -> p g n", g=NG)
        o = NG * QKV_W
        ctx_k = R[:, o:o + 1280].rearrange("p (h d) -> p h d", d=HD)
        ctx_v = R[:, o + 1280:o + 2560].rearrange("p (h d) -> p h d", d=HD)
        o += 2560
        q_t = R[:, o:o + 1024].rearrange("p (g h t) -> p g h t", g=NG, h=4)
        k_t = R[:, o + 1024:o + 2048].rearrange("p (g h t) -> p g h t", g=NG, h=4)
        ck_t = R[:, o + 2048:o + 2560].rearrange("p (h t) -> p h t", h=4)
        prob_s = R[:, o + 2560:o + 3584].rearrange("p (h t) -> p h t", h=4)
        prob_p = R[:, o + 3584:o + 4096].rearrange("p (h t) -> p h t", h=4)
        pc_t = R[:, o + 4096:o + 4608].rearrange("p (h t) -> p h t", h=4)
        rope_a = R[:, o + 4096:o + 4352].rearrange("p (h a f) -> p h a f", h=4, a=2)
        rope_b = R[:, o + 4352:o + 4608].rearrange("p (h a f) -> p h a f", h=4, a=2)
        xc = R[:, 0:4096].rearrange("p (c g t) -> p c g t", g=NG, t=T)
        gr = R[:, 4096:8192].rearrange("p (c t) -> p c t", t=NG * T)
        w_rg = R[:, 8192:9216].rearrange("p (s k j) -> p s k j", s=2, k=4)
        xr = R[:, 9216:10240].rearrange("p (c g t) -> p c g t", c=4, g=NG)
        gel = R[:, 9216:10240].rearrange("p (c n) -> p c n", c=4)
        decay = R[:, 10240:12288].rearrange("p (c d n) -> p c d n", c=4, d=2)
        drive = R[:, 12288:14336].rearrange("p (c d n) -> p c d n", c=4, d=2)
        root = R[:, 14336:16384].rearrange("p (c d n) -> p c d n", c=4, d=2)
        diag = R[:, 0:256].rearrange("p (g t) -> p g t", g=NG)
        h_mod = R[:, 256:1280].rearrange("p (s c g t) -> p s c g t", s=2, c=2, g=NG)
        junk = R[:, 4096:8192].rearrange("p (a n) -> p a n", a=4)
        stage = R[:, 2048:2048 + 3 * P].rearrange("p (a k) -> p a k", a=3)
        lam_t = R[:, 3072:3072 + 6 * 2 * KC].rearrange("p (a k) -> p a k", a=6)
        silu_t = R[:, 3584:3584 + 2 * NG * KC].rearrange("p (a k) -> p a k", a=2)
        ssq = small[:, 0:8].rearrange("p (g b) -> p g b", g=NG)
        ssq_x = small[:, 8:12].rearrange("p (g b) -> p g b", g=NG)
        mean = small[:, 12:14]
        rstd = small[:, 14:16]
        half_neg = small[:, 16:18]
        gs = small[:, 18:50].rearrange("p (c g) -> p c g", g=NG)
        mx = small[:, 50:58].rearrange("p (g h) -> p g h", g=NG)
        den = small[:, 58:66].rearrange("p (g h) -> p g h", g=NG)
        sink = small[:, 66:74]
        sink_e = small[:, 74:82].rearrange("p (g h) -> p g h", g=NG)
        states = rope_cos[:, 0:2 * KC]
        state_rows = rpb[0:2 * KC, 0, :]
        CONV_W, CONV_B, B_A, B_X, LAM, H0 = 0, 64, 80, 112, 144, 176

        ps = [ctx.enter_context(nc.psum_tensor(f"bank{i}", [P, BLK], fp32)) for i in range(8)]

        raw_landed = [sem(f"raw_landed{i}") for i in range(NRAW)]
        hi_ready = sem("hi_ready")
        lo_ready = sem("lo_ready")
        half_used = sem("half_used")
        ada_used = sem("ada_used")
        g0_done = sem("g0_done")
        chunk_done = sem("chunk_done")
        out_read_act = sem("out_read_act")
        out_read_dve = sem("out_read_dve")
        lo_copied = sem("lo_copied")
        chunk_read = sem("chunk_read")
        hidden_ready = sem("hidden_ready")
        bias_landed = sem("bias_landed")
        gain_landed = sem("gain_landed")
        ada_step = sem("ada_step")
        ada_row = sem("ada_row")
        ada_small = sem("ada_small")
        ada_fin = sem("ada_fin")
        x_landed = sem("x_landed")
        id_landed = sem("id_landed")
        const_landed = sem("const_landed")
        vec_a_landed = sem("vec_a_landed")
        vec_r_landed = sem("vec_r_landed")
        cache_landed = sem("cache_landed")
        rpb_landed = sem("rpb_landed")
        rg_landed = [sem("rg_landed0"), sem("rg_landed1")]
        stored = sem("stored")
        cleared = sem("cleared")
        dve_step = sem("dve_step")
        vec_turned = sem("vec_turned")
        vec_ready = sem("vec_ready")
        sel_ready = sem("sel_ready")
        cond_tanh = sem("cond_tanh")
        cond_ready = sem("cond_ready")
        lam_abs = sem("lam_abs")
        lam_exp = sem("lam_exp")
        rg_ready = sem("rg_ready")
        x_ready = sem("x_ready")
        ssq_ready = sem("ssq_ready")
        mean_ready = sem("mean_ready")
        rstd_ready = sem("rstd_ready")
        diag_ready = sem("diag_ready")
        turned = sem("turned")
        mod_ready = sem("mod_ready")
        mod_hi = sem("mod_hi")
        xt_ready = sem("xt_ready")
        qk_turned = sem("qk_turned")
        qk_copied_act = sem("qk_copied_act")
        qk_copied_dve = sem("qk_copied_dve")
        roped = sem("roped")
        scores_done = sem("scores_done")
        scores_scaled = sem("scores_scaled")
        bias_used = sem("bias_used")
        max_ready = sem("max_ready")
        exp_done = sem("exp_done")
        probs_ready = sem("probs_ready")
        probs_turned = sem("probs_turned")
        probs_copied_act = sem("probs_copied_act")
        probs_copied_dve = sem("probs_copied_dve")
        pv_done = sem("pv_done")
        heads_hi = sem("heads_hi")
        heads_ready = sem("heads_ready")
        conv_step = sem("conv_step")
        conv_ready = sem("conv_ready")
        gates_done = sem("gates_done")
        gates_read = sem("gates_read")
        roots_ready = sem("roots_ready")
        drive_step = sem("drive_step")
        scan_step = sem("scan_step")
        scanned = sem("scanned")
        act_step = sem("act_step")
        gelu_square = sem("gelu_square")
        gelu_arg = sem("gelu_arg")
        gelu_tanh = sem("gelu_tanh")
        gelu_ready = sem("gelu_ready")
        y_ready = sem("y_ready")
        y_hi = sem("y_hi")
        y_split = sem("y_split")
        states_turned = sem("states_turned")
        state_rows_ready = sem("state_rows_ready")

        block = ctx.enter_context(nc.Block())

        def first(it):
            return isinstance(it, int) and it == 0

        RG_GATES_AT, RG_TANHS_AT, RG_DRIVE_AT, RG_SCAN_AT = (0, 2, 3, 5), (2, 3, 5, 7), (3, 4, 6, 7), (0, 1, 3, 5)

        NORM_BANKS = (6, 7, 5)
        PROB_BANKS = ((0, 1, 2), (0, 1, 2), (0, 1, 2), (5, 6, 7))
        NORM_BEFORE = ("att_in_a", "ff1_0", "rec_in_a", "ff1_1")
        NORM_ADA = {0: 8, 1: 20, 2: 28, 3: 44}

        def heads_of(i):
            if i < 2:
                return True, QA0 + i * BLK, KA0 + i * BLK, VA0 + i * BLK, 4 * i, 4
            return False, QB0 + (i - 2) * BLK, KB0 + (i - 2) * HD, VB0 + (i - 2) * HD, NA + i - 2, 1

        def stream(s, it, p):
            return p % NRAW, 16 * (s.pos0 // NRAW + it * (len(s.order) // NRAW) + p // NRAW + 1)

        def released(s, it, p):
            if p >= NRAW:
                at, upto = (s, it), p - NRAW + 1
            elif first(it):
                k = sweeps.index(s)
                if k == 0:
                    return None
                b = sweeps[k - 1]
                at, upto = (b, b.n - 1), len(b.order) - NRAW + p + 1
            else:
                at, upto = (s, it - 1), len(s.order) - NRAW + p + 1
            b, i = at
            if b.order[upto - 1] == "M":
                return lo_ready, 2 * (b.main0 + i * b.order.count("M") + b.order[:upto].count("M"))
            return ada_used, TILE * b.ada0 + i * b.order.count("A") + b.order[:upto].count("A")

        def iterations(eng, s, body, before):
            body(s, 0, before)
            if s.n == 2:
                body(s, 1, (s, 0))
            elif s.n > 2:
                with eng.Fori(1, s.n) as it:
                    body(s, it, (s, it - 1))
            return s, s.n - 1

        class Steps:

            def __init__(self, eng, sem):
                self.eng, self.sem, self.n, self.ahead = eng, sem, 0, 0

            def __call__(self, ins):
                self.n += 1
                ins.then_inc(self.sem, 1)
                self.eng.wait_ge(self.sem, self.n + self.ahead)

        @block.sync
        def _(sp):
            def tiles(s, it, before):
                m = a = 0
                for p, kind in enumerate(s.order):
                    if kind == "M":
                        b, t = divmod(m, s.tiles)
                        w, col = s.weight[t], (s.col0 + it * s.blocks + b) * BLK
                        m += 1
                    else:
                        layer, col0 = s.ada_at
                        w, col = W_ada[layer][a], (col0 + it) * BLK
                        a += 1
                    if not isinstance(it, int):
                        col = sp.snap(col)
                    free = released(s, it, p)
                    if free:
                        sp.wait_ge(*free)
                    sp.dma_start(raw[:, p % NRAW, :, :], w[:, :, bass.ds(col, BLK)]).then_inc(raw_landed[p % NRAW], 16)

            sp.dma_start(stage[0:96, 0, :], A["vectors"][0:96, :]).then_inc(vec_a_landed, 16)
            sp.dma_start(ident[:, :], A["ident"]).then_inc(id_landed, 16)
            sp.dma_start(sel[:, :], A["sel"]).then_inc(id_landed, 16)
            for s in sweeps:
                iterations(sp, s, tiles, None)

        @block.gpsimd
        def _(pool):
            def ada_loads(s, it, before):
                b = s.ada0 + it
                layer, col = s.ada_at
                if not isinstance(b, int) or b > 0:
                    pool.wait_ge(ada_row, b)
                src = A["b_ada"][layer:layer + 1, bass.ds((col + it) * BLK, BLK)]
                pool.dma_start(bias_rows[0:2 * NG, :], src.broadcast_to([2 * NG, BLK])).then_inc(bias_landed, 16)
                if s.ada == "gate":
                    name = "g_post_ffn" if col >= 20 else "g_post_mix"
                    pool.wait_ge(ada_fin, b)
                    src = A[name][layer:layer + 1, bass.ds(it * BLK, BLK)]
                    pool.dma_start(gain_rows[:, :], src.broadcast_to([P, BLK])).then_inc(gain_landed, 16)

            def rsqrt(n):
                pool.wait_ge(mean_ready, n)
                nc.gpsimd.tensor_tensor(rstd, mean, half_neg, ALU.pow).then_inc(rstd_ready, 1)

            pool.wait_ge(cleared, 1)
            pool.dma_start(stage[0:112, 1, :], A["vectors"][96:208, :]).then_inc(vec_r_landed, 16)
            pool.dma_start(stage[0:96, 2, :], A["vectors"][208:304, :]).then_inc(vec_r_landed, 16)
            pool.dma_start(x[:, 0, :], A["x_prompt"][0]).then_inc(x_landed, 16)
            pool.dma_start(x[:, 1, :], A["x_sample"][0]).then_inc(x_landed, 16)
            pool.dma_start(flip[:, :], A["flip"]).then_inc(const_landed, 16)
            pool.dma_start(window[:, :], A["window"]).then_inc(const_landed, 16)
            pool.dma_start(rope_cos[:, :], A["rope_cos"]).then_inc(const_landed, 16)
            pool.dma_start(rope_sin[:, :], A["rope_sin"]).then_inc(const_landed, 16)
            pool.dma_start(sink, A["sink_b"].rearrange("a k g -> a (k g)").broadcast_to([P, 8])).then_inc(const_landed, 16)

            def load_rpb(quad):
                for r in range(2):
                    for rk in range(2):
                        at = 4 * quad * RPB_ROWS * RPB_COLS + (rk - r + 7) * RPB_COLS - 48
                        src = bass.AP(tensor=A["rpb_a"].tensor, offset=at,
                                      ap=[[1, GRID_W], [RPB_ROWS * RPB_COLS, 4], [1, GRID_W]])
                        pool.dma_start(rpb[GRID_W * r:GRID_W * (r + 1), :, GRID_W * rk:GRID_W * (rk + 1)], src)\
                            .then_inc(rpb_landed, 16)

            load_rpb(0)
            iterations(pool, S["ada0"], ada_loads, None)
            rsqrt(1)
            iterations(pool, S["att_in_a"], ada_loads, None)
            pool.wait_ge(xt_ready, KC // 2)
            pool.dma_start(ctx_k[:, 0:NA, :], A["cache_a_k"][0, 0]).then_inc(cache_landed, 16)
            pool.dma_start(ctx_k[:, NA:NA + NKV, :], A["cache_b_k"][0, 0]).then_inc(cache_landed, 16)
            pool.dma_start(ctx_v[:, 0:NA, :], A["cache_a_v"][0, 0]).then_inc(cache_landed, 16)
            pool.dma_start(ctx_v[:, NA:NA + NKV, :], A["cache_b_v"][0, 0]).then_inc(cache_landed, 16)
            iterations(pool, S["att_in_b"], ada_loads, None)
            pool.wait_ge(out_read_act, NG * QKV_BLOCKS)
            for a, c0, c1 in (("new_a_k", KA0, VA0), ("new_a_v", VA0, QB0), ("new_b_k", KB0, VB0),
                              ("new_b_v", VB0, QKV_W)):
                pool.dma_start(out[a][0, 0].rearrange("t h d -> t (h d)"), qkv[:, 0, c0:c1]).then_inc(stored, 16)
            pool.wait_ge(bias_used, 1)
            load_rpb(1)
            iterations(pool, S["att_out_a"], ada_loads, None)
            rsqrt(2)
            rsqrt(3)
            pool.wait_ge(stored, 16 * 4)
            iterations(pool, S["ff1_0"], ada_loads, None)
            iterations(pool, S["ff2_0"], ada_loads, None)
            rsqrt(4)
            rsqrt(5)
            iterations(pool, S["rec_in_a"], ada_loads, None)

            def rg_loads(s, it, before):
                for j in range(4):
                    if not (first(it) and j < 2):
                        pool.wait_ge(gates_done, 4 * it + j - 1)
                    for k, name in enumerate(("w_rg_a", "w_rg_x")):
                        src = A[name][0, :, bass.ds(4 * it + j, 1), :, :].rearrange("d o k j -> k d (o j)")
                        pool.dma_start(w_rg[:, j % 2, 2 * k:2 * k + 2, :], src).then_inc(rg_landed[j % 2], 16)
                ada_loads(s, it, before)

            pool.wait_ge(xt_ready, 3 * KC // 2)
            iterations(pool, S["rec_in_b"], rg_loads, None)
            iterations(pool, S["rec_out"], ada_loads, None)
            rsqrt(6)
            rsqrt(7)
            pool.wait_ge(state_rows_ready, 1)
            pool.dma_start(out["new_rg_fwd"].rearrange("a b (n k) -> (a b n) k", k=P), state_rows[0:KC, :]).then_inc(stored, 16)
            pool.dma_start(out["new_rg_bwd"].rearrange("a b (n k) -> (a b n) k", k=P), state_rows[KC:2 * KC, :]).then_inc(stored, 16)
            iterations(pool, S["ff2_1"], ada_loads, None)
            rsqrt(8)
            for k in range(4):
                pool.wait_ge(x_ready, 12 + k + 1)
                g, c = divmod(k, 2)
                pool.dma_start(out["y_prompt" if g == 0 else "y_sample"][0][:, c * 1024:(c + 1) * 1024],
                               x[:, g, c * 1024:(c + 1) * 1024]).then_inc(stored, 16)
            pool.wait_ge(stored, 16 * 10)

        @block.tensor
        def _(pe):
            def ada_tile(s, it, p, a):
                slot, landed = stream(s, it, p)
                b = s.ada0 + it
                pe.wait_ge(raw_landed[slot], landed)
                if a == 0 and not (isinstance(b, int) and b == 0):
                    pe.wait_ge(ada_row, b)
                for j in range(TILE):
                    mm = nc.tensor.matmul(ps[4][32 * j:32 * j + 32, :], cond[:, TILE * a + j, :],
                                          raw[:, slot, j, :], start=(a == 0), stop=(a == TILE - 1))
                mm.then_inc(ada_used, 1)

            def ada_ahead(s):
                at = [p for p in range(s.ada_early) if s.order[p] == "A"]
                for a, p in enumerate(at):
                    ada_tile(s, 0, p, a)

            def ada_end(s, it):
                b = s.ada0 + it
                pe.wait_ge(ada_row, b + 1)
                if not (isinstance(b, int) and b == 0):
                    pe.wait_ge(ada_fin, b)
                if s.name == "rec_in_a" and isinstance(it, int) and it == s.n - 1:
                    pe.wait_ge(gates_read, 4)
                if s.ada == "cols":
                    for m in range(BLK // P):
                        mm = nc.tensor.matmul(ps[5][:, NG * m:NG * m + NG], ada_rows[:, m * P:(m + 1) * P],
                                              sel_r[:, :], start=True, stop=True)
                else:
                    for g in range(NG):
                        mm = nc.tensor.matmul(ps[5 + g][:, :], sel_r[:, g:g + 1].broadcast_to([P, P]),
                                              ada_rows[:, :], start=True, stop=True)
                mm.then_inc(ada_small, 1)

            def token_half(s, h, g, hh, begin, end):
                for k in range(2):
                    c = (2 * hh + k) % KC
                    hi = xt[:, c, g * T:(g + 1) * T]
                    lo = xt[:, c, (NG + g) * T:(NG + g + 1) * T]
                    o = ps[g][:, :]
                    nc.tensor.matmul(o, hi, w_hi[:, h, k, :], start=(begin and k == 0), stop=False)
                    nc.tensor.matmul(o, hi, w_lo[:, h, k, :], start=False, stop=False)
                    mm = nc.tensor.matmul(o, lo, w_hi[:, h, k, :], start=False, stop=(end and k == 1))
                return mm

            def feature_half(s, h, m, hh, begin, end):
                for k in range(2):
                    c = (2 * hh + k) % KC
                    nc.tensor.matmul(ps[m][:, :], w_hi[:, h, k, m * P:(m + 1) * P], xt[:, c, :],
                                     start=(begin and k == 0), stop=False)
                    mm = nc.tensor.matmul(ps[m][:, 0:NG * T], w_lo[:, h, k, m * P:(m + 1) * P],
                                          xt[:, c, 0:NG * T], start=False, stop=(end and k == 1))
                return mm

            def rg_gates(it, j):
                n = 4 * it + j
                pe.wait_ge(rg_landed[j % 2], 32 * (2 * it + j // 2 + 1))
                pe.wait_ge(conv_ready, n + 1)
                if not (first(it) and j == 0):
                    pe.wait_ge(gates_read, n)
                if not first(it) and j == 0:
                    pe.wait_ge(ada_fin, S["rec_in_b"].ada0)
                for k in range(4):
                    at = (k % 2) * NG * T
                    mm = nc.tensor.matmul(ps[6 + k // 2][:, at:at + NG * T], w_rg[:, j % 2, k, :],
                                          xc[:, bass.ds(n, 1), :, :].rearrange("p o g t -> p (o g) t"), start=True, stop=True)
                mm.then_inc(gates_done, 1)

            def body(s, it, before):
                lanes = NG if s.mode == "token" else BLK // P
                m = a = 0
                for p, kind in enumerate(s.order):
                    if kind == "A":
                        if not (first(it) and p < s.ada_early):
                            ada_tile(s, it, p, a)
                        a += 1
                        if s.mode is None and a == 1 and before and before[0].ada:
                            ada_end(*before)
                        continue
                    b, t = divmod(m, s.tiles)
                    blk = it * s.blocks + b
                    for q in range(2):
                        hh = 2 * t + q
                        h = 2 * m + q
                        n = s.half0 + it * s.halves + h
                        if first(it) and s.name == "att_out_a" and hh == 2:
                            att_values(3)
                        if first(it) and b == 0 and s.name in NORM_BEFORE and hh + 3 < KC // 2:
                            turn_normed(NORM_BEFORE.index(s.name), hh + 3, hh + 4)
                        if first(it) and b == 0 and s.xt_ready is not None:
                            s_, base, per = s.xt_ready
                            pe.wait_ge(s_, base + hh // per + 1)
                        if s.out == "gr" and hh in RG_GATES_AT:
                            rg_gates(it, RG_GATES_AT.index(hh))
                        pe.wait_ge(lo_ready, n + 1)
                        if t == s.tiles - 1:
                            continue
                        for lane in range(lanes):
                            if hh == 0:
                                bank_free(s, blk, lane)
                            if s.mode == "token":
                                mm = token_half(s, h % NSPLIT, lane, hh, hh == 0, False)
                            else:
                                mm = feature_half(s, h % NSPLIT, lane, hh, hh == 0, False)
                        mm.then_inc(half_used, 1)
                    if t == s.tiles - 1:
                        for lane in range(lanes):
                            for q in range(2):
                                hh, h = 2 * t + q, 2 * m + q
                                if s.mode == "token":
                                    mm = token_half(s, h % NSPLIT, lane, hh, False, q == 1)
                                else:
                                    mm = feature_half(s, h % NSPLIT, lane, hh, False, q == 1)
                                if lane == lanes - 1:
                                    mm.then_inc(half_used, 1)
                                elif q == 1:
                                    mm.then_inc(g0_done if s.mode == "token" else chunk_done, 1)
                    m += 1
                    if m == (3 if s.out == "gr" else 2) and before and before[0].ada and before[0].skew:
                        ada_end(*before)
                    if not s.skew and m == 11:
                        ada_end(s, it)

            def bank_free(s, blk, lane):
                if s.mode == "token":
                    n = NG * (s.token0 + blk) - NG + lane + 1
                    if s.out == "qkv":
                        if not (first(blk) and s.token0 == 0):
                            pe.wait_ge(out_read_act, n)
                    elif not (first(blk) and s.name == "att_out_a"):
                        pe.wait_ge(out_read_dve, n - NG * QKV_BLOCKS)
                    if first(blk) and lane == 0 and s.feature0:
                        pe.wait_ge(chunk_read, 4 * s.feature0)
                else:
                    if not (first(blk) and s.feature0 == 0):
                        pe.wait_ge(chunk_read, 4 * (s.feature0 + blk) - 4 + lane + 1)
                    if first(blk) and lane == 0:
                        pe.wait_ge(out_read_dve, NG * (s.token0 - QKV_BLOCKS))

            def turn_normed(n, j0, j1):
                pe.wait_ge(diag_ready, n + 1)
                for j in range(j0, j1):
                    if j == 2:
                        pe.wait_ge(ada_fin, NORM_ADA[n])
                    if j >= 3:
                        pe.wait_ge(mod_ready, n * KC // 2 + j - 2)
                    for c in range(2):
                        for g in range(NG):
                            at = (c * NG + g) * T
                            mm = nc.tensor.matmul(ps[NORM_BANKS[j % 3]][:, at:at + T], x[:, g, (2 * j + c) * P:(2 * j + c + 1) * P],
                                                  diag[:, g, :], start=True, stop=True)
                    mm.then_inc(turned, 1)

            def att_turn(i):
                _, q0, k0, _, h0, nk = heads_of(i)
                if i == 0:
                    pe.wait_ge(out_read_act, NG * QKV_BLOCKS)
                    pe.wait_ge(cache_landed, 16 * 4)
                    pe.wait_ge(const_landed, 16 * 5)
                if i >= 2:
                    pe.wait_ge(heads_ready, i - 1)
                    pe.wait_ge(roped, 3)
                if i in (1, 2):
                    pe.wait_ge(bias_used, i)
                for g in range(NG):
                    for j in range(4):
                        nc.tensor.transpose(ps[g][:, j * T:(j + 1) * T], qkv[:, g, q0 + j * HD:q0 + (j + 1) * HD], ident[:, :])
                for j in range(nk):
                    for g in range(NG):
                        o = ps[2 + g][:, j * T:(j + 1) * T]
                        nc.tensor.transpose(o, qkv[:, g, k0 + j * HD:k0 + (j + 1) * HD], ident[:, :])
                    mm = nc.tensor.transpose(ps[4][:, j * T:(j + 1) * T], ctx_k[:, h0 + j, :], ident[:, :])
                mm.then_inc(qk_turned, 1)

            def att_scores(i):
                near = heads_of(i)[0]
                pe.wait_ge(qk_copied_act, i + 1)
                pe.wait_ge(qk_copied_dve, i + 1)
                for j in range(4):
                    kj = j if near else 0
                    for bank, g, keys in ((5, 0, k_t[:, 0, kj, :]), (6, 1, k_t[:, 1, kj, :]), (7, 1, ck_t[:, kj, :])):
                        mm = nc.tensor.matmul(ps[bank][:, j * T:(j + 1) * T], q_t[:, g, j, :], keys, start=True, stop=True)
                if near:
                    pe.wait_ge(rpb_landed, 16 * 4 * (i + 1))
                    mm = nc.tensor.matmul(ps[4][:, :], flip[:, :], rpb[:, :, :], start=True, stop=True)
                mm.then_inc(scores_done, 1)

            def att_values(i):
                _, q0, _, v0, h0, nk = heads_of(i)
                own_p, own_s, context = (ps[b] for b in PROB_BANKS[i])
                pe.wait_ge(probs_ready, i + 1)
                for j in range(4):
                    nc.tensor.transpose(own_p[:, j * T:(j + 1) * T], prob_p[:, j, :], ident[:, :])
                    nc.tensor.transpose(own_s[:, j * T:(j + 1) * T], prob_s[:, j, 0:T], ident[:, :])
                    mm = nc.tensor.transpose(context[:, j * T:(j + 1) * T], prob_s[:, j, T:2 * T], ident[:, :])
                mm.then_inc(probs_turned, 1)
                pe.wait_ge(probs_copied_act, i + 1)
                pe.wait_ge(probs_copied_dve, i + 1)
                for j in range(nk):
                    n = 4 * T // nk
                    cols = slice(j * n, (j + 1) * n)
                    keys = slice(q0 + j * n, q0 + (j + 1) * n)
                    vj = slice(v0 + j * HD, v0 + (j + 1) * HD)
                    nc.tensor.matmul(ps[3][:, cols], qkv[:, 0, vj], qkv[:, 0, keys], start=True, stop=True)
                    nc.tensor.matmul(ps[2][:, cols], qkv[:, 1, vj], qkv[:, 1, keys], start=True, stop=False)
                    mm = nc.tensor.matmul(ps[2][:, cols], ctx_v[:, h0 + j, :],
                                          pc_t[:, j * (4 // nk):(j + 1) * (4 // nk), :], start=False, stop=True)
                mm.then_inc(pv_done, 1)

            for s in sweeps:
                s.xt_ready = None
            S["att_in_a"].xt_ready = (xt_ready, 0, 1)
            S["att_out_a"].xt_ready = (heads_ready, 0, 2)
            S["ff1_0"].xt_ready = (xt_ready, KC // 2, 1)
            S["rec_in_a"].xt_ready = (xt_ready, 2 * KC // 2, 1)
            S["rec_out"].xt_ready = (y_split, 0, 1)
            S["ff1_1"].xt_ready = (xt_ready, 3 * KC // 2, 1)

            pe.wait_ge(vec_a_landed, 16)
            pe.wait_ge(id_landed, 32)
            nc.tensor.transpose(ps[5][:, 0:96], stage[0:96, 0, :], ident[0:96, 0:96]).then_inc(vec_turned, 1)
            pe.wait_ge(vec_r_landed, 32)
            nc.tensor.transpose(ps[6][:, 0:112], stage[0:112, 1, :], ident[0:112, 0:112])
            nc.tensor.transpose(ps[6][:, 112:208], stage[0:96, 2, :], ident[0:96, 0:96]).then_inc(vec_turned, 1)
            pe.wait_ge(vec_ready, 2)
            pe.wait_ge(cond_ready, 1)
            pe.wait_ge(sel_ready, 1)
            last = iterations(pe, S["ada0"], body, None)
            ada_end(*last)
            turn_normed(0, 0, 3)
            last = iterations(pe, S["att_in_a"], body, None)
            last = iterations(pe, S["att_in_b"], body, last)
            ada_end(*last)
            att_turn(0)
            att_scores(0)
            for i in range(3):
                att_turn(i + 1)
                att_scores(i + 1)
                att_values(i)
            last = iterations(pe, S["att_out_a"], body, None)
            last = iterations(pe, S["att_out_b"], body, last)
            ada_ahead(S["ff1_0"])
            turn_normed(1, 0, 3)
            last = iterations(pe, S["ff1_0"], body, None)
            last = iterations(pe, S["ff2_0"], body, last)
            ada_ahead(S["rec_in_a"])
            turn_normed(2, 0, 3)
            last = iterations(pe, S["rec_in_a"], body, None)
            last = iterations(pe, S["rec_in_b"], body, last)
            ada_end(*last)
            last = iterations(pe, S["rec_out"], body, None)
            pe.wait_ge(scanned, KC)
            nc.tensor.matmul(ps[6][0:2 * KC, 0:P], states, ident[:, :], start=True, stop=True).then_inc(states_turned, 1)
            ada_end(*last)
            pe.wait_ge(state_rows_ready, 1)
            turn_normed(3, 0, 3)
            last = iterations(pe, S["ff1_1"], body, None)
            last = iterations(pe, S["ff2_1"], body, last)

        @block.scalar
        def _(act):
            def split(s, it, h):
                n = s.half0 + it * s.halves + h
                t, q = divmod(h, 2)
                p = [i for i, k in enumerate(s.order) if k == "M"][t]
                slot, landed = stream(s, it, p)
                if s.tiles == 16:
                    if first(it):
                        act.wait_ge(hidden_ready, hidden0[s.name] + 2 * h + 2)
                if q == 0:
                    act.wait_ge(raw_landed[slot], landed)
                if not isinstance(n, int) or n >= NSPLIT:
                    act.wait_ge(half_used, n - NSPLIT + 1)
                if s.tiles == 16:
                    c = 2 * h % KC
                    nc.scalar.activation(xt[:, c:c + 2, 0:NG * T], hidden[:, 2 * h:2 * h + 2, :], ACT.Copy)
                nc.scalar.activation(w_hi[:, h % NSPLIT, :, :], raw[:, slot, 2 * q:2 * q + 2, :], ACT.Copy)\
                    .then_inc(hi_ready, 1)

            def split_early(name, h0, h1):
                for h in range(h0, h1):
                    split(S[name], 0, h)

            def out_ready(s, blk, g):
                if g == 0:
                    act.wait_ge(g0_done, s.token0 + blk + 1)
                else:
                    act.wait_ge(half_used, s.half0 + (blk + 1) * 2 * s.tiles)

            def token_out(s, blk, g):
                out_ready(s, blk, g)
                if s.out == "qkv":
                    nc.scalar.activation(qkv[:, g, bass.ds((s.col0 + blk) * BLK, BLK)], ps[g][:, :], ACT.Copy)\
                        .then_inc(out_read_act, 1)
                else:
                    act.wait_ge(out_read_act, NG * (s.token0 + blk) + g)
                    nc.scalar.activation(ps[7][:, :], ps[g][:, :], ACT.Square,
                                         accum_out=ssq[:, g, bass.ds(s.col0 + blk, 1)]).then_inc(out_read_act, 1)

            def feature_out(s, blk, m):
                if m < 3:
                    act.wait_ge(chunk_done, 3 * (s.feature0 + blk) + m + 1)
                else:
                    act.wait_ge(half_used, s.half0 + (blk + 1) * 2 * s.tiles)
                dst = hidden[:, bass.ds(4 * (s.col0 + blk) + m, 1), :]
                if s.out == "xr":
                    dst = gel[:, m:m + 1, :]
                    if m == 0 and not first(blk):
                        act.wait_ge(conv_ready, 4 * blk)
                nc.scalar.activation(dst, ps[m][:, NG * T:2 * NG * T].rearrange("p (o t) -> p o t", o=1), ACT.Copy)\
                    .then_inc(lo_copied, 1)

            def rg_tanhs(it, j):
                n = 4 * it + j
                steps.n, steps.ahead = 0, n * 2
                act.wait_ge(gates_done, n + 1)
                if not first(it):
                    act.wait_ge(scanned, n - 3)
                for d in range(2):
                    cols = [vec_r[:, bass.ds(base + d * KC + n, 1)] for base in (B_A, LAM, B_X)]
                    fast = decay_cols[:, bass.ds(d * KC + n, 1)]
                    steps(nc.scalar.activation(th_a[:, d, :], ps[6][:, d * NG * T:(d + 1) * NG * T],
                                               ACT.Tanh, scale=0.5, bias=cols[0]))
                    nc.scalar.activation(root[:, j, d, :], th_a[:, d, :], ACT.Tanh, scale=cols[1], bias=cols[1])
                    nc.scalar.activation(decay[:, j, d, :], th_a[:, d, :], ACT.Exp, scale=fast, bias=fast)
                    e = nc.scalar.activation(drive[:, j, d, :], ps[7][:, d * NG * T:(d + 1) * NG * T],
                                             ACT.Tanh, scale=0.5, bias=cols[2])
                e.then_inc(gates_read, 1)

            def rg_roots(it):
                act.wait_ge(gates_read, 4 * it + 4)
                flat = root.rearrange("p c d n -> p (c d n)")
                nc.scalar.activation(flat, flat, ACT.Sqrt).then_inc(roots_ready, 1)

            def gelu_squares(blk):
                act.wait_ge(chunk_read, 4 * (S["rec_in_b"].feature0 + blk) + 4)
                if first(blk):
                    act.wait_ge(conv_ready, KC)
                else:
                    act.wait_ge(y_ready, blk)
                nc.scalar.activation(gel, gr[:, bass.ds(4 * blk, 4), :], ACT.Square,
                                     scale=(0.044715 * GELU_C) ** 0.5).then_inc(gelu_square, 1)

            def gelu_tanhs(blk):
                act.wait_ge(gelu_arg, blk + 1)
                nc.scalar.activation(gel, gel, ACT.Tanh).then_inc(gelu_tanh, 1)

            def body(s, it, before):
                for b in range(s.blocks):
                    last = (s, it * s.blocks + b - 1) if b else (before and (before[0], before[1] * before[0].blocks + before[0].blocks - 1))
                    for hh in range(2 * s.tiles):
                        h = b * 2 * s.tiles + hh
                        if not (first(it) and h < s.early):
                            split(s, it, h)
                        if last and last[0].mode == "token" and hh == 1:
                            for g in range(NG):
                                token_out(*last, g)
                        if last and last[0].mode == "feature" and hh == 1:
                            for m in range(4):
                                feature_out(*last, m)
                        if s.out == "gr":
                            if last[0] is s and hh == 3:
                                gelu_squares(last[1])
                            if last[0] is s and hh == 4:
                                gelu_tanhs(last[1])
                            if hh in RG_TANHS_AT:
                                rg_tanhs(it, RG_TANHS_AT.index(hh))
                            if hh == 7:
                                rg_roots(it)

            def flush(last):
                s, it = last
                blk = it * s.blocks + s.blocks - 1
                if s.mode == "token":
                    for g in range(NG):
                        token_out(s, blk, g)
                else:
                    for m in range(4):
                        feature_out(s, blk, m)

            def squares_of_x(n):
                for k in range(4):
                    g, c = divmod(k, 2)
                    if n == 0:
                        act.wait_ge(x_landed, 32)
                    else:
                        act.wait_ge(x_ready, 4 * (n - 1) + k + 1)
                    nc.scalar.activation(junk[:, k, :], x[:, g, c * 1024:(c + 1) * 1024], ACT.Square,
                                         accum_out=ssq_x[:, g, c:c + 1]).then_inc(ssq_ready, 1)

            def norm(n, ahead, h0):
                for j in range(KC // 2):
                    if j >= h0:
                        split_early(ahead, j, j + 1)
                    act.wait_ge(mod_ready, n * KC // 2 + j + 1)
                    nc.scalar.activation(xt[:, 2 * j:2 * j + 2, 0:NG * T],
                                         h_mod[:, j % 2].rearrange("p c g t -> p c (g t)"), ACT.Copy).then_inc(mod_hi, 1)

            def att_copy_qk(i):
                n = heads_of(i)[5] * T
                act.wait_ge(qk_turned, i + 1)
                nc.scalar.activation(q_t[:, 0].rearrange("p h t -> p (h t)"), ps[0][:, :], ACT.Copy)
                nc.scalar.activation(k_t[:, 0].rearrange("p h t -> p (h t)")[:, 0:n], ps[2][:, 0:n], ACT.Copy)\
                    .then_inc(qk_copied_act, 1)

            def att_scale(i):
                act.wait_ge(scores_done, i + 1)
                nc.scalar.activation(prob_s[:, :, T:2 * T], ps[7][:, :].rearrange("p (h t) -> p h t", h=4), ACT.Copy, scale=SCALE)
                if i >= 2:
                    nc.scalar.activation(prob_s[:, :, 0:T], ps[6][:, :].rearrange("p (h t) -> p h t", h=4), ACT.Copy, scale=SCALE)
                nc.scalar.activation(prob_p.rearrange("p h t -> p (h t)"), ps[5][:, :], ACT.Copy, scale=SCALE).then_inc(scores_scaled, 1)

            def att_exp(i):
                act.wait_ge(max_ready, i + 1)
                if i >= 2:
                    nc.scalar.activation(sink_e, sink_e, ACT.Exp)
                for g, pr in ((0, prob_p), (1, prob_s)):
                    for j in range(4):
                        e = nc.scalar.activation(pr[:, j, :], pr[:, j, :], ACT.Exp, bias=mx[:, g, j:j + 1],
                                                 accum_out=den[:, g, j:j + 1])
                e.then_inc(exp_done, 1)

            def att_copy_probs(i):
                q0 = heads_of(i)[1]
                act.wait_ge(probs_turned, i + 1)
                nc.scalar.activation(qkv[:, 0, q0:q0 + BLK], ps[PROB_BANKS[i][0]][:, :], ACT.Copy).then_inc(probs_copied_act, 1)

            def att_heads(i):
                act.wait_ge(pv_done, i + 1)
                for g in range(NG):
                    e = nc.scalar.activation(xt[:, 4 * i:4 * i + 4, g * T:(g + 1) * T],
                                             ps[3 - g][:, :].rearrange("p (h t) -> p h t", h=4), ACT.Copy)
                e.then_inc(heads_hi, 1)

            steps = Steps(act, act_step)

            hidden0 = {"ff2_0": 0, "ff2_1": 4 * FF // BLK}

            act.wait_ge(vec_ready, 1)
            nc.scalar.activation(silu_t[:, 0, :], vec_a[:, 0:2 * KC], ACT.Tanh, scale=0.5).then_inc(cond_tanh, 1)
            act.wait_ge(lam_abs, 1)
            nc.scalar.activation(lam_t[:, 1, :], lam_t[:, 0, :], ACT.Exp, scale=-1.0).then_inc(lam_exp, 1)
            squares_of_x(0)
            split_early("att_in_a", 0, 1)
            norm(0, "att_in_a", 1)
            last = iterations(act, S["att_in_a"], body, None)
            last = iterations(act, S["att_in_b"], body, last)
            split_early("att_out_a", 0, 2)
            flush(last)
            att_copy_qk(0)
            split_early("att_out_a", 2, 4)
            att_scale(0)
            att_exp(0)
            att_copy_qk(1)
            for i in range(4):
                att_copy_probs(i)
                if i < 3:
                    att_scale(i + 1)
                att_heads(i)
                if i < 3:
                    att_exp(i + 1)
                if i < 2:
                    att_copy_qk(i + 2)
            last = iterations(act, S["att_out_a"], body, None)
            last = iterations(act, S["att_out_b"], body, last)
            split_early("ff1_0", 0, 2)
            flush(last)
            split_early("ff1_0", 2, 4)
            squares_of_x(1)
            norm(1, "ff1_0", 4)
            last = iterations(act, S["ff1_0"], body, None)
            last = iterations(act, S["ff2_0"], body, last)
            split_early("rec_in_a", 0, 2)
            flush(last)
            split_early("rec_in_a", 2, 4)
            squares_of_x(2)
            norm(2, "rec_in_a", 4)
            last = iterations(act, S["rec_in_a"], body, None)
            act.wait_ge(rg_ready, 1)
            last = iterations(act, S["rec_in_b"], body, last)
            split_early("rec_out", 0, 2)
            flush(last)
            split_early("rec_out", 2, 4)
            gelu_squares(3)
            for pair in range(KC // 2):
                if pair == 6:
                    gelu_tanhs(3)
                    split_early("rec_out", 4, 6)
                act.wait_ge(y_ready, pair // 2 + 1)
                nc.scalar.activation(xt[:, 2 * pair:2 * pair + 2, 0:NG * T],
                                     xc[:, 2 * pair:2 * pair + 2].rearrange("p c g t -> p c (g t)"), ACT.Copy)\
                    .then_inc(y_hi, 1)
            last = iterations(act, S["rec_out"], body, None)
            split_early("ff1_1", 0, 2)
            flush(last)
            split_early("ff1_1", 2, 4)
            squares_of_x(3)
            norm(3, "ff1_1", 4)
            last = iterations(act, S["ff1_1"], body, None)
            last = iterations(act, S["ff2_1"], body, last)
            flush(last)

        @block.vector
        def _(dve):
            steps = Steps(dve, dve_step)
            V = nc.vector

            def split(s, it, h):
                n = s.half0 + it * s.halves + h
                t, q = divmod(h, 2)
                slot = [i for i, k in enumerate(s.order) if k == "M"][t] % NRAW
                dve.wait_ge(hi_ready, n + 1)
                if s.tiles == 16:
                    c = 2 * h % KC
                    V.tensor_tensor(xt[:, c:c + 2, NG * T:2 * NG * T], hidden[:, 2 * h:2 * h + 2, :],
                                    xt[:, c:c + 2, 0:NG * T].bitcast(fp32), ALU.subtract)
                V.tensor_tensor(w_lo[:, h % NSPLIT, :, :], raw[:, slot, 2 * q:2 * q + 2, :],
                                w_hi[:, h % NSPLIT, :, :].bitcast(fp32), ALU.subtract).then_inc(lo_ready, 1)

            def split_early(name, h0, h1):
                for h in range(h0, h1):
                    split(S[name], 0, h)

            def token_out(s, blk, g):
                if s.out == "op":
                    dve.wait_ge(out_read_act, NG * (s.token0 + blk) + g + 1)
                    dst = gate[:, g, bass.ds((s.col0 + blk) * BLK, BLK)]
                    V.tensor_tensor(dst, ps[g][:, :], dst, ALU.mult).then_inc(out_read_dve, 1)

            def feature_out(s, blk, m):
                n = 4 * (s.feature0 + blk) + m
                dve.wait_ge(lo_copied, n + 1)
                dst = hidden[:, bass.ds(4 * (s.col0 + blk) + m, 1), :].rearrange("p o t -> p (o t)")
                if s.out == "xr":
                    dst = gel[:, m, :]
                V.tensor_tensor(dst, ps[m][:, 0:NG * T], dst, ALU.add).then_inc(chunk_read, 1)
                if s.out == "hidden":
                    dve.wait_ge(chunk_read, n + 1)
                    V.scalar_tensor_tensor(out=dst, in0=dst, scalar=0.0, in1=dst, op0=ALU.max, op1=ALU.mult)\
                        .then_inc(hidden_ready, 1)

            def ada_rows_out(s, it):
                b = s.ada0 + it
                dve.wait_ge(ada_used, TILE * (b + 1))
                dve.wait_ge(bias_landed, 16 * (b + 1))
                if not (isinstance(b, int) and b == 0):
                    dve.wait_ge(ada_small, b)
                V.tensor_tensor(ada_sum[:, :], ps[4][:, :], bias_rows[:, :], ALU.add).then_inc(ada_step, 1)
                dve.wait_ge(ada_step, 2 * b + 1)
                V.tensor_copy(ada_rows[:, :], ada_sum[:, :]).then_inc(ada_step, 1)
                dve.wait_ge(ada_step, 2 * b + 2)
                V.scalar_tensor_tensor(out=ada_rows[:, :], in0=ada_rows[:, :].bitcast(fp32), scalar=sel[:, 2:3],
                                       in1=ada_sum[:, :], op0=ALU.mult, op1=ALU.add).then_inc(ada_row, 1)

            def ada_store(s, it):
                b = s.ada0 + it
                dve.wait_ge(ada_small, b + 1)
                if s.ada == "cols":
                    base = s.ada_at[1] - (12 if s.ada_at[1] >= 12 else 0)
                    flat = ada_cols[:, :, :, :].rearrange("p a c g -> p (a c g)")
                    V.tensor_copy(flat[:, bass.ds((base + it) * 4 * NG, 4 * NG)], ps[5][:, 0:4 * NG]).then_inc(ada_fin, 1)
                else:
                    dve.wait_ge(gain_landed, 16 * (s.gate0 + it + 1))
                    for g in range(NG):
                        e = V.tensor_tensor(gate[:, g, bass.ds(it * BLK, BLK)], ps[5 + g][:, :], gain_rows[:, :], ALU.mult)
                    e.then_inc(ada_fin, 1)

            def body(s, it, before):
                if s.mode is None:
                    if before:
                        ada_store(*before)
                    ada_rows_out(s, it)
                    return
                for b in range(s.blocks):
                    last = (s, it * s.blocks + b - 1) if b else (before and (before[0], before[1] * before[0].blocks + before[0].blocks - 1))
                    for hh in range(2 * s.tiles):
                        h = b * 2 * s.tiles + hh
                        if not (first(it) and h < s.early):
                            split(s, it, h)
                        if last and last[0].mode == "token" and hh == 1:
                            if last[0].out == "op":
                                dve.wait_ge(ada_fin, gate_of(*last))
                            for g in range(NG):
                                token_out(*last, g)
                        if last and last[0].mode == "feature" and hh == 1:
                            for m in range(4):
                                feature_out(*last, m)
                        if last and last[0].out == "xr" and hh == 3:
                            convolve(last[1])
                        if s.out == "gr":
                            if last[0] is s and hh in RG_SCAN_AT:
                                rg_scan(last[1], RG_SCAN_AT.index(hh))
                            if hh in RG_DRIVE_AT:
                                rg_drive(it, RG_DRIVE_AT.index(hh))
                            if last[0] is s and hh == 3:
                                gelu_arguments(last[1])
                            if last[0] is s and hh == 6:
                                outputs(last[1])
                        if before and before[0].ada and before[0].skew and b == 0:
                            if hh == 1:
                                ada_rows_out(*before)
                            if hh == 7:
                                ada_store(*before)
                        if not s.skew and hh == 19:
                            ada_rows_out(s, it)
                        if not s.skew and hh == 25:
                            ada_store(s, it)

            def gate_of(s, blk):
                return {"att_out_a": 12, "att_out_b": 12, "ff2_0": S["ff2_0"].ada0 + blk + 1,
                        "rec_out": S["rec_in_a"].ada0 + 4, "ff2_1": S["ff2_1"].ada0 + blk + 1}[s.name]

            def flush(last):
                s, it = last
                blk = it * s.blocks + s.blocks - 1
                if s.mode == "token":
                    if s.out == "op":
                        dve.wait_ge(ada_fin, gate_of(s, blk))
                    for g in range(NG):
                        token_out(s, blk, g)
                else:
                    for m in range(4):
                        feature_out(s, blk, m)

            def mean_of(sums, b):
                steps(V.tensor_reduce(mean, sums, AX, ALU.add))
                V.tensor_scalar(mean, mean, 1.0 / D, EPS, ALU.mult, ALU.add).then_inc(mean_ready, 1)

            def residual(n, ahead=None):
                dve.wait_ge(out_read_dve, NG * (blocks_done[n] - QKV_BLOCKS))
                mean_of(ssq, 4)
                if ahead:
                    split_early(ahead, 2, 3)
                dve.wait_ge(rstd_ready, 2 * n)
                for k in range(4):
                    g, c = divmod(k, 2)
                    cols = slice(c * 1024, (c + 1) * 1024)
                    V.scalar_tensor_tensor(out=x[:, g, cols], in0=gate[:, g, cols], scalar=rstd[:, g:g + 1],
                                           in1=x[:, g, cols], op0=ALU.mult, op1=ALU.add).then_inc(x_ready, 1)

            def norm_scale(n, ahead, h):
                dve.wait_ge(ssq_ready, 4 * (n + 1))
                mean_of(ssq_x, 2)
                split_early(ahead, h, h + 1)
                dve.wait_ge(rstd_ready, 2 * n + 1)
                for g in range(NG):
                    e = V.tensor_scalar(diag[:, g, :], ident[:, :], rstd[:, g:g + 1], None, ALU.mult)
                e.then_inc(diag_ready, 1)

            def norm(n, gain, ahead, h0):
                dve.wait_ge(ada_fin, NORM_ADA[n])
                steps(V.scalar_tensor_tensor(out=gs, in0=ada_cols[:, 1], scalar=1.0,
                                             in1=vec_a[:, gain:gain + KC].unsqueeze(2).broadcast_to([P, KC, NG]),
                                             op0=ALU.add, op1=ALU.mult))

                def rest(j):
                    dve.wait_ge(mod_hi, n * KC // 2 + j + 1)
                    V.tensor_tensor(xt[:, 2 * j:2 * j + 2, NG * T:2 * NG * T],
                                    h_mod[:, j % 2].rearrange("p c g t -> p c (g t)"),
                                    xt[:, 2 * j:2 * j + 2, 0:NG * T].bitcast(fp32), ALU.subtract).then_inc(xt_ready, 1)

                for j in range(KC // 2):
                    dve.wait_ge(turned, n * KC // 2 + j + 1)
                    if j >= 2:
                        dve.wait_ge(xt_ready, n * KC // 2 + j - 1)
                    for c in range(2):
                        for g in range(NG):
                            at = (c * NG + g) * T
                            e = V.tensor_scalar(h_mod[:, j % 2, c, g, :], ps[NORM_BANKS[j % 3]][:, at:at + T],
                                                gs[:, 2 * j + c, g:g + 1], ada_cols[:, 0, 2 * j + c, g:g + 1],
                                                ALU.mult, ALU.add)
                    e.then_inc(mod_ready, 1)
                    if j:
                        rest(j - 1)
                    if j >= h0:
                        split_early(ahead, j, j + 1)
                rest(KC // 2 - 1)

            def rope():
                for n, (c0, c1) in enumerate(((QB0, QB0 + BLK), (QB0 + BLK, KB0), (KB0, VB0))):
                    h = (c1 - c0) // HD
                    qk = qkv[:, 1, c0:c1].rearrange("p (h a f) -> p h a f", h=h, a=2)
                    x1, x2 = qk[:, :, :, 0:32], qk[:, :, :, 32:64]
                    cos = rope_cos[:, :].rearrange("p (a f) -> p a f", a=2).unsqueeze(1).broadcast_to([P, h, 2, 32])
                    sin = rope_sin[:, :].rearrange("p (a f) -> p a f", a=2).unsqueeze(1).broadcast_to([P, h, 2, 32])
                    V.tensor_tensor(rope_a[:, 0:h], x2, sin, ALU.mult)
                    steps(V.tensor_tensor(rope_b[:, 0:h], x1, sin, ALU.mult))
                    V.tensor_tensor(x1, x1, cos, ALU.mult)
                    steps(V.tensor_tensor(x2, x2, cos, ALU.mult))
                    V.tensor_tensor(x1, x1, rope_a[:, 0:h], ALU.subtract)
                    V.tensor_tensor(x2, x2, rope_b[:, 0:h], ALU.add).then_inc(roped, 1)
                    dve.wait_ge(roped, n + 1)

            def att_copy_qk(i):
                n = heads_of(i)[5] * T
                dve.wait_ge(qk_turned, i + 1)
                V.tensor_copy(q_t[:, 1].rearrange("p h t -> p (h t)"), ps[1][:, :])
                V.tensor_copy(k_t[:, 1].rearrange("p h t -> p (h t)")[:, 0:n], ps[3][:, 0:n])
                V.tensor_copy(ck_t.rearrange("p h t -> p (h t)")[:, 0:n], ps[4][:, 0:n]).then_inc(qk_copied_dve, 1)

            def att_max(i):
                near = i < 2
                dve.wait_ge(scores_done, i + 1)
                if near:
                    steps(V.tensor_tensor(rpb[:, :, :], ps[4][:, :].rearrange("p (h t) -> p h t", h=4),
                                          window[:, :].unsqueeze(1).broadcast_to([P, 4, T]), ALU.add))
                    V.scalar_tensor_tensor(out=prob_s[:, :, 0:T], in0=ps[6][:, :].rearrange("p (h t) -> p h t", h=4),
                                           scalar=SCALE, in1=rpb[:, :, :], op0=ALU.mult, op1=ALU.add).then_inc(bias_used, 1)
                    dve.wait_ge(bias_used, i + 1)
                dve.wait_ge(scores_scaled, i + 1)
                V.tensor_reduce(mx[:, 0, :], prob_p, AX, ALU.max)
                steps(V.tensor_reduce(mx[:, 1, :], prob_s, AX, ALU.max))
                if not near:
                    sinks = sink[:, 4 * (i - 2):4 * (i - 1)].unsqueeze(1).broadcast_to([P, NG, 4])
                    steps(V.tensor_tensor(mx, mx, sinks, ALU.max))
                    steps(V.tensor_tensor(sink_e, sinks, mx, ALU.subtract))
                V.tensor_scalar(mx, mx, -1.0, None, ALU.mult).then_inc(max_ready, 1)

            def att_norm(i):
                dve.wait_ge(exp_done, i + 1)
                if i >= 2:
                    steps(V.tensor_tensor(den, den, sink_e, ALU.add))
                steps(V.reciprocal(den, den))
                V.tensor_tensor(prob_p, prob_p, den[:, 0, :].unsqueeze(2).broadcast_to([P, 4, T]), ALU.mult)
                V.tensor_tensor(prob_s, prob_s, den[:, 1, :].unsqueeze(2).broadcast_to([P, 4, 2 * T]), ALU.mult)\
                    .then_inc(probs_ready, 1)

            def att_copy_probs(i):
                q0 = heads_of(i)[1]
                dve.wait_ge(probs_turned, i + 1)
                V.tensor_copy(qkv[:, 1, q0:q0 + BLK], ps[PROB_BANKS[i][1]][:, :])
                V.tensor_copy(pc_t.rearrange("p h t -> p (h t)"), ps[PROB_BANKS[i][2]][:, :]).then_inc(probs_copied_dve, 1)

            def att_heads(i):
                dve.wait_ge(heads_hi, i + 1)
                for g in range(NG):
                    e = V.tensor_tensor(xt[:, 4 * i:4 * i + 4, (NG + g) * T:(NG + g + 1) * T],
                                        ps[3 - g][:, :].rearrange("p (h t) -> p h t", h=4),
                                        xt[:, 4 * i:4 * i + 4, g * T:(g + 1) * T].bitcast(fp32), ALU.subtract)
                e.then_inc(heads_ready, 1)

            def decay_rates():
                lam = vec_r[:, LAM:LAM + 2 * KC]
                L = [lam_t[:, a, :] for a in range(6)]
                V.tensor_scalar(vec_r[:, B_A:B_A + 4 * KC], vec_r[:, B_A:B_A + 4 * KC], 0.5, None, ALU.mult)
                V.scalar_tensor_tensor(out=L[0], in0=lam, scalar=-1.0, in1=lam, op0=ALU.mult, op1=ALU.max)\
                    .then_inc(lam_abs, 1)
                dve.wait_ge(lam_exp, 1)
                steps(V.tensor_scalar(L[2], L[1], 2.0, None, ALU.add))
                steps(V.reciprocal(L[2], L[2]))
                steps(V.tensor_tensor(L[2], L[1], L[2], ALU.mult))
                steps(V.tensor_tensor(L[3], L[2], L[2], ALU.mult))
                steps(V.tensor_scalar(L[4], L[3], 1.0 / 17, None, ALU.mult))
                for k in range(15, 1, -2):
                    steps(V.scalar_tensor_tensor(out=L[4], in0=L[4], scalar=1.0 / k, in1=L[3], op0=ALU.add, op1=ALU.mult))
                steps(V.scalar_tensor_tensor(out=L[4], in0=L[4], scalar=1.0, in1=L[2], op0=ALU.add, op1=ALU.mult))
                steps(V.tensor_scalar(L[5], lam, -1.0, 0.0, ALU.mult, ALU.max))
                steps(V.scalar_tensor_tensor(out=L[5], in0=L[4], scalar=2.0, in1=L[5], op0=ALU.mult, op1=ALU.add))
                V.tensor_scalar(decay_cols, L[5], -4.0, None, ALU.mult)
                V.tensor_scalar(vec_r[:, H0:H0 + 2 * KC], vec_r[:, H0:H0 + 2 * KC], 2.0, None, ALU.mult)
                V.tensor_scalar(lam, L[5], 2.0, None, ALU.mult).then_inc(rg_ready, 1)

            def convolve(blk):
                def param(base, m):
                    return vec_r[:, bass.ds(base + 4 * blk + m, 1)]

                def wait_taps(k):
                    dve.wait_ge(conv_step, 3 * blk + k)

                dve.wait_ge(chunk_read, 4 * (S["rec_in_a"].feature0 + blk) + 4)
                xs = [xr[:, m] for m in range(4)]
                ys = [xc[:, bass.ds(4 * blk + m, 1)].rearrange("p o g t -> p (o g) t") for m in range(4)]
                for m in range(4):
                    e = V.tensor_scalar(ys[m], xs[m], param(CONV_W + 2 * KC, m), param(CONV_B, m), ALU.mult, ALU.add)
                e.then_inc(conv_step, 1)
                for k, (tap, back) in enumerate(((0, 2), (1, 1))):
                    wait_taps(k + 1)
                    for m in range(4):
                        e = V.scalar_tensor_tensor(out=ys[m][:, :, back:], in0=xs[m][:, :, 0:T - back],
                                                   scalar=param(CONV_W + tap * KC, m), in1=ys[m][:, :, back:],
                                                   op0=ALU.mult, op1=ALU.add)
                    e.then_inc(conv_step, 1)
                wait_taps(3)
                for m in range(4):
                    V.scalar_tensor_tensor(out=ys[m][:, :, 0:T - 1], in0=xs[m][:, :, 1:T],
                                           scalar=param(CONV_W + 3 * KC, m), in1=ys[m][:, :, 0:T - 1],
                                           op0=ALU.mult, op1=ALU.add).then_inc(conv_ready, 1)

            drive_steps, scan_steps = Steps(dve, drive_step), Steps(dve, scan_step)

            def rg_drive(it, j):
                n = 4 * it + j
                drive_steps.n, drive_steps.ahead = 0, 2 * n
                dve.wait_ge(gates_read, n + 1)
                x_c = xc[:, bass.ds(n, 1)].rearrange("p o g t -> p o (g t)").broadcast_to([P, 2, NG * T])
                v = drive[:, j]
                drive_steps(V.scalar_tensor_tensor(out=v, in0=v, scalar=1.0, in1=x_c, op0=ALU.add, op1=ALU.mult))
                drive_steps(V.scalar_tensor_tensor(out=v, in0=decay[:, j], scalar=1.0, in1=v, op0=ALU.add, op1=ALU.mult))

            def rg_scan(it, j):
                n = 4 * it + j
                scan_steps.n, scan_steps.ahead = 0, 2 * n
                dve.wait_ge(roots_ready, it + 1)
                scan_steps(V.tensor_tensor(drive[:, j], drive[:, j], root[:, j], ALU.mult))
                for d in range(2):
                    for g in range(NG):
                        way = slice(None, None, -1) if d else slice(None)
                        a, b, h = (z[:, j, d, g * T:(g + 1) * T][:, way] for z in (decay, drive, root))
                        h0 = 0.0 if g == 0 else vec_r[:, bass.ds(H0 + d * KC + n, 1)]
                        e = V.tensor_tensor_scan(h, a, b, h0, ALU.mult, ALU.add)
                scan_steps(e)
                for d in range(2):
                    end = 0 if d else T - 1
                    V.tensor_scalar(states[:, bass.ds(d * KC + n, 1)], root[:, j, d, end:end + 1], 0.5, None, ALU.mult)
                V.tensor_tensor(xc[:, bass.ds(n, 1)].rearrange("p o g t -> p (o g t)"), root[:, j, 0, :],
                                root[:, j, 1, :], ALU.add).then_inc(scanned, 1)

            def gelu_arguments(blk):
                dve.wait_ge(gelu_square, blk + 1)
                V.scalar_tensor_tensor(out=gel, in0=gel, scalar=GELU_C, in1=gr[:, bass.ds(4 * blk, 4), :],
                                       op0=ALU.add, op1=ALU.mult).then_inc(gelu_arg, 1)

            def outputs(blk):
                dve.wait_ge(gelu_tanh, blk + 1)
                V.scalar_tensor_tensor(out=gel, in0=gel, scalar=1.0, in1=gr[:, bass.ds(4 * blk, 4), :],
                                       op0=ALU.add, op1=ALU.mult).then_inc(gelu_ready, 1)
                dve.wait_ge(gelu_ready, blk + 1)
                dve.wait_ge(scanned, 4 * blk + 4)
                y = xc[:, bass.ds(4 * blk, 4)].rearrange("p c g t -> p c (g t)")
                V.scalar_tensor_tensor(out=y, in0=gel, scalar=0.25, in1=y, op0=ALU.mult, op1=ALU.mult)\
                    .then_inc(y_ready, 1)

            blocks_done = {1: 13, 2: 17, 3: 21, 4: 25}

            V.memset(bias_rows[:, :], 0.0)
            V.memset(half_neg, -0.5)
            steps(V.memset(cond[:, :, :], 0.0))
            V.memset(ssq_x, 0.0).then_inc(cleared, 1)
            dve.wait_ge(vec_turned, 1)
            V.tensor_copy(vec_a[:, :], ps[5][:, 0:96]).then_inc(vec_ready, 1)
            dve.wait_ge(cond_tanh, 1)
            steps(V.scalar_tensor_tensor(out=silu_t[:, 1, :], in0=silu_t[:, 0, :], scalar=1.0, in1=vec_a[:, 0:2 * KC],
                                         op0=ALU.add, op1=ALU.mult))
            for part in range(2):
                e = V.tensor_scalar(cond[:, :, part * NG:(part + 1) * NG].rearrange("p c g -> p g c"),
                                    silu_t[:, 1, :].rearrange("p (g c) -> p g c", g=NG), 0.5, None, ALU.mult)
            e.then_inc(cond_ready, 1)
            dve.wait_ge(id_landed, 32)
            V.tensor_copy(sel_r[:, :], sel[:, 0:2]).then_inc(sel_ready, 1)
            dve.wait_ge(vec_turned, 2)
            V.tensor_copy(vec_r[:, :], ps[6][:, 0:208]).then_inc(vec_ready, 1)
            dve.wait_ge(vec_ready, 2)
            decay_rates()
            last = iterations(dve, S["ada0"], body, None)
            norm_scale(0, "att_in_a", 0)
            ada_store(*last)
            norm(0, 2 * KC, "att_in_a", 1)
            last = iterations(dve, S["att_in_a"], body, None)
            last = iterations(dve, S["att_in_b"], body, last)
            split_early("att_out_a", 0, 2)
            flush(last)
            ada_rows_out(*last)
            ada_store(*last)
            att_copy_qk(0)
            rope()
            att_max(0)
            att_copy_qk(1)
            split_early("att_out_a", 2, 3)
            att_norm(0)
            for i in range(4):
                att_copy_probs(i)
                if i < 3:
                    att_max(i + 1)
                att_heads(i)
                if i < 2:
                    att_copy_qk(i + 2)
                if i == 2:
                    split_early("att_out_a", 3, 4)
                if i < 3:
                    att_norm(i + 1)
            last = iterations(dve, S["att_out_a"], body, None)
            last = iterations(dve, S["att_out_b"], body, last)
            split_early("ff1_0", 0, 2)
            flush(last)
            residual(1, "ff1_0")
            norm_scale(1, "ff1_0", 3)
            norm(1, 4 * KC, "ff1_0", 4)
            last = iterations(dve, S["ff1_0"], body, None)
            last = iterations(dve, S["ff2_0"], body, last)
            split_early("rec_in_a", 0, 2)
            flush(last)
            residual(2, "rec_in_a")
            norm_scale(2, "rec_in_a", 3)
            norm(2, 3 * KC, "rec_in_a", 4)
            last = iterations(dve, S["rec_in_a"], body, None)
            last = iterations(dve, S["rec_in_b"], body, last)
            split_early("rec_out", 0, 2)
            flush(last)
            ada_rows_out(*last)
            split_early("rec_out", 2, 4)
            gelu_arguments(3)
            ada_store(*last)
            for pair in range(KC // 2):
                if pair == 6:
                    for j in range(4):
                        if j >= 2:
                            split_early("rec_out", 2 + j, 3 + j)
                        rg_scan(3, j)
                    outputs(3)
                dve.wait_ge(y_hi, pair + 1)
                V.tensor_tensor(xt[:, 2 * pair:2 * pair + 2, NG * T:2 * NG * T],
                                xc[:, 2 * pair:2 * pair + 2].rearrange("p c g t -> p c (g t)"),
                                xt[:, 2 * pair:2 * pair + 2, 0:NG * T].bitcast(fp32), ALU.subtract).then_inc(y_split, 1)
            last = iterations(dve, S["rec_out"], body, None)
            split_early("ff1_1", 0, 2)
            flush(last)
            ada_rows_out(*last)
            dve.wait_ge(states_turned, 1)
            V.tensor_copy(state_rows, ps[6][0:2 * KC, 0:P]).then_inc(state_rows_ready, 1)
            ada_store(*last)
            residual(3, "ff1_1")
            norm_scale(3, "ff1_1", 3)
            norm(3, 5 * KC, "ff1_1", 4)
            last = iterations(dve, S["ff1_1"], body, None)
            last = iterations(dve, S["ff2_1"], body, last)
            flush(last)
            residual(4)


_OUTS = [("y_prompt", (1, T, D)), ("y_sample", (1, T, D)),
         ("new_a_k", (1, 1, T, NA, HD)), ("new_a_v", (1, 1, T, NA, HD)),
         ("new_b_k", (1, 1, T, NKV, HD)), ("new_b_v", (1, 1, T, NKV, HD)),
         ("new_rg_fwd", (1, 1, D)), ("new_rg_bwd", (1, 1, D))]
_WHOLE = ["x_prompt", "x_sample", "cache_a_k", "cache_a_v", "cache_b_k", "cache_b_v", "w_ada", "b_ada",
          "g_post_mix", "g_post_ffn", "w_att_in", "w_att_out", "sink_b", "rpb_a", "w_rec_in", "w_rg_a",
          "w_rg_x", "w_rec_out", "w_ff1", "w_ff2"]


def tables(np):
    t = np.arange(T)
    flip = np.zeros((P, P), np.float32)
    flip[(t // GRID_W) * GRID_W + GRID_W - 1 - t % GRID_W, t] = 1
    sel = np.zeros((P, 2 * NG), np.float32)
    for j in range(TILE):
        for g in range(NG):
            sel[[32 * j + g, 32 * j + NG + g], g] = 1
            sel[32 * j + NG + g, NG] = -1
    col = t % GRID_W
    start = np.clip(col - 8, 0, GRID_W - 16)[:, None]
    window = np.where((col[None, :] >= start) & (col[None, :] < start + 16), 0.0, -1e30).astype(np.float32)
    inv = np.float32(10000.0) ** (-np.arange(0, 64, 2, dtype=np.float32) / np.float32(64))
    ang = np.concatenate([(t // GRID_W).astype(np.float32)[:, None] * inv,
                          (t % GRID_W).astype(np.float32)[:, None] * inv], axis=1).astype(np.float32)
    return {"ident": np.eye(P, dtype=np.float32), "flip": flip, "sel": sel, "window": window,
            "rope_cos": np.cos(ang), "rope_sin": np.sin(ang)}


def kernel(**inputs):
    import numpy as np
    import concourse.bacc as bacc
    from concourse.bass_utils import run_bass_kernel_spmd

    nc = bacc.Bacc("TRN2", target_bir_lowering=False, num_devices=1)
    given = {k: np.ascontiguousarray(v) for k, v in inputs.items()}
    rows = [given[k].reshape(-1, P) for k in ("c_ctx", "c", "g_pre_mix", "g_pre_ffn", "conv_w", "conv_b",
                                              "b_rg_a", "b_rg_x", "rg_lambda", "state_rg_fwd", "state_rg_bwd")]
    host = {k: given[k] for k in _WHOLE}
    host["vectors"] = np.concatenate(rows, axis=0)
    host.update(tables(np))
    arrays, A, out = {}, {}, {}
    for name, a in host.items():
        arrays[f"in_{name}"] = a
        A[name] = nc.dram_tensor(f"in_{name}", a.shape, mybir.dt.from_np(a.dtype), kind="ExternalInput").ap()
    for name, shape in _OUTS:
        out[name] = nc.dram_tensor(f"out_{name}", shape, mybir.dt.float32, kind="ExternalOutput").ap()
    hybrid_step(nc, A, out)
    r = run_bass_kernel_spmd(nc, [arrays], core_ids=[0])
    return tuple(r.results[0][f"out_{name}"] for name, _ in _OUTS)
```
